# Optimizing a Trainium2 kernel written in Bass

```python
import math
import jax, jax.numpy as jnp
from jax import lax
import numpy as np

D_MODEL = 1024
BATCH = 1
SEQ = 512
DEPTH = 1
DEC_BATCH = 8
DEC_SEQ = 1
PAST_LEN = 4096
PAGE_SIZE = 128

MIX_WIDTH = D_MODEL
POOL_WIDTH = MIX_WIDTH // 2
POOL_WINDOWS = (2, 4, 8, 16)
POOL_GROUPS = len(POOL_WINDOWS)
POOL_GROUP_DIM = POOL_WIDTH // POOL_GROUPS
POOL_BUF = max(POOL_WINDOWS) - 1
SSD_WIDTH = MIX_WIDTH - POOL_WIDTH
SSD_HEAD_DIM = 64
SSD_HEADS = SSD_WIDTH // SSD_HEAD_DIM
SSD_GROUPS = 2
SSD_STATE = 64
SSD_CONV = 4
SSD_CHUNK = 128
SSD_BC = SSD_GROUPS * SSD_STATE
CONV_DIM = SSD_WIDTH + 2 * SSD_BC
IN_DIM = POOL_WIDTH + SSD_WIDTH + CONV_DIM + SSD_HEADS
N_EXPERT_GROUPS = 4
EXPERTS_PER_GROUP = 8
EXPERT_TOP_K = 2
EXPERT_FF = 256
PLE_DIM = 256
EPS = 1e-6

kernel_name = 'hybrid_pool_ssd_hmoe_step'

def _rmsnorm(x, g):
    xf = x.astype(jnp.float32)
    y = xf * lax.rsqrt(jnp.mean(xf * xf, axis=-1, keepdims=True) + EPS) * g.astype(jnp.float32)
    return y.astype(x.dtype)

def _pool_mixer(v, buf, pos0, lin_w, lin_b, scale):
    n, L, c = v.shape
    ext = jnp.concatenate([buf.astype(v.dtype), v], axis=1)
    extf = ext.astype(jnp.float32)
    cs = jnp.concatenate([jnp.zeros((n, 1, c), jnp.float32), jnp.cumsum(extf, axis=1)], axis=1)
    pos = jnp.arange(L, dtype=jnp.int32) + pos0
    end = cs[:, POOL_BUF + 1:POOL_BUF + 1 + L]
    tok = extf[:, POOL_BUF:]
    groups = []
    for g, w in enumerate(POOL_WINDOWS):
        sl = slice(g * POOL_GROUP_DIM, (g + 1) * POOL_GROUP_DIM)
        start = cs[:, POOL_BUF + 1 - w:POOL_BUF + 1 - w + L, sl]
        cnt = jnp.minimum(pos + 1, w).astype(jnp.float32)[None, :, None]
        groups.append((end[..., sl] - start) / cnt - tok[..., sl])
    m = jnp.stack(groups, axis=2)
    y = jnp.einsum('blgc,gcd->blgd', m, lin_w.astype(jnp.float32)) + lin_b.astype(jnp.float32)
    y = y.reshape(n, L, POOL_WIDTH) * scale.astype(jnp.float32)
    return y.astype(v.dtype), ext[:, -POOL_BUF:]

def _ssd_chunked(x, dt, a, bm, cm, h0, chunk):
    n, L, H, P = x.shape
    nc = L // chunk
    hpg = H // bm.shape[2]
    bh = jnp.repeat(bm, hpg, axis=2).reshape(n, nc, chunk, H, -1)
    ch = jnp.repeat(cm, hpg, axis=2).reshape(n, nc, chunk, H, -1)
    xdt = (x * dt[..., None]).reshape(n, nc, chunk, H, P)
    acs = jnp.cumsum((dt * a).reshape(n, nc, chunk, H), axis=2)
    idx = jnp.arange(chunk)
    causal = (idx[:, None] >= idx[None, :])[:, :, None]
    seg = acs[:, :, :, None, :] - acs[:, :, None, :, :]
    decay = jnp.exp(jnp.where(causal, seg, -jnp.inf))
    scores = jnp.einsum('bclhn,bcshn->bclsh', ch, bh) * decay
    y_diag = jnp.einsum('bclsh,bcshp->bclhp', scores, xdt)
    to_end = jnp.exp(acs[:, :, -1:, :] - acs)
    chunk_states = jnp.einsum('bclhn,bclh,bclhp->bchpn', bh, to_end, xdt)
    chunk_decay = jnp.exp(acs[:, :, -1, :])

    def step(h, inp):
        s, d = inp
        return h * d[:, :, None, None] + s, h

    h_final, h_in = lax.scan(step, h0, (jnp.moveaxis(chunk_states, 1, 0), jnp.moveaxis(chunk_decay, 1, 0)))
    h_in = jnp.moveaxis(h_in, 0, 1)
    y_off = jnp.einsum('bclhn,bchpn->bclhp', ch, h_in) * jnp.exp(acs)[..., None]
    return (y_diag + y_off).reshape(n, L, H, P), h_final

def _ssd_mixer(z, xbc, dt_raw, conv_buf, h0, conv_w, conv_b, dt_bias, a_log, d_skip, norm_w):
    n, L, _ = xbc.shape
    f32 = jnp.float32
    ext = jnp.concatenate([conv_buf.astype(xbc.dtype), xbc], axis=1)
    extf = ext.astype(f32)
    cw = conv_w.astype(f32)
    conv = conv_b.astype(f32) + extf[:, 0:L] * cw[0]
    for k in range(1, SSD_CONV):
        conv = conv + extf[:, k:k + L] * cw[k]
    conv = jax.nn.silu(conv)
    xs = conv[..., :SSD_WIDTH].reshape(n, L, SSD_HEADS, SSD_HEAD_DIM)
    bm = conv[..., SSD_WIDTH:SSD_WIDTH + SSD_BC].reshape(n, L, SSD_GROUPS, SSD_STATE)
    cm = conv[..., SSD_WIDTH + SSD_BC:].reshape(n, L, SSD_GROUPS, SSD_STATE)
    dt = jax.nn.softplus(dt_raw.astype(f32) + dt_bias.astype(f32))
    a = -jnp.exp(a_log.astype(f32))
    y, h_final = _ssd_chunked(xs, dt, a, bm, cm, h0.astype(f32), math.gcd(L, SSD_CHUNK))
    y = y + d_skip.astype(f32)[:, None] * xs
    y = y.reshape(n, L, SSD_WIDTH) * jax.nn.silu(z.astype(f32))
    yg = y.reshape(n, L, SSD_GROUPS, SSD_WIDTH // SSD_GROUPS)
    yg = yg * lax.rsqrt(jnp.mean(yg * yg, axis=-1, keepdims=True) + EPS)
    y = yg.reshape(n, L, SSD_WIDTH) * norm_w.astype(f32)
    return y.astype(z.dtype), ext[:, -(SSD_CONV - 1):], h_final.astype(h0.dtype)

def _hier_moe(u, rg_w, rg_b, re_w, re_b, w_gate, w_up, w_down):
    f32 = jnp.float32
    n, L, d = u.shape
    t = u.reshape(n * L, d)
    g_prob = jax.nn.softmax((t @ rg_w + rg_b).astype(f32), axis=-1)
    g_w, g_idx = lax.top_k(g_prob, 1)
    e_logit = (t @ re_w + re_b).astype(f32).reshape(-1, N_EXPERT_GROUPS, EXPERTS_PER_GROUP)
    e_sel = jnp.take_along_axis(e_logit, g_idx[:, :, None], axis=1)[:, 0]
    e_w, e_idx = lax.top_k(jax.nn.softmax(e_sel, axis=-1), EXPERT_TOP_K)
    e_w = e_w / jnp.sum(e_w, axis=-1, keepdims=True)
    local_gate = jnp.einsum('tk,tke->te', g_w * e_w, jax.nn.one_hot(e_idx, EXPERTS_PER_GROUP, dtype=f32))
    group_mask = jax.nn.one_hot(g_idx[:, 0], N_EXPERT_GROUPS, dtype=f32)
    out = jnp.zeros((n * L, d), f32)
    for g in range(N_EXPERT_GROUPS):
        gate = local_gate * group_mask[:, g:g + 1]
        hg = jnp.einsum('td,edf->tef', t, w_gate[g]).astype(f32)
        hu = jnp.einsum('td,edf->tef', t, w_up[g]).astype(f32)
        act = jax.nn.silu(hg) * hu * gate[:, :, None]
        out = out + jnp.einsum('tef,efd->td', act, w_down[g].astype(f32))
    return out.reshape(n, L, d).astype(u.dtype)

def _layer(h, p, pool_buf, conv_buf, ssm_h, pos0,
           norm_mix, w_in, pool_lin_w, pool_lin_b, pool_scale, conv_w, conv_b, dt_bias, a_log,
           d_skip, ssd_norm, w_out, norm_ffn, router_grp_w, router_grp_b, router_exp_w,
           router_exp_b, exp_w_gate, exp_w_up, exp_w_down, norm_ple, ple_gate_w, ple_gate_b,
           ple_proj_w):
    a = _rmsnorm(h, norm_mix)
    proj = a @ w_in
    o1 = POOL_WIDTH
    o2 = o1 + SSD_WIDTH
    o3 = o2 + CONV_DIM
    v_pool = proj[..., :o1]
    z = proj[..., o1:o2]
    xbc = proj[..., o2:o3]
    dt_raw = proj[..., o3:]
    pool_out, new_pool = _pool_mixer(v_pool, pool_buf, pos0, pool_lin_w, pool_lin_b, pool_scale)
    ssd_out, new_conv, new_ssm = _ssd_mixer(z, xbc, dt_raw, conv_buf, ssm_h, conv_w, conv_b,
                                            dt_bias, a_log, d_skip, ssd_norm)
    h = h + jnp.concatenate([pool_out, ssd_out], axis=-1) @ w_out
    h = h + _hier_moe(_rmsnorm(h, norm_ffn), router_grp_w, router_grp_b, router_exp_w,
                      router_exp_b, exp_w_gate, exp_w_up, exp_w_down)
    gate = jax.nn.sigmoid((_rmsnorm(h, norm_ple) @ ple_gate_w + ple_gate_b).astype(jnp.float32))
    h = h + (gate * (p @ ple_proj_w).astype(jnp.float32)).astype(h.dtype)
    return h, new_pool, new_conv, new_ssm

def _trunk(x, p, pool_st, conv_st, ssm_st, pos0, layer_weights, norm_final):
    h = x
    pools, convs, ssms = [], [], []
    for i in range(DEPTH):
        lw = [w[i] for w in layer_weights]
        h, ps, cs, ss = _layer(h, p[i], pool_st[i], conv_st[i], ssm_st[i], pos0, *lw)
        pools.append(ps)
        convs.append(cs)
        ssms.append(ss)
    return _rmsnorm(h, norm_final), jnp.stack(pools), jnp.stack(convs), jnp.stack(ssms)

def setup_inputs(seed: int = 0) -> dict:
    key = jax.random.key(seed)
    ks = iter(jax.random.split(key, 40))
    f32 = jnp.float32

    def nrm(shape, scale):
        return jax.random.normal(next(ks), shape, f32) * scale

    def gain(shape):
        return 1.0 + nrm(shape, 0.05)

    dt0 = jnp.exp(jax.random.uniform(next(ks), (DEPTH, SSD_HEADS), f32, math.log(1e-3), math.log(1e-1)))
    dt_bias = dt0 + jnp.log(-jnp.expm1(-dt0))
    a_log = jnp.log(jax.random.uniform(next(ks), (DEPTH, SSD_HEADS), f32, 1.0, 16.0))
    NE = N_EXPERT_GROUPS * EXPERTS_PER_GROUP
    return {
        'x_prompt': nrm((BATCH, SEQ, D_MODEL), 1.0),
        'x_sample': nrm((DEC_BATCH, DEC_SEQ, D_MODEL), 1.0),
        'p_prompt': nrm((DEPTH, BATCH, SEQ, PLE_DIM), 1.0),
        'p_sample': nrm((DEPTH, DEC_BATCH, DEC_SEQ, PLE_DIM), 1.0),
        'state_pool': nrm((DEPTH, DEC_BATCH, POOL_BUF, POOL_WIDTH), 1.0),
        'state_conv': nrm((DEPTH, DEC_BATCH, SSD_CONV - 1, CONV_DIM), 1.0),
        'state_ssm': nrm((DEPTH, DEC_BATCH, SSD_HEADS, SSD_HEAD_DIM, SSD_STATE), 0.5),
        'norm_mix': gain((DEPTH, D_MODEL)),
        'w_in': nrm((DEPTH, D_MODEL, IN_DIM), D_MODEL ** -0.5),
        'pool_lin_w': nrm((DEPTH, POOL_GROUPS, POOL_GROUP_DIM, POOL_GROUP_DIM), POOL_GROUP_DIM ** -0.5),
        'pool_lin_b': nrm((DEPTH, POOL_GROUPS, POOL_GROUP_DIM), 0.02),
        'pool_scale': gain((DEPTH, POOL_WIDTH)),
        'conv_w': nrm((DEPTH, SSD_CONV, CONV_DIM), SSD_CONV ** -0.5),
        'conv_b': nrm((DEPTH, CONV_DIM), 0.02),
        'dt_bias': dt_bias,
        'a_log': a_log,
        'd_skip': 1.0 + nrm((DEPTH, SSD_HEADS), 0.1),
        'ssd_norm': gain((DEPTH, SSD_WIDTH)),
        'w_out': nrm((DEPTH, MIX_WIDTH, D_MODEL), MIX_WIDTH ** -0.5),
        'norm_ffn': gain((DEPTH, D_MODEL)),
        'router_grp_w': nrm((DEPTH, D_MODEL, N_EXPERT_GROUPS), D_MODEL ** -0.5),
        'router_grp_b': nrm((DEPTH, N_EXPERT_GROUPS), 0.01),
        'router_exp_w': nrm((DEPTH, D_MODEL, NE), D_MODEL ** -0.5),
        'router_exp_b': nrm((DEPTH, NE), 0.01),
        'exp_w_gate': nrm((DEPTH, N_EXPERT_GROUPS, EXPERTS_PER_GROUP, D_MODEL, EXPERT_FF), D_MODEL ** -0.5),
        'exp_w_up': nrm((DEPTH, N_EXPERT_GROUPS, EXPERTS_PER_GROUP, D_MODEL, EXPERT_FF), D_MODEL ** -0.5),
        'exp_w_down': nrm((DEPTH, N_EXPERT_GROUPS, EXPERTS_PER_GROUP, EXPERT_FF, D_MODEL), EXPERT_FF ** -0.5),
        'norm_ple': gain((DEPTH, D_MODEL)),
        'ple_gate_w': nrm((DEPTH, D_MODEL, D_MODEL), D_MODEL ** -0.5),
        'ple_gate_b': nrm((DEPTH, D_MODEL), 0.02),
        'ple_proj_w': nrm((DEPTH, PLE_DIM, D_MODEL), PLE_DIM ** -0.5),
        'norm_final': gain((D_MODEL,)),
    }

def reference(x_prompt, x_sample, p_prompt, p_sample, state_pool, state_conv, state_ssm,
              norm_mix, w_in, pool_lin_w, pool_lin_b, pool_scale, conv_w, conv_b, dt_bias, a_log,
              d_skip, ssd_norm, w_out, norm_ffn, router_grp_w, router_grp_b, router_exp_w,
              router_exp_b, exp_w_gate, exp_w_up, exp_w_down, norm_ple, ple_gate_w, ple_gate_b,
              ple_proj_w, norm_final):
    layer_weights = (norm_mix, w_in, pool_lin_w, pool_lin_b, pool_scale, conv_w, conv_b, dt_bias,
                     a_log, d_skip, ssd_norm, w_out, norm_ffn, router_grp_w, router_grp_b,
                     router_exp_w, router_exp_b, exp_w_gate, exp_w_up, exp_w_down, norm_ple,
                     ple_gate_w, ple_gate_b, ple_proj_w)
    nb = x_prompt.shape[0]
    dtp = x_prompt.dtype
    pool0 = jnp.zeros((DEPTH, nb, POOL_BUF, POOL_WIDTH), dtp)
    conv0 = jnp.zeros((DEPTH, nb, SSD_CONV - 1, CONV_DIM), dtp)
    ssm0 = jnp.zeros((DEPTH, nb, SSD_HEADS, SSD_HEAD_DIM, SSD_STATE), dtp)
    y_prompt, pool_p, conv_p, ssm_p = _trunk(x_prompt, p_prompt, pool0, conv0, ssm0, 0,
                                             layer_weights, norm_final)
    y_sample, pool_s, conv_s, ssm_s = _trunk(x_sample, p_sample, state_pool, state_conv, state_ssm,
                                             PAST_LEN, layer_weights, norm_final)
    return (y_prompt, y_sample, pool_p, conv_p, ssm_p, pool_s, conv_s, ssm_s)


_drawn_inputs = setup_inputs


def setup_inputs(seed=0):
    import zlib

    import numpy as np

    out = dict(_drawn_inputs(seed))
    spreads = {}
    factors = {'pool_lin_b': 3.072,
     'router_grp_b': 28.089,
     'router_exp_b': 6.986,
     'norm_ple': 21.523,
     'ple_gate_b': 50.71}
    for name, (base, spread) in spreads.items():
        noise = np.random.default_rng([zlib.crc32(name.encode()), seed]).standard_normal(out[name].shape)
        drawn = base * np.exp(spread * noise) if base else spread * noise
        out[name] = __import__('jax').numpy.asarray(drawn.astype(out[name].dtype))
    for name, factor in factors.items():
        out[name] = (out[name] * factor).astype(out[name].dtype)
    return out
```

```python
import concourse.bass as bass
from concourse import mybir
from contextlib import ExitStack

F32 = mybir.dt.float32
BF16 = mybir.dt.bfloat16
I32 = mybir.dt.int32
U32 = mybir.dt.uint32
ALU = mybir.AluOpType
ACT = mybir.ActivationFunctionType
AX = mybir.AxisListType

P = 128
D = 1024
KT = D // P
SEQ, NS = 512, 8
TOK = SEQ + NS
HALF = TOK // 2
NT = 5
ROWS = [128, 128, 128, 128, NS]
PW, NG, WINS, BUF = 512, 4, (2, 4, 8, 16), 15
NH, HD, NST = 8, 64, 64
XT = 6
CONV = XT * P
TAPS = 4
NC_ = SEQ // P
IN_DIM = 1800
NE, FF, PLE = 32, 256, 256
S = 64
EXTRA = 2 * TOK // S
NB = NE + EXTRA
U = 4
NBT = NB + U
NONE = 1 << 20
EPS = 1e-6
GU = KT * 2 * FF
DN = 2 * D

V_MIX, V_PB, V_PS, V_CW, V_CB, V_SN, V_FFN, V_PLE, NV = 0, 8, 12, 16, 40, 46, 50, 58, 66

C_ID, C_CAUSAL, C_BEFORE, C_ONES, C_I2, C_INV, C_POOLSEL, C_IOTA, C_TOKID, C_BAD, C_INVW, C_EPS = (
    0, 128, 256, 384, 512, 576, 640, 672, 704, 709, 714, 718)
NCONST = 719
H_EXP, H_ROW, NHEAD = 0, 512, 1536


def shape_constants(np):
    c = np.zeros((P, NCONST), np.float32)
    i = np.arange(P)
    c[:, C_ID:C_ID + P] = np.eye(P)
    c[:, C_CAUSAL:C_CAUSAL + P] = i[None, :] >= i[:, None]
    c[:, C_BEFORE:C_BEFORE + P] = i[:, None] < i[None, :]
    c[:, C_ONES:C_ONES + P] = 1
    c[:, C_I2:C_I2 + 64] = (i[:, None] % 64) == np.arange(64)[None, :]
    for g, w in enumerate(WINS):
        c[:, C_INV + 16 * g:C_INV + 16 * g + 16] = 1.0 / np.minimum(np.arange(16) + 1, w)
        for b in range(NS):
            for tau in range(BUF):
                c[b * BUF + tau, C_POOLSEL + 8 * g + b] = tau >= BUF + 1 - w
        c[:, C_INVW + g] = 1.0 / w
    c[:, C_IOTA:C_IOTA + 32] = np.arange(32)
    for t in range(NT):
        c[:, C_TOKID + t] = t * P + i
        c[:, C_BAD + t] = 4096.0 * (i >= ROWS[t])
    c[:, C_EPS] = EPS
    h = np.zeros((NH, NHEAD), np.float32)
    for t in range(4):
        for p in range(P):
            h[2 * t + p // 64, H_EXP + t * P + p] = 1
    for k in range(NH):
        h[k, H_ROW + k * P:H_ROW + (k + 1) * P] = 1
    return c, h


def build(nc, a, o):
    ctx = ExitStack()
    with ctx:
        def sem(name):
            return ctx.enter_context(nc.semaphore(name))

        class Steps:

            def __init__(self, eng, own):
                self.eng, self.own, self.n = eng, own, 0

            def __call__(self, ins):
                self.n += 1
                ins.then_inc(self.own, 1)
                self.eng.wait_ge(self.own, self.n)

        top = [0]

        def region(n):
            start = top[0]
            top[0] += (n + 7) // 8 * 8
            return start

        R_const = region(NCONST)
        R_x = region(NT * D)
        R_gu = region(U * GU)
        R_dn = region(2 * DN)
        R_aT = region(KT * TOK)
        R_v = region(NG * (SEQ + BUF))
        R_xc = region(XT * TOK)
        R_xbc = region(XT * (SEQ + TAPS - 1))
        R_z = region(4 * TOK)
        R_row = region(2 * D)
        R_tb = region(2 * D)
        R_g = region(2 * D)
        R_act = region(4 * 2 * S)
        R_samp = region(3072)
        R_dt = region(2 * TOK)
        R_small = region(1136)
        mem = ctx.enter_context(nc.sbuf_tensor("mem", [P, top[0]], F32))

        def at(off, *shape, rows=P):
            n = 1
            for s in shape:
                n *= s
            view = mem[0:rows, off:off + n]
            if len(shape) == 2:
                view = view.rearrange("p (a b) -> p a b", b=shape[1])
            if len(shape) == 3:
                view = view.rearrange("p (a b c) -> p a b c", b=shape[1], c=shape[2])
            return view

        const = at(R_const, NCONST)
        ident = const[:, C_ID:C_ID + P]
        ones = const[:, C_ONES:C_ONES + P]
        eps = const[:, C_EPS:C_EPS + 1]
        h1 = at(R_x, NT, D)
        w_in = at(R_gu, KT, IN_DIM)
        gu = [at(R_gu + s * GU, 2 * KT, FF) for s in range(U)]
        dn = [at(R_dn + s * DN, 2, D) for s in range(2)]
        w_out = at(R_gu + 2 * GU, KT, D)
        aT = at(R_aT, KT, TOK)
        mixT = aT
        xbc = at(R_xbc, XT, SEQ + TAPS - 1)
        xdtT = at(R_xbc, 4, TOK)
        zs = at(R_z, 4, TOK)
        v = at(R_v, NG, SEQ + BUF)
        xc = at(R_xc, XT, TOK)
        row = at(R_row, 2, D)
        junk = at(R_g, D)
        spool = at(R_act, PW, rows=NS * BUF)
        sconv = at(R_dt, CONV, rows=NS * (TAPS - 1))
        headc = at(R_tb, NHEAD, rows=NH)
        w_lin = at(R_tb + NHEAD, NG, P)
        fin = at(R_dn, 4, NST)
        stage_c = at(R_gu + KT * IN_DIM, CONV, rows=11)
        stage_v = at(R_row, PW, rows=23)
        H = at(R_gu, NC_, 512)
        xdtE = at(R_gu + 2048, NC_, 512)
        eE = at(R_gu + 4096, 4, SEQ)
        rsg = at(R_gu + 4096, 2, TOK)
        y = at(R_gu + 6144, 4, SEQ)
        dtw = [at(R_dn + i * TOK, TOK, rows=NH) for i in range(6)]
        M = at(R_dn, NH, SEQ)
        BC = at(R_dn + 2048, 4, 512)
        zeros = at(R_dn + 3584, 512)
        dt = at(R_dt, TOK, rows=NH)
        acs = at(R_dt + TOK, TOK, rows=NH)
        xtok = at(R_g, NC_, 512)
        Btok = at(R_act, NC_, P)
        seg = at(R_row, 2, SEQ)
        Gm = at(R_row + 1024, 2, SEQ)
        hs = at(R_samp, 4, NS * NST)
        stmp = at(R_samp + 2048, 2, NS * NST)
        win = [at(R_xbc + i * 528, 528) for i in range(2)]
        pp = at(R_xbc, NT, D)
        w_pp = at(R_v, 2, D)
        pT = at(R_xc, 2, TOK)
        prow = at(R_xc + 2 * TOK, NT, PLE)
        w_ple = at(R_aT, KT, D)
        bfin = at(R_samp + 1024, D)
        bple = at(R_samp + 2048, D)
        uTr = at(R_tb, 2, KT * P)
        uT = at(R_tb, 2, KT * S)
        G = at(R_g, 2, D, rows=S)
        sg = at(R_act, 2, 2 * S)
        actT = at(R_act + 4 * S, 2, 2 * S)
        ysb = at(R_row, 2, D, rows=S)
        Yg = at(R_gu, 2 * NT, D)
        yout = at(R_gu + 2 * NT * D, NT, D)
        sm = [R_small]

        def small(*shape, rows=P):
            r = at(sm[0], *shape, rows=rows)
            n = 1
            for s in shape:
                n *= s
            sm[0] += n
            assert sm[0] <= R_small + 1136
            return r

        vec = small(NV)
        ss = small(24)
        ln_ = small(24)
        rstd = small(24)
        acsT = small(NC_, NH)
        RL = small(NC_, NH)
        te = small(NC_, NH)
        cd = small(NC_, NH)
        xcs = small(XT, NS, TAPS)
        cprod = stmp[:, 0, 0:XT * NS * TAPS].rearrange("p (m b k) -> p m b k", b=NS, k=TAPS)
        vs = small(NG, NS)
        vsum = small(NG, NS)
        cst = small(XT, 11)
        vst = small(NG, 23)
        dx = small(4, NS + 1)
        ys = small(4, NS)
        h9 = small(NS + 1, rows=NH)
        hv = small(4, rows=NH)
        rbias = small(36)
        w_rt = small(KT, 36)
        idle = small(8)
        wgt = small(NT, 2)
        ro = [R_samp]

        def rout(*shape, base=ro):
            r = at(base[0], *shape)
            n = 1
            for s in shape:
                n *= s
            base[0] += n
            return r

        L = rout(NT, 36)
        Lg = rout(NT, 8)
        gmax = rout(NT, 8)
        gidx = rout(NT, 8).bitcast(U32)
        m4 = rout(NT, 4)
        ex4 = rout(NT, 4)
        es = rout(NT, 8)
        ev = rout(NT, 8)
        eidx = rout(NT, 8).bitcast(U32)
        gf = rout(NT)
        gw = rout(NT)
        eid = rout(NT, 2)
        e21 = rout(NT)
        rk = rout(NT, 2)
        rq = rout(NT, 2)
        rr = rout(NT, 2)
        ovt = rout(NT, 2)
        cmp0 = rout(NT, 2)
        ohs = rout(NT * 16).bitcast(BF16)
        bef = rout(P // 2).bitcast(BF16)
        oneb = rout(P // 2).bitcast(BF16)
        ovn = rout(NE)
        ove = rout(NE)
        ovb = rout(NE)
        assert ro[0] <= R_samp + 1024
        ro2 = [R_dt]
        oh = rout(NT, 2 * NE, base=ro2)
        tmp = rout(NT, 2 * NE, base=ro2)
        assert ro2[0] <= R_dt + 2 * TOK
        vecrow = ctx.enter_context(nc.sbuf_tensor("vecrow", [NV, P], F32))
        slot_i = ctx.enter_context(nc.sbuf_tensor("slot_i", [P, NT, 2], I32))
        int_w = ctx.enter_context(nc.sbuf_tensor("int_w", [P, NE], I32))
        tok_i = ctx.enter_context(nc.sbuf_tensor("tok_i", [P, NT], I32))
        idx_i = [ctx.enter_context(nc.sbuf_tensor(f"idx_i{q}", [S, 1], I32)) for q in range(2)]
        btab = ctx.enter_context(nc.sbuf_tensor("btab", [1, NB + 8], I32))
        nloop = ctx.enter_context(nc.sbuf_tensor("nloop", [1, 2], I32))
        PS = [ctx.enter_context(nc.psum_tensor(f"PS{i}", [P, 512], F32)) for i in range(8)]

        u_dram = nc.dram_tensor("u_rows", (TOK, D), F32).ap()
        slots_dram = nc.dram_tensor("slot_tokens", (NBT * S, 1), I32).ap()
        y_dram = nc.dram_tensor("block_rows", (NB * S, D), F32).ap()

        COLS = [("xbc", m, 2 * PW + m * P, P) for m in range(XT)] + [("dt", 0, IN_DIM - NH, NH)]
        COLS += [("z", m, PW + m * P, P) for m in range(4)] + [("v", m, m * P, P) for m in range(NG)]

        ld_bias = sem("ld_bias")
        ld_const = sem("ld_const")
        ld_head = sem("ld_head")
        ld_hs = sem("ld_hs")
        ld_hv = sem("ld_hv")
        ld_lin = sem("ld_lin")
        ld_p = sem("ld_p")
        ld_rt = sem("ld_rt")
        ld_state = sem("ld_state")
        ld_vec = sem("ld_vec")
        ld_wout = sem("ld_wout")
        ld_wple = sem("ld_wple")
        own_act = sem("own_act")
        own_dve = sem("own_dve")
        own_pool = sem("own_pool")
        s_M_ready = sem("s_M_ready")
        s_R_done = sem("s_R_done")
        s_R_out = sem("s_R_out")
        s_S_done = sem("s_S_done")
        s_S_out = sem("s_S_out")
        s_T_done = sem("s_T_done")
        s_YO_done = sem("s_YO_done")
        s_Y_done = sem("s_Y_done")
        s_Y_out = sem("s_Y_out")
        s_Y_ready = sem("s_Y_ready")
        s_aT_taken = sem("s_aT_taken")
        s_act_ready = sem("s_act_ready")
        s_cnt_done = sem("s_cnt_done")
        s_cnt_taken = sem("s_cnt_taken")
        s_conv_out = sem("s_conv_out")
        s_conv_pre = sem("s_conv_pre")
        s_convs_pre = sem("s_convs_pre")
        s_cst_T = sem("s_cst_T")
        s_cst_out = sem("s_cst_out")
        s_cst_ready = sem("s_cst_ready")
        s_diag_ready = sem("s_diag_ready")
        s_dt_exp = sem("s_dt_exp")
        s_dt_ln = sem("s_dt_ln")
        s_dt_neg = sem("s_dt_neg")
        s_dt_ready = sem("s_dt_ready")
        s_dt_u = sem("s_dt_u")
        s_dta_ready = sem("s_dta_ready")
        s_eE_done = sem("s_eE_done")
        s_eE_out = sem("s_eE_out")
        s_exp_a = sem("s_exp_a")
        s_f_T = sem("s_f_T")
        s_f_g = sem("s_f_g")
        s_f_gb = sem("s_f_gb")
        s_f_h2 = sem("s_f_h2")
        s_f_h3 = sem("s_f_h3")
        s_f_r2 = sem("s_f_r2")
        s_f_rstd = sem("s_f_rstd")
        s_f_sig = sem("s_f_sig")
        s_f_v = sem("s_f_v")
        s_f_vT = sem("s_f_vT")
        s_f_y = sem("s_f_y")
        s_fin_T = sem("s_fin_T")
        s_fin_out = sem("s_fin_out")
        s_g_init = sem("s_g_init")
        s_gate_done = sem("s_gate_done")
        s_gated = sem("s_gated")
        s_gn_done = sem("s_gn_done")
        s_gn_ln = sem("s_gn_ln")
        s_gn_out = sem("s_gn_out")
        s_h9_ready = sem("s_h9_ready")
        s_idle = sem("s_idle")
        s_inproj_done = sem("s_inproj_done")
        s_inproj_out = sem("s_inproj_out")
        s_lg_done = sem("s_lg_done")
        s_lg_out = sem("s_lg_out")
        s_loop_out = sem("s_loop_out")
        s_m_ready = sem("s_m_ready")
        s_mixP_ready = sem("s_mixP_ready")
        s_mix_ready = sem("s_mix_ready")
        s_oh_ready = sem("s_oh_ready")
        s_outp_done = sem("s_outp_done")
        s_outp_out = sem("s_outp_out")
        s_pT_done = sem("s_pT_done")
        s_pT_out = sem("s_pT_out")
        s_pads = sem("s_pads")
        s_pool_done = sem("s_pool_done")
        s_pp_done = sem("s_pp_done")
        s_pp_out = sem("s_pp_out")
        s_r_rstd = sem("s_r_rstd")
        s_rstd_x = sem("s_rstd_x")
        s_rt_a = sem("s_rt_a")
        s_rt_b = sem("s_rt_b")
        s_rt_ready = sem("s_rt_ready")
        s_samp_done = sem("s_samp_done")
        s_scan1_done = sem("s_scan1_done")
        s_scan1_out = sem("s_scan1_out")
        s_seg_exp = sem("s_seg_exp")
        s_sg_ready = sem("s_sg_ready")
        s_sq_out = sem("s_sq_out")
        s_states_T = sem("s_states_T")
        s_states_in = sem("s_states_in")
        s_te_in = sem("s_te_in")
        s_te_ready = sem("s_te_ready")
        s_uT_ready = sem("s_uT_ready")
        s_uTr_done = sem("s_uTr_done")
        s_uTr_out = sem("s_uTr_out")
        s_u_ready = sem("s_u_ready")
        s_up_done = sem("s_up_done")
        s_vec_T = sem("s_vec_T")
        s_vst_T = sem("s_vst_T")
        s_vst_out = sem("s_vst_out")
        s_vst_ready = sem("s_vst_ready")
        s_xT_done = sem("s_xT_done")
        s_xdtE_ready = sem("s_xdtE_ready")
        s_xn_ready = sem("s_xn_ready")
        s_ysb_free = sem("s_ysb_free")
        slots_filled = sem("slots_filled")
        st_conv = sem("st_conv")
        st_fin = sem("st_fin")
        st_hs = sem("st_hs")
        st_out = sem("st_out")
        st_pool = sem("st_pool")
        st_shift = sem("st_shift")
        st_slots = sem("st_slots")
        st_zeros = sem("st_zeros")
        ld_x = [sem(f"ld_x{i}") for i in range(NT)]
        ld_w = [sem(f"ld_w{i}") for i in range(3)]
        w_full = [sem(f"w_full{i}") for i in range(U)]
        d_full = [sem(f"d_full{i}") for i in range(2)]
        idx_full = [sem(f"idx_full{i}") for i in range(2)]
        g_full = [sem(f"g_full{i}") for i in range(2)]
        y_written = [sem(f"y_written{i}") for i in range(2)]
        u_stored = [sem(f"u_stored{i}") for i in range(2)]
        yg_full = [sem(f"yg_full{i}") for i in range(NT)]
        block = ctx.enter_context(nc.Block())

        @block.sync
        def _(sp):
            sp.dma_start(const, a["consts"]).then_inc(ld_const, 16)
            for t in range(NT):
                src = a["x_prompt"][0, t * P:(t + 1) * P, :] if t < 4 else a["x_sample"][:, 0, :]
                sp.dma_start(h1[0:ROWS[t], t, :], src).then_inc(ld_x[t], 16)
            w = a["w_in"][0].rearrange("(k p) n -> p k n", p=P)
            for i, (lo, hi) in enumerate([(2 * PW, IN_DIM), (PW, 2 * PW), (0, PW)]):
                sp.dma_start(w_in[:, :, lo:hi], w[:, :, lo:hi]).then_inc(ld_w[i], 16)
            for t in range(4):
                sp.dma_start(hs[:, t].rearrange("p (b n) -> p b n", n=NST),
                             a["state_ssm"][0, :, 2 * t:2 * t + 2].rearrange("b h p n -> (h p) b n")
                             ).then_inc(ld_hs, 16)
            sp.dma_start(o["pool_s"][0, :, 0:BUF - 1, :], a["state_pool"][0, :, 1:BUF, :]).then_inc(st_shift, 16)
            sp.dma_start(o["conv_s"][0, :, 0:2, :], a["state_conv"][0, :, 1:3, :]).then_inc(st_shift, 16)
            sp.wait_ge(s_cst_out, 1)
            sp.dma_start(o["conv_p"][0, 0], stage_c[0:3, :]).then_inc(st_conv, 16)
            sp.dma_start(o["conv_s"][0, :, 2, :], stage_c[3:11, :]).then_inc(st_conv, 16)
            sp.wait_ge(s_inproj_done, len(COLS))
            sp.wait_ge(st_conv, 32)
            sp.dma_start(w_out, a["w_out"][0].rearrange("(k p) n -> p k n", p=P)).then_inc(ld_wout, 16)
            sp.wait_ge(s_vst_out, 1)
            sp.dma_start(o["pool_p"][0, 0], stage_v[0:BUF, :]).then_inc(st_pool, 16)
            sp.dma_start(o["pool_s"][0, :, BUF - 1, :], stage_v[BUF:23, :]).then_inc(st_pool, 16)
            sp.wait_ge(s_samp_done, 1)
            for t in range(4):
                sp.dma_start(o["ssm_s"][0, :, 2 * t:2 * t + 2].rearrange("b h p n -> (h p) b n"),
                             hs[:, t].rearrange("p (b n) -> p b n", n=NST)).then_inc(st_hs, 16)
            sp.wait_ge(s_fin_out, 1)
            sp.dma_start(o["ssm_p"][0, 0].rearrange("(t h) p n -> (h p) t n", h=2), fin).then_inc(st_fin, 16)
            sp.wait_ge(s_gated, 4)
            sp.wait_ge(s_mixP_ready, NG)
            sp.dma_start(w_pp, a["ple_proj_w"][0].rearrange("(k p) n -> p k n", p=P)).then_inc(ld_p, 16)
            sp.dma_start(prow[:, 0:4, :], a["p_prompt"][0, 0].rearrange("(t p) n -> p t n", p=P)).then_inc(ld_p, 16)
            sp.dma_start(prow[0:NS, 4, :], a["p_sample"][0, :, 0, :]).then_inc(ld_p, 16)

            def load_gate_up(slot, src_e):
                sp.dma_start(gu[slot][:, 0:KT, :], a["exp_w_gate"][src_e].rearrange("a (k p) f -> p (a k) f", p=P)
                             ).then_inc(w_full[slot], 16)
                sp.dma_start(gu[slot][:, KT:2 * KT, :], a["exp_w_up"][src_e].rearrange("a (k p) f -> p (a k) f", p=P)
                             ).then_inc(w_full[slot], 16)

            def load_down(slot, src_e):
                sp.dma_start(dn[slot], a["exp_w_down"][src_e].rearrange("a (k p) n -> p (a k) n", p=P)
                             ).then_inc(d_full[slot], 16)

            sp.wait_ge(st_fin, 16)
            sp.wait_ge(s_mix_ready, 4)
            for b in range(2):
                load_gate_up(b, bass.ds(b, 1))
                load_down(b, bass.ds(b, 1))
            for t in range(NT):
                sp.wait_ge(s_u_ready, t + 1)
                rows = ROWS[t]
                sp.dma_start(u_dram[t * P:t * P + rows, :], row[0:rows, t % 2, :]).then_inc(u_stored[t % 2], 16)
            sp.wait_ge(st_hs, 64)
            sp.dma_start(bfin, a["norm_final"].unsqueeze(0).to_broadcast((P, D))).then_inc(ld_bias, 16)
            sp.dma_start(bple, a["ple_gate_b"].to_broadcast((P, D))).then_inc(ld_bias, 16)
            sp.wait_ge(s_outp_done, NT)
            for b in range(2, U):
                load_gate_up(b, bass.ds(b, 1))
            sp.wait_ge(s_rt_ready, 1)
            m = sp.value_load(nloop[0:1, 1:2], min_val=NE // U - 1, max_val=NB // U - 1)
            sp.wait_ge(s_pp_out, 2 * NT)
            sp.dma_start(w_ple, a["ple_gate_w"][0].rearrange("(k p) n -> p k n", p=P)).then_inc(ld_wple, 16)
            with sp.Fori(0, m) as i:
                for s in range(U):
                    e = sp.value_load(btab[0:1, bass.ds(i * U + (U + s), 1)], min_val=0, max_val=NE - 1)
                    sp.wait_ge(s_up_done, i * U + (s + 1))
                    load_gate_up(s, bass.ds(e, 1))
                    e = sp.value_load(btab[0:1, bass.ds(i * U + (s + 2), 1)], min_val=0, max_val=NE - 1)
                    sp.wait_ge(s_Y_ready, i * U + (s + 1))
                    load_down(s % 2, bass.ds(e, 1))
            for s in range(2):
                e = sp.value_load(btab[0:1, bass.ds(m * U + (s + 2), 1)], min_val=0, max_val=NE - 1)
                sp.wait_ge(s_Y_ready, m * U + (s + 1))
                load_down(s % 2, bass.ds(e, 1))
            for t in range(NT):
                rows = ROWS[t]
                sp.wait_ge(s_f_y, t + 1)
                dst = o["y_p"][0, t * P:(t + 1) * P, :] if t < 4 else o["y_s"][:, 0, :]
                sp.dma_start(dst, yout[0:rows, t, :]).then_inc(st_out, 16)
            sp.wait_ge(st_out, 16 * NT)
            sp.wait_ge(st_shift, 32)
            sp.wait_ge(st_pool, 32)
            sp.wait_ge(st_hs, 64)
            sp.wait_ge(st_slots, 16)

        @block.tensor
        def _(pe):
            def transpose(dst, src, n):
                return pe.transpose(dst, src, ident[0:n, 0:n])

            pe.wait_ge(ld_const, 16)
            pe.wait_ge(ld_vec, 16 * 8)
            transpose(PS[6][:, 0:NV], vecrow[:, :], NV).then_inc(s_vec_T, 1)
            pe.wait_ge(ld_state, 32)
            for m in range(XT):
                transpose(PS[7][:, m * 24:(m + 1) * 24], sconv[:, m * P:(m + 1) * P], 24)
            for g in range(NG):
                ins = pe.matmul(PS[7][:, 256 + g * NS:256 + (g + 1) * NS], spool[:, g * P:(g + 1) * P],
                                const[0:NS * BUF, C_POOLSEL + 8 * g:C_POOLSEL + 8 * g + 8], start=True, stop=True)
            ins.then_inc(s_states_T, 1)
            for j in range(2 * NT):
                t, half = j // 2, j % 2
                R = ROWS[t]
                pe.wait_ge(s_xn_ready, t + 1)
                if j >= 2:
                    pe.wait_ge(s_aT_taken, j - 1)
                for q in range(4):
                    k = 4 * half + q
                    ins = transpose(PS[4 + j % 2][:, q * P:q * P + R], row[0:R, t % 2, k * P:(k + 1) * P], R)
                ins.then_inc(s_xT_done, 1)

            def inproj(j):
                kind, m, col, n = COLS[j]
                pe.wait_ge(ld_w[0 if j <= XT else 1 if kind == "z" else 2], 16)
                if j >= 2:
                    pe.wait_ge(s_inproj_out, j - 1)
                for k in range(KT):
                    for h in range(2):
                        ins = pe.matmul(PS[2 * (j % 2) + h][0:n, 0:HALF], w_in[:, k, col:col + n],
                                        aT[:, k, h * HALF:(h + 1) * HALF], start=(k == 0), stop=(k == KT - 1))
                ins.then_inc(s_inproj_done, 1)

            pe.wait_ge(s_aT_taken, 2 * NT)
            for j in range(8):
                inproj(j)
            pe.wait_ge(s_cst_ready, 1)
            for m in range(XT):
                ins = transpose(PS[4 + m // 4][0:11, (m % 4) * P:(m % 4 + 1) * P], cst[:, m, :], P)
            ins.then_inc(s_cst_T, 1)
            inproj(8)
            inproj(9)
            inproj(10)
            pe.wait_ge(s_dt_ready, 1)
            pe.wait_ge(ld_head, 16)
            pe.wait_ge(s_cst_out, 1)
            for t in range(4):
                if t >= 2:
                    pe.wait_ge(s_scan1_out, t - 1)
                for h in range(2):
                    ins = pe.matmul(PS[4 + 2 * (t % 2) + h][:, 0:HALF], headc[:, H_EXP + t * P:H_EXP + (t + 1) * P],
                                    dt[:, h * HALF:(h + 1) * HALF], start=True, stop=True)
                ins.then_inc(s_scan1_done, 1)
            pe.wait_ge(s_scan1_out, 3)
            for c in range(NC_):
                ins = transpose(PS[4][:, c * NH:(c + 1) * NH], acs[:, c * P:(c + 1) * P], NH)
            ins.then_inc(s_scan1_done, 1)
            for c in range(NC_):
                ins = transpose(PS[5][:, c * P:(c + 1) * P], xc[:, 4, c * P:(c + 1) * P], P)
            ins.then_inc(s_scan1_done, 1)
            pe.wait_ge(s_scan1_out, 4)
            for g in range(2):
                rows = slice(64 * g, 64 * g + 64)
                for c in range(NC_):
                    cc = slice(c * P, (c + 1) * P)
                    ins = pe.matmul(PS[6 + g][:, cc], xc[rows, 4, cc], xc[rows, 5, cc], start=True, stop=True)
                ins.then_inc(s_scan1_done, 1)
            for c in range(NC_):
                pe.wait_ge(s_scan1_out, 5 + c)
                for t in range(4):
                    ins = transpose(PS[4 + c][:, t * P:(t + 1) * P], xdtT[:, t, c * P:(c + 1) * P], P)
                ins.then_inc(s_scan1_done, 1)
            pe.wait_ge(s_h9_ready, 1)
            pe.wait_ge(s_scan1_out, 9)
            for t in range(4):
                ins = pe.matmul(PS[4][:, t * (NS + 1):(t + 1) * (NS + 1)], headc[:, H_EXP + t * P:H_EXP + (t + 1) * P],
                                h9[:, :], start=True, stop=True)
            ins.then_inc(s_scan1_done, 1)
            for q in range(4):
                kind, g = q // 2, q % 2
                rows = slice(64 * g, 64 * g + 64)
                pe.wait_ge(s_diag_ready, kind + 1)
                pe.wait_ge(s_scan1_out, 14 if q == 3 else 10 + q)
                ins = pe.matmul(PS[5 + q % 3][:, :], ones[rows, :], stmp[rows, kind, :], start=True, stop=True)
                ins.then_inc(s_scan1_done, 1)

            def head_row(h):
                pe.wait_ge(s_scan1_out, 17)
                if h >= 4:
                    pe.wait_ge(s_R_out, h - 3)
                pe.matmul(PS[4 + h % 4][:, :], headc[:, H_ROW + h * P:H_ROW + (h + 1) * P], acs[:, 0:SEQ],
                          start=True, stop=True).then_inc(s_R_done, 1)

            for q in range(4):
                inproj(11 + q)
                head_row(2 * q)
                head_row(2 * q + 1)
            for t in range(4):
                pe.wait_ge(s_R_out, 5 + t)
                pe.matmul(PS[4 + t][:, :], headc[:, H_EXP + t * P:H_EXP + (t + 1) * P], acs[:, 0:SEQ],
                          start=True, stop=True).then_inc(s_eE_done, 1)
            for c in range(NC_):
                pe.wait_ge(s_xdtE_ready, c + 1)
                pe.wait_ge(s_eE_out, c + 1)
                pe.matmul(PS[4 + c][:, :], Btok[:, c, :], xdtE[:, c, :], start=True, stop=True).then_inc(s_S_done, 1)
            pe.wait_ge(s_inproj_out, len(COLS))
            for h in range(NH):
                pe.wait_ge(s_M_ready, h + 1)
                for c in range(NC_):
                    ins = pe.matmul(PS[h // 2][64 * (h % 2):64 * (h % 2) + 64, c * P:(c + 1) * P],
                                    xtok[:, c, h * HD:(h + 1) * HD], M[:, h, c * P:(c + 1) * P],
                                    start=True, stop=True)
                if h % 2:
                    ins.then_inc(s_Y_done, 1)
            for t in range(4):
                rows = slice(64 * (t // 2), 64 * (t // 2) + 64)
                pe.wait_ge(s_S_out, 4)
                for c in range(1, NC_):
                    ins = pe.matmul(PS[4 + t][:, c * P:(c + 1) * P], H[rows, c - 1, t * P:(t + 1) * P],
                                    xc[rows, 5, c * P:(c + 1) * P], start=True, stop=True)
                ins.then_inc(s_YO_done, 1)
            for t in range(4):
                g = t // 2
                rows = slice(64 * g, 64 * g + 64)
                if t == 0 or t == 2:
                    pe.wait_ge(s_Y_out, t + 1)
                ins = pe.transpose(PS[4 + 2 * g][:, (t % 2) * NST:(t % 2 + 1) * NST], H[rows, NC_ - 1, t * P:(t + 1) * P],
                                   ident[rows, 64 * g:64 * g + 64])
            ins.then_inc(s_fin_T, 1)
            pe.wait_ge(s_vst_ready, 1)
            pe.wait_ge(s_Y_out, 2)
            for g in range(NG):
                ins = transpose(PS[5][0:23, g * P:(g + 1) * P], vst[:, g, :], P)
            ins.then_inc(s_vst_T, 1)
            for g in range(NG):
                pe.wait_ge(s_m_ready, g + 1)
                pe.wait_ge(ld_lin, 16)
                if g == 0:
                    pe.wait_ge(s_Y_out, 4)
                    pe.wait_ge(s_fin_out, 1)
                if g >= 1:
                    pe.wait_ge(s_mixP_ready, g)
                for h in range(2):
                    ins = pe.matmul(PS[6 + h][:, 0:HALF], w_lin[:, g, :], mixT[:, g, h * HALF:(h + 1) * HALF],
                                    start=True, stop=True)
                ins.then_inc(s_pool_done, 1)
            for g in range(2):
                pe.wait_ge(s_sq_out, 2 * g + 2)
                for h in range(2):
                    for q in range(2):
                        ins = pe.matmul(PS[2 * g + h][:, 0:HALF], ones, zs[:, 2 * g + q, h * HALF:(h + 1) * HALF],
                                        start=(q == 0), stop=(q == 1))
                ins.then_inc(s_gn_done, 1)

            def outproj(t):
                R = ROWS[t]
                if t == 0:
                    pe.wait_ge(ld_wout, 16)
                    pe.wait_ge(s_mixP_ready, NG)
                    pe.wait_ge(s_mix_ready, 4)
                if t >= 2:
                    pe.wait_ge(s_outp_out, t - 1)
                for h in range(2):
                    for k in range(KT):
                        ins = pe.matmul(PS[2 * (t % 2) + h][0:R, :], mixT[:, k, t * P:t * P + R],
                                        w_out[:, k, h * 512:(h + 1) * 512], start=(k == 0), stop=(k == KT - 1))
                ins.then_inc(s_outp_done, 1)

            def route(t):
                R = ROWS[t]
                pe.wait_ge(s_u_ready, t + 1)
                for half in range(2):
                    j = 2 * t + half
                    if t == 0 and half == 0:
                        pe.wait_ge(s_fin_out, 1)
                        pe.wait_ge(s_vst_out, 1)
                    if t >= 1:
                        pe.wait_ge(s_uTr_out, j - 1)
                    for q in range(4):
                        k = 4 * half + q
                        ins = transpose(PS[4 + half][:, q * P:q * P + R], row[0:R, t % 2, k * P:(k + 1) * P], R)
                    ins.then_inc(s_uTr_done, 1)
                pe.wait_ge(s_uTr_out, 2 * t + 2)
                pe.wait_ge(ld_rt, 64)
                for k in range(KT):
                    ins = pe.matmul(PS[6][0:R, t * 36:(t + 1) * 36], uTr[:, t % 2, k * P:k * P + R],
                                    w_rt[:, k, :], start=(k == 0), stop=(k == KT - 1))
                ins.then_inc(s_lg_done, 1)

            outproj(0)
            outproj(1)
            route(0)
            outproj(2)
            route(1)
            outproj(3)
            route(2)
            outproj(4)
            route(3)
            route(4)
            pe.wait_ge(ld_p, 48)
            for t in range(NT):
                R = ROWS[t]
                if t >= 1:
                    pe.wait_ge(s_pT_out, t)
                for q in range(2):
                    ins = transpose(PS[7][:, q * P:q * P + R], prow[0:R, t, q * P:(q + 1) * P], R)
                ins.then_inc(s_pT_done, 1)

            def pleproj(t):
                R = ROWS[t]
                for h in range(2):
                    j = 2 * t + h
                    if j == 0:
                        pe.wait_ge(s_pT_out, NT)
                        pe.wait_ge(s_outp_out, NT)
                    if j >= 4:
                        pe.wait_ge(s_pp_out, j - 3)
                    for q in range(2):
                        ins = pe.matmul(PS[j % 4][0:R, :], pT[:, q, t * P:t * P + R], w_pp[:, q, h * 512:(h + 1) * 512],
                                        start=(q == 0), stop=(q == 1))
                    ins.then_inc(s_pp_done, 1)

            pleproj(0)
            pe.wait_ge(s_oh_ready, 1)
            for t in range(NT + 1):
                for t2 in range(min(t + 1, NT)):
                    last = t2 == min(t, NT - 1)
                    ins = pe.matmul(PS[7][:, t * NE:(t + 1) * NE], bef if t2 == t else oneb, ohs[:, t2 * NE:(t2 + 1) * NE],
                                    start=(t2 == 0), stop=last)
            ins.then_inc(s_cnt_done, 1)
            for t in range(1, NT):
                pleproj(t)

            pe.wait_ge(s_rt_ready, 1)
            n = pe.value_load(nloop[0:1, 0:1], min_val=NE // U, max_val=NB // U)
            pe.wait_ge(s_cnt_taken, 1)
            pe.wait_ge(s_lg_out, NT)
            pe.wait_ge(g_full[0], 16)

            def block_rows(b2):
                for k in range(KT):
                    ins = transpose(PS[6 + b2][:, k * S:(k + 1) * S], G[:, b2, k * P:(k + 1) * P], S)
                ins.then_inc(s_T_done, 1)

            block_rows(0)
            pe.wait_ge(s_pp_out, 2 * NT)
            with pe.Fori(0, n) as i:
                for s in range(U):
                    pe.wait_ge(s_uT_ready, i * U + (s + 1))
                    pe.wait_ge(w_full[s], i * 32 + 32)
                    for part in range(2):
                        if part:
                            pe.wait_ge(g_full[(s + 1) % 2], i * 32 + 16 * ((s + 1) // 2 + 1))
                        for f in range(2):
                            for k in range(KT):
                                ins = pe.matmul(PS[part][:, f * S:(f + 1) * S],
                                                gu[s][:, part * KT + k, f * P:(f + 1) * P],
                                                uT[:, s % 2, k * S:(k + 1) * S], start=(k == 0), stop=(k == KT - 1))
                        ins.then_inc(s_up_done if part else s_gate_done, 1)
                    block_rows((s + 1) % 2)
                    pe.wait_ge(s_act_ready, i * U + (s + 1))
                    pe.wait_ge(s_ysb_free, i * U + (s + 1))
                    pe.wait_ge(d_full[s % 2], i * 32 + 16 * (s // 2 + 1))
                    for h in range(2):
                        for f in range(2):
                            ins = pe.matmul(PS[4 + h][0:S, :], actT[:, s % 2, f * S:(f + 1) * S],
                                            dn[s % 2][:, f, h * 512:(h + 1) * 512], start=(f == 0), stop=(f == 1))
                    ins.then_inc(s_Y_ready, 1)

            def v_rows(t):
                R = ROWS[t]
                pe.wait_ge(s_f_v, t + 1)
                for half in range(2):
                    if t >= 1:
                        pe.wait_ge(s_f_vT, 2 * t - 1 + half)
                    for q in range(4):
                        k = 4 * half + q
                        ins = transpose(PS[6 + half][:, q * P:q * P + R], row[0:R, t % 2, k * P:(k + 1) * P], R)
                    ins.then_inc(s_f_T, 1)

            def gates(t):
                R = ROWS[t]
                pe.wait_ge(s_f_vT, 2 * t + 2)
                if t == 0:
                    pe.wait_ge(ld_wple, 16)
                if t >= 2:
                    pe.wait_ge(s_f_gb, 2 * t - 2)
                for h in range(2):
                    for k in range(KT):
                        ins = pe.matmul(PS[2 * (t % 2) + h][0:R, :], uTr[:, t % 2, k * P:k * P + R],
                                        w_ple[:, k, h * 512:(h + 1) * 512], start=(k == 0), stop=(k == KT - 1))
                    ins.then_inc(s_f_g, 1)

            v_rows(0)
            for t in range(NT):
                if t + 1 < NT:
                    v_rows(t + 1)
                gates(t)

        @block.scalar
        def _(act):
            step = Steps(act, own_act)
            A = act.activation
            for n, (name, lo, hi) in enumerate([("norm_mix", V_MIX, V_PB), ("pool_lin_b", V_PB, V_PS),
                                                ("pool_scale", V_PS, V_CW), ("conv_w", V_CW, V_CB),
                                                ("conv_b", V_CB, V_SN), ("ssd_norm", V_SN, V_FFN),
                                                ("norm_ffn", V_FFN, V_PLE), ("norm_ple", V_PLE, NV)]):
                src = a[name]
                if name == "conv_w":
                    src = src.rearrange("a k (m p) -> (a k m) p", p=P)
                elif name == "pool_lin_b":
                    src = src.rearrange("a g p -> (a g) p")
                else:
                    src = src.rearrange("a (m p) -> (a m) p", p=P)
                act.dma_start(vecrow[lo:hi, :], src).then_inc(ld_vec, 16)
            act.dma_start(sconv, a["state_conv"][0].rearrange("b r c -> (b r) c")).then_inc(ld_state, 16)
            act.dma_start(spool, a["state_pool"][0].rearrange("b r c -> (b r) c")).then_inc(ld_state, 16)
            act.dma_start(headc, a["heads"]).then_inc(ld_head, 16)
            act.dma_start(hv[:, 0:1], a["dt_bias"].rearrange("a h -> h a")).then_inc(ld_hv, 16)
            act.dma_start(hv[:, 1:2], a["a_log"].rearrange("a h -> h a")).then_inc(ld_hv, 16)
            act.dma_start(h9[:, NS:NS + 1], a["d_skip"].rearrange("a h -> h a")).then_inc(ld_hv, 16)
            act.dma_start(w_lin, a["pool_lin_w"][0].rearrange("g c d -> c g d")).then_inc(ld_lin, 16)
            act.dma_start(w_rt[:, :, 0:4], a["router_grp_w"][0].rearrange("(k p) n -> p k n", p=P)).then_inc(ld_rt, 16)
            act.dma_start(w_rt[:, :, 4:36], a["router_exp_w"][0].rearrange("(k p) n -> p k n", p=P)).then_inc(ld_rt, 16)
            act.dma_start(rbias[:, 0:4], a["router_grp_b"].to_broadcast((P, 4))).then_inc(ld_rt, 16)
            act.dma_start(rbias[:, 4:36], a["router_exp_b"].to_broadcast((P, NE))).then_inc(ld_rt, 16)

            def rms(t, src, j, squares, ready):
                R = ROWS[t]
                step(A(squares[0:R, :], src, ACT.Square, accum_out=ss[0:R, j:j + 1]))
                step(A(ln_[0:R, j:j + 1], ss[0:R, j:j + 1], ACT.Ln, bias=eps[0:R, :], scale=1.0 / D))
                A(rstd[0:R, j:j + 1], ln_[0:R, j:j + 1], ACT.Exp, scale=-0.5).then_inc(ready, 1)

            act.wait_ge(ld_const, 16)
            for t in range(NT):
                act.wait_ge(ld_x[t], 16)
                rms(t, h1[0:ROWS[t], t, :], t, junk, s_rstd_x)
            act.wait_ge(s_states_T, 1)
            A(xcs[:, :, :, 0:3], PS[7][:, 0:144].rearrange("p (m b k) -> p m b k", b=NS, k=3), ACT.Copy)
            A(vsum, PS[7][:, 256:256 + NG * NS].rearrange("p (g b) -> p g b", b=NS), ACT.Copy).then_inc(s_states_in, 1)

            def out(j):
                kind, m, _, n = COLS[j]
                a0, b0 = PS[2 * (j % 2)], PS[2 * (j % 2) + 1]
                cut = SEQ - HALF
                act.wait_ge(s_inproj_done, j + 1)
                if kind == "xbc":
                    A(xbc[:, m, 3:3 + HALF], a0[:, 0:HALF], ACT.Copy)
                    A(xbc[:, m, 3 + HALF:3 + SEQ], b0[:, 0:cut], ACT.Copy)
                    A(xcs[:, m, :, 3], b0[:, cut:HALF], ACT.Copy).then_inc(s_inproj_out, 1)
                elif kind == "dt":
                    A(dtw[0][:, 0:HALF], a0[0:n, 0:HALF], ACT.Identity, bias=hv[:, 0:1])
                    A(dtw[0][:, HALF:TOK], b0[0:n, 0:HALF], ACT.Identity, bias=hv[:, 0:1]).then_inc(s_inproj_out, 1)
                elif kind == "z":
                    A(zs[:, m, 0:HALF], a0[:, 0:HALF], ACT.Silu)
                    A(zs[:, m, HALF:TOK], b0[:, 0:HALF], ACT.Silu).then_inc(s_inproj_out, 1)
                else:
                    A(v[:, m, BUF:BUF + HALF], a0[:, 0:HALF], ACT.Copy)
                    A(v[:, m, BUF + HALF:BUF + SEQ], b0[:, 0:cut], ACT.Copy)
                    A(vs[:, m, :], b0[:, cut:HALF], ACT.Copy).then_inc(s_inproj_out, 1)

            def conv_silu(m):
                act.wait_ge(s_conv_pre, m + 1)
                A(xc[:, m, 0:SEQ], xc[:, m, 0:SEQ], ACT.Silu).then_inc(s_conv_out, 1)

            for j in range(XT):
                out(j)
                if j >= 1:
                    conv_silu(j - 1)
            act.wait_ge(ld_hv, 48)
            out(6)
            conv_silu(5)
            act.wait_ge(s_convs_pre, 1)
            A(xc[:, :, SEQ:TOK], xc[:, :, SEQ:TOK], ACT.Silu).then_inc(s_conv_out, 1)
            A(hv[:, 2:3], hv[:, 1:2], ACT.Exp).then_inc(s_exp_a, 1)
            act.wait_ge(s_dt_neg, 1)
            A(dtw[2], dtw[1], ACT.Exp).then_inc(s_dt_exp, 1)
            act.wait_ge(s_dt_u, 1)
            A(dtw[4], dtw[3], ACT.Ln).then_inc(s_dt_ln, 1)
            act.wait_ge(s_dta_ready, 1)
            A(h9[:, 0:NS], dtw[5][:, SEQ:TOK], ACT.Exp).then_inc(s_h9_ready, 1)
            out(7)
            act.wait_ge(s_cst_T, 1)
            A(stage_c[0:11, 0:512], PS[4][0:11, :], ACT.Copy)
            A(stage_c[0:11, 512:768], PS[5][0:11, 0:256], ACT.Copy).then_inc(s_cst_out, 1)
            out(8)
            out(9)
            out(10)

            def seg_exp(h):
                act.wait_ge(s_R_out, h + 1)
                A(seg[:, h % 2, :], seg[:, h % 2, :], ACT.Exp).then_inc(s_seg_exp, 1)

            for q in range(4):
                out(11 + q)
                seg_exp(2 * q)
                seg_exp(2 * q + 1)
            act.wait_ge(s_te_in, 1)
            A(te, te, ACT.Exp)
            A(cd, RL, ACT.Exp).then_inc(s_te_ready, 1)
            for t in range(4):
                act.wait_ge(s_eE_done, t + 1)
                A(eE[:, t, :], PS[4 + t][:, :], ACT.Exp).then_inc(s_eE_out, 1)
            act.wait_ge(s_fin_T, 1)
            for g in range(2):
                ins = A(fin[:, 2 * g:2 * g + 2, :], PS[4 + 2 * g][:, 0:2 * NST].rearrange("p (t n) -> p t n", n=NST), ACT.Copy)
            ins.then_inc(s_fin_out, 1)
            act.wait_ge(s_vst_T, 1)
            A(stage_v[0:23, :], PS[5][0:23, :], ACT.Copy).then_inc(s_vst_out, 1)
            for t in range(4):
                act.wait_ge(s_gated, t + 1)
                A(zs[:, t, 0:SEQ], y[:, t, :], ACT.Square)
                A(zs[:, t, SEQ:TOK], ys[:, t, :], ACT.Square).then_inc(s_sq_out, 1)
            for g in range(2):
                act.wait_ge(s_gn_done, g + 1)
                for h in range(2):
                    A(rsg[:, g, h * HALF:(h + 1) * HALF], PS[2 * g + h][:, 0:HALF], ACT.Ln,
                      bias=eps, scale=1.0 / (2 * P)).then_inc(s_gn_ln, 1)
                act.wait_ge(s_gn_ln, 2 * g + 2)
                A(rsg[:, g, :], rsg[:, g, :], ACT.Exp, scale=-0.5).then_inc(s_gn_out, 1)
            for t in range(NT):
                act.wait_ge(s_outp_out, t + 1)
                rms(t, h1[0:ROWS[t], t, :], 5 + t, junk, s_r_rstd)
            for t in range(NT):
                R = ROWS[t]
                act.wait_ge(s_pT_done, t + 1)
                A(pT[:, :, t * P:t * P + R], PS[7][:, 0:2 * P].rearrange("p (q c) -> p q c", c=P)[:, :, 0:R],
                  ACT.Copy).then_inc(s_pT_out, 1)

            def pp_out(j):
                R = ROWS[j // 2]
                act.wait_ge(s_pp_done, j + 1)
                A(pp[0:R, j // 2, (j % 2) * 512:(j % 2 + 1) * 512], PS[j % 4][0:R, :], ACT.Copy).then_inc(s_pp_out, 1)

            pp_out(0)
            pp_out(1)
            act.wait_ge(s_rt_a, 1)
            step(A(ex4, ex4, ACT.Exp))
            A(e21, e21, ACT.Exp).then_inc(s_rt_b, 1)
            for j in range(2, 2 * NT):
                pp_out(j)
            act.wait_ge(s_rt_ready, 1)
            n = act.value_load(nloop[0:1, 0:1], min_val=NE // U, max_val=NB // U)
            with act.Fori(0, n) as i:
                for s in range(U):
                    act.wait_ge(s_gate_done, i * U + (s + 1))
                    A(sg[:, s % 2, :], PS[0][:, 0:2 * S], ACT.Silu).then_inc(s_sg_ready, 1)
                    act.wait_ge(s_Y_ready, i * U + (s + 1))
                    act.wait_ge(y_written[s % 2], i * 32 + 16 * (s // 2 + 1))
                    A(ysb[:, s % 2, 0:512], PS[4][0:S, :], ACT.Copy)
                    A(ysb[:, s % 2, 512:1024], PS[5][0:S, :], ACT.Copy).then_inc(s_ysb_free, 1)
                    act.wait_ge(s_ysb_free, i * U + (s + 2))
                    act.dma_start(y_dram[bass.ds(i * (U * S) + s * S, S), :], ysb[:, s % 2, :]).then_inc(y_written[s % 2], 16)
            def norm_h2(t):
                act.wait_ge(s_f_h2, t + 1)
                rms(t, h1[0:ROWS[t], t, :], 10 + t, yout[:, t, :], s_f_rstd)

            def final(t):
                R = ROWS[t]
                act.wait_ge(s_f_gb, 2 * t + 2)
                A(Yg[0:R, 2 * t, :], Yg[0:R, 2 * t, :], ACT.Sigmoid).then_inc(s_f_sig, 1)
                act.wait_ge(s_f_h3, t + 1)
                rms(t, h1[0:R, t, :], 15 + t, yout[:, t, :], s_f_r2)

            norm_h2(0)
            norm_h2(1)
            for t in range(NT):
                if t + 2 < NT:
                    norm_h2(t + 2)
                final(t)

        @block.gpsimd
        def _(pool):
            step = Steps(pool, own_pool)
            step(pool.memset(idle[:, :], 0.0))
            pool.memset(xbc[:, :, 0:TAPS - 1], 0.0)
            pool.memset(v[:, :, 0:BUF], 0.0).then_inc(s_pads, 1)
            step(pool.memset(zeros, 0.0))
            step(pool.memset(int_w[:, :], NONE))
            pool.dma_start(slots_dram.rearrange("(p s) a -> p (s a)", s=NBT * S // P), int_w[:, 0:NBT * S // P]
                           ).then_inc(st_slots, 16)
            pool.wait_ge(s_inproj_out, XT)
            pool.dma_start(y_dram[NE * S:NB * S, :].rearrange("(p r) (h n) -> p (r h) n", p=P, n=512),
                           zeros.unsqueeze(1).to_broadcast((P, EXTRA * S * 2 // P, 512))).then_inc(st_zeros, 16)
            pool.tensor_copy(cst[:, :, 0:3], xbc[:, :, SEQ:SEQ + 3])
            pool.tensor_copy(cst[:, :, 3:11], xcs[:, :, :, 3]).then_inc(s_cst_ready, 1)
            pool.wait_ge(s_scan1_out, 17)
            pool.wait_ge(ld_hs, 64)

            def bn(view):
                return view.rearrange("p (b n) -> p b n", n=NST)

            for t in range(4):
                step(pool.tensor_tensor(bn(hs[:, t]), bn(hs[:, t]), dx[:, t, 0:NS].unsqueeze(2).to_broadcast((P, NS, NST)), ALU.mult))
                step(pool.tensor_tensor(bn(stmp[:, 0]), bn(BC[:, t // 2]), xdtT[:, t, SEQ:TOK].unsqueeze(2).to_broadcast((P, NS, NST)), ALU.mult))
                step(pool.tensor_tensor(hs[:, t], hs[:, t], stmp[:, 0], ALU.add))
                step(pool.tensor_tensor(stmp[:, 1], hs[:, t], BC[:, 2 + t // 2], ALU.mult))
                half = NST // 2
                while half > 1:
                    lo = bn(stmp[:, 1])[:, :, 0:half]
                    step(pool.tensor_tensor(lo, lo, bn(stmp[:, 1])[:, :, half:2 * half], ALU.add))
                    half //= 2
                ins = pool.tensor_tensor(ys[:, t, :], bn(stmp[:, 1])[:, :, 0], bn(stmp[:, 1])[:, :, 1], ALU.add)
                if t < 3:
                    step(ins)
            ins.then_inc(s_samp_done, 1)
            pool.wait_ge(s_inproj_out, len(COLS))
            pool.tensor_copy(vst[:, :, 0:BUF], v[:, :, SEQ:SEQ + BUF])
            pool.tensor_copy(vst[:, :, BUF:23], vs[:, :, :]).then_inc(s_vst_ready, 1)
            for g in range(NG):
                src = v[:, g, :]
                lo = 1
                for q in range(g + 1):
                    dst = win[q % 2][:, 0:SEQ + BUF]
                    sh = 1 << q
                    lo = 2 * sh - 1
                    step(pool.tensor_tensor(dst[:, lo:], src[:, lo:SEQ + BUF], src[:, lo - sh:SEQ + BUF - sh], ALU.add))
                    src = dst
                step(pool.tensor_tensor(mixT[:, g, 0:16], src[:, BUF:BUF + 16], const[:, C_INV + 16 * g:C_INV + 16 * g + 16], ALU.mult))
                step(pool.tensor_scalar(mixT[:, g, 16:SEQ], src[:, BUF + 16:BUF + SEQ], 1.0 / WINS[g], None, ALU.mult))
                step(pool.tensor_tensor(vsum[:, g, :], vsum[:, g, :], vs[:, g, :], ALU.add))
                step(pool.tensor_scalar(mixT[:, g, SEQ:TOK], vsum[:, g, :], 1.0 / WINS[g], None, ALU.mult))
                step(pool.tensor_tensor(mixT[:, g, SEQ:TOK], mixT[:, g, SEQ:TOK], vs[:, g, :], ALU.subtract))
                pool.tensor_tensor(mixT[:, g, 0:SEQ], mixT[:, g, 0:SEQ], v[:, g, BUF:BUF + SEQ], ALU.subtract).then_inc(s_m_ready, 1)
            pool.wait_ge(s_m_ready, NG)
            pool.wait_ge(s_rt_ready, 1)
            pool.wait_ge(st_slots, 16)
            for t in range(NT):
                R = ROWS[t]
                for k in range(2):
                    pool.indirect_dma_start(slots_dram, bass.IndirectOffsetOnAxis(ap=slot_i[0:R, t, k:k + 1], axis=0),
                                            tok_i[0:R, t:t + 1], None).then_inc(slots_filled, 16)
            pool.wait_ge(slots_filled, 16 * 2 * NT)
            n = pool.value_load(nloop[0:1, 0:1], min_val=NE // U, max_val=NB // U)
            pool.wait_ge(u_stored[0], 48)
            pool.wait_ge(u_stored[1], 32)
            pool.wait_ge(s_g_init, 1)
            for q in range(2):
                pool.memset(idle[:, 5 + q:6 + q], 0.0).then_inc(y_written[q], 16)

            def idle_step(before):
                pool.wait_ge(s_idle, before)
                pool.tensor_tensor(idle[:, 0:1], idle[:, 1:2], idle[:, 2:3], ALU.add).then_inc(s_idle, 1)

            pool.tensor_tensor(idle[:, 0:1], idle[:, 1:2], idle[:, 2:3], ALU.add).then_inc(s_idle, 1)

            def gather(q):
                pool.indirect_dma_start(G[:, q, :], None, u_dram, bass.IndirectOffsetOnAxis(ap=idx_i[q][:, 0:1], axis=0),
                                        bounds_check=TOK - 1, oob_is_err=False).then_inc(g_full[q], 16)

            for q in range(2):
                pool.dma_start(idx_i[q][:, :], slots_dram[q * S:(q + 1) * S, :]).then_inc(idx_full[q], 16)
            for q in range(2):
                pool.wait_ge(idx_full[q], 16)
                gather(q)
            with pool.Fori(0, n) as i:
                for s in range(U):
                    pool.wait_ge(s_T_done, i * U + (s + 1))
                    pool.wait_ge(g_full[s % 2], i * 32 + 16 * (s // 2 + 1))
                    idle_step(i * 2 * U + (2 * s + 1))
                    pool.dma_start(idx_i[s % 2][:, :], slots_dram[bass.ds(i * (U * S) + (s + 2) * S, S), :]
                                   ).then_inc(idx_full[s % 2], 16)
                    pool.wait_ge(idx_full[s % 2], i * 32 + 16 * (s // 2 + 2))
                    idle_step(i * 2 * U + (2 * s + 2))
                    gather(s % 2)
            pool.wait_ge(y_written[0], n * 32 + 16)
            pool.wait_ge(y_written[1], n * 32 + 16)
            pool.wait_ge(s_idle, n * 2 * U + 1)
            pool.tensor_tensor(idle[:, 0:1], idle[:, 1:2], idle[:, 2:3], ALU.add).then_inc(s_loop_out, 1)
            pool.wait_ge(s_loop_out, 1)
            for t in range(NT):
                R = ROWS[t]
                for k in range(2):
                    pool.indirect_dma_start(Yg[0:R, 2 * t + k, :], None, y_dram,
                                            bass.IndirectOffsetOnAxis(ap=slot_i[0:R, t, k:k + 1], axis=0)
                                            ).then_inc(yg_full[t], 16)

        @block.vector
        def _(dve):
            step = Steps(dve, own_dve)
            tt, ts, stt = dve.tensor_tensor, dve.tensor_scalar, dve.scalar_tensor_tensor

            def last(ins, signal, count):
                ins.then_inc(signal, 1)
                dve.wait_ge(signal, count)

            def tiles(bank, n=4):
                return bank.rearrange("p (c l) -> p c l", l=bank.shape[1] // n)

            def gains(col, k, n, m):
                return vec[:, col + k:col + k + n].unsqueeze(2).to_broadcast((P, n, m))

            dve.wait_ge(s_vec_T, 1)
            step(dve.tensor_copy(vec, PS[6][:, 0:NV]))

            def norm_x(t):
                R = ROWS[t]
                dve.wait_ge(s_rstd_x, t + 1)
                if t >= 2:
                    dve.wait_ge(s_xT_done, 2 * (t - 1))
                ts(row[0:R, t % 2, :], h1[0:R, t, :], rstd[0:R, t:t + 1], None, ALU.mult).then_inc(s_xn_ready, 1)

            def take_x(j):
                t, half = j // 2, j % 2
                R = ROWS[t]
                dve.wait_ge(s_xT_done, j + 1)
                tt(aT[:, 4 * half:4 * half + 4, t * P:t * P + R], tiles(PS[4 + j % 2][:, :])[:, :, 0:R],
                   gains(V_MIX, 4 * half, 4, R), ALU.mult).then_inc(s_aT_taken, 1)

            norm_x(0)
            norm_x(1)
            for t in range(NT):
                take_x(2 * t)
                take_x(2 * t + 1)
                if t + 2 < NT:
                    norm_x(t + 2)
            dve.wait_ge(s_pads, 1)
            for m in range(XT):
                dve.wait_ge(s_inproj_out, m + 1)
                acc = xc[:, m, 0:SEQ]
                step(ts(acc, xbc[:, m, 0:SEQ], vec[:, V_CW + m:V_CW + m + 1], vec[:, V_CB + m:V_CB + m + 1],
                        ALU.mult, ALU.add))
                for k in range(1, TAPS):
                    col = V_CW + k * XT + m
                    ins = stt(acc, xbc[:, m, k:k + SEQ], vec[:, col:col + 1], acc, ALU.mult, ALU.add)
                    if k < TAPS - 1:
                        step(ins)
                ins.then_inc(s_conv_pre, 1)
            dve.wait_ge(s_states_in, 1)
            taps = vec[:, V_CW:V_CW + TAPS * XT].rearrange("p (k m) -> p m k", m=XT)
            step(tt(cprod, xcs, taps.unsqueeze(2).to_broadcast((P, XT, NS, TAPS)), ALU.mult))
            step(dve.tensor_reduce(xc[:, :, SEQ:TOK], cprod, AX.X, ALU.add))
            tt(xc[:, :, SEQ:TOK], xc[:, :, SEQ:TOK], gains(V_CB, 0, XT, NS), ALU.add).then_inc(s_convs_pre, 1)
            raw, neg, e, u, lnu, dta = dtw
            dve.wait_ge(s_inproj_out, XT + 1)
            stt(neg, raw, -1.0, raw, ALU.mult, ALU.min).then_inc(s_dt_neg, 1)
            dve.wait_ge(s_dt_exp, 1)
            last(ts(u, e, 1.0, None, ALU.add), s_dt_u, 1)
            step(stt(neg, u, -1.0, e, ALU.add, ALU.subtract))
            step(dve.reciprocal(dt, u))
            step(tt(neg, neg, dt, ALU.mult))
            dve.wait_ge(s_dt_ln, 1)
            step(stt(raw, raw, 0.0, lnu, ALU.max, ALU.add))
            step(tt(dt, raw, neg, ALU.subtract))
            dve.wait_ge(s_exp_a, 1)
            step(ts(hv[:, 3:4], hv[:, 2:3], -1.0, None, ALU.mult))
            last(ts(dta, dt, hv[:, 3:4], None, ALU.mult), s_dta_ready, 1)
            for c in range(NC_):
                cc = slice(c * P, (c + 1) * P)
                ins = dve.tensor_tensor_scan(acs[:, cc], ones[0:NH, :], dta[:, cc], 0.0, ALU.mult, ALU.add)
            last(ins, s_dt_ready, 1)
            dve.wait_ge(s_conv_out, XT + 1)
            i2 = const[:, C_I2:C_I2 + NST].unsqueeze(1).to_broadcast((P, NS, NST))
            for kind in range(2):
                tt(stmp[:, kind, :].rearrange("p (b n) -> p b n", n=NST),
                   xc[:, 4 + kind, SEQ:TOK].unsqueeze(2).to_broadcast((P, NS, NST)), i2, ALU.mult).then_inc(s_diag_ready, 1)
            dve.wait_ge(s_cst_ready, 1)
            for t in range(4):
                dve.wait_ge(s_scan1_done, t + 1)
                for h in range(2):
                    hh = slice(h * HALF, (h + 1) * HALF)
                    ins = tt(xdtT[:, t, hh], PS[4 + 2 * (t % 2) + h][:, 0:HALF], xc[:, t, hh], ALU.mult)
                ins.then_inc(s_scan1_out, 1)
            dve.wait_ge(s_scan1_done, 5)
            dve.tensor_copy(acsT, PS[4][:, 0:NC_ * NH].rearrange("p (c h) -> p c h", h=NH)).then_inc(s_scan1_out, 1)
            dve.wait_ge(s_scan1_done, 6)
            dve.tensor_copy(Btok, tiles(PS[5][:, :])).then_inc(s_scan1_out, 1)
            causal = const[:, C_CAUSAL:C_CAUSAL + P].unsqueeze(1).to_broadcast((P, NC_, P))
            for g in range(2):
                dve.wait_ge(s_scan1_done, 7 + g)
                tt(tiles(Gm[:, g, :]), tiles(PS[6 + g][:, :]), causal, ALU.mult).then_inc(s_scan1_out, 1)
            for c in range(NC_):
                dve.wait_ge(s_scan1_done, 9 + c)
                dve.tensor_copy(xtok[:, c, :], PS[4 + c][:, :]).then_inc(s_scan1_out, 1)
            dve.wait_ge(s_scan1_done, 13)
            dve.tensor_copy(dx, PS[4][:, 0:4 * (NS + 1)].rearrange("p (t b) -> p t b", b=NS + 1)).then_inc(s_scan1_out, 1)
            for q in range(4):
                dve.wait_ge(s_scan1_done, 14 + q)
                if q == 3:
                    dve.wait_ge(st_zeros, 16)
                dve.tensor_copy(BC[:, q, :], PS[5 + q % 3][:, :]).then_inc(s_scan1_out, 1)
            dve.wait_ge(s_scan1_out, 17)

            def head_seg(h):
                dve.wait_ge(s_R_done, h + 1)
                bank = PS[4 + h % 4]
                dve.tensor_copy(RL[:, :, h], tiles(bank[:, :])[:, :, P - 1])
                for c in range(NC_):
                    cc = slice(c * P, (c + 1) * P)
                    ins = ts(seg[:, h % 2, cc], bank[:, cc], acsT[:, c, h:h + 1], 0.0, ALU.subtract, ALU.min)
                ins.then_inc(s_R_out, 1)

            def head_scores(h):
                dve.wait_ge(s_seg_exp, h + 1)
                if h == 4:
                    dve.wait_ge(s_samp_done, 1)
                last(tt(M[:, h, :], seg[:, h % 2, :], Gm[:, h // 4, :], ALU.mult), s_M_ready, h + 1)

            head_seg(0)
            for h in range(NH):
                if h + 1 < NH:
                    head_seg(h + 1)
                head_scores(h)
            dve.wait_ge(s_R_out, NH)
            tt(te, RL, acsT, ALU.subtract).then_inc(s_te_in, 1)
            dve.wait_ge(s_te_ready, 1)
            dve.wait_ge(s_inproj_done, len(COLS))
            for c in range(NC_):
                tt(xdtE[:, c, :].rearrange("p (h q) -> p h q", q=HD), xtok[:, c, :].rearrange("p (h q) -> p h q", q=HD),
                   te[:, c, :].unsqueeze(2).to_broadcast((P, NH, HD)), ALU.mult).then_inc(s_xdtE_ready, 1)
            dve.wait_ge(s_S_done, 1)
            last(dve.tensor_copy(H[:, 0, :], PS[4][:, :]), s_S_out, 1)
            for c in range(1, NC_):
                step(tt(H[:, c, :].rearrange("p (h q) -> p h q", q=HD), H[:, c - 1, :].rearrange("p (h q) -> p h q", q=HD),
                        cd[:, c, :].unsqueeze(2).to_broadcast((P, NH, HD)), ALU.mult))
                dve.wait_ge(s_S_done, c + 1)
                last(tt(H[:, c, :], H[:, c, :], PS[4 + c][:, :], ALU.add), s_S_out, c + 1)
            dve.wait_ge(s_eE_out, 4)
            for t in range(4):
                D_col = dx[:, t, NS:NS + 1]
                dve.wait_ge(s_Y_done, t + 1)
                step(stt(y[:, t, :], xc[:, t, 0:SEQ], D_col, PS[t][:, :], ALU.mult, ALU.add))
                dve.wait_ge(s_YO_done, t + 1)
                last(tt(eE[:, t, P:SEQ], PS[4 + t][:, P:SEQ], eE[:, t, P:SEQ], ALU.mult), s_Y_out, t + 1)
                step(tt(y[:, t, P:SEQ], y[:, t, P:SEQ], eE[:, t, P:SEQ], ALU.add))
                dve.wait_ge(s_samp_done, 1)
                step(stt(ys[:, t, :], xc[:, t, SEQ:TOK], D_col, ys[:, t, :], ALU.mult, ALU.add))
                tt(y[:, t, :], y[:, t, :], zs[:, t, 0:SEQ], ALU.mult)
                last(tt(ys[:, t, :], ys[:, t, :], zs[:, t, SEQ:TOK], ALU.mult), s_gated, t + 1)
            for g in range(NG):
                dve.wait_ge(s_pool_done, g + 1)
                for h in range(2):
                    ins = ts(mixT[:, g, h * HALF:(h + 1) * HALF], PS[6 + h][:, 0:HALF], vec[:, V_PB + g:V_PB + g + 1],
                             vec[:, V_PS + g:V_PS + g + 1], ALU.add, ALU.mult)
                ins.then_inc(s_mixP_ready, 1)
            for t in range(4):
                dve.wait_ge(s_gn_out, t // 2 + 1)
                wn = vec[:, V_SN + t:V_SN + t + 1]
                stt(mixT[:, 4 + t, 0:SEQ], y[:, t, :], wn, rsg[:, t // 2, 0:SEQ], ALU.mult, ALU.mult)
                stt(mixT[:, 4 + t, SEQ:TOK], ys[:, t, :], wn, rsg[:, t // 2, SEQ:TOK], ALU.mult, ALU.mult).then_inc(s_mix_ready, 1)

            def residual(t):
                R = ROWS[t]
                dve.wait_ge(s_outp_done, t + 1)
                for h in range(2):
                    hh = slice(h * 512, (h + 1) * 512)
                    ins = tt(h1[0:R, t, hh], PS[2 * (t % 2) + h][0:R, :], h1[0:R, t, hh], ALU.add)
                ins.then_inc(s_outp_out, 1)

            def norm_u(t):
                R = ROWS[t]
                dve.wait_ge(s_r_rstd, t + 1)
                if t < 2:
                    dve.wait_ge(st_pool, 32)
                else:
                    dve.wait_ge(u_stored[t % 2], 16 * (t // 2))
                    dve.wait_ge(s_uTr_done, 2 * (t - 1))
                ts(row[0:R, t % 2, :], h1[0:R, t, :], rstd[0:R, 5 + t:6 + t], None, ALU.mult).then_inc(s_u_ready, 1)

            def take_rows(bank, t, half, gain_col, signal):
                R = ROWS[t]
                tt(uTr[:, t % 2, :].rearrange("p (k c) -> p k c", c=P)[:, 4 * half:4 * half + 4, 0:R],
                   tiles(bank[:, :])[:, :, 0:R], gains(gain_col, 4 * half, 4, R), ALU.mult).then_inc(signal, 1)

            def take_u(t):
                if t >= 2:
                    dve.wait_ge(s_lg_done, t - 1)
                for half in range(2):
                    dve.wait_ge(s_uTr_done, 2 * t + half + 1)
                    take_rows(PS[4 + half], t, half, V_FFN, s_uTr_out)

            def take_logits(t):
                R = ROWS[t]
                dve.wait_ge(s_lg_done, t + 1)
                last(tt(L[0:R, t, :], PS[6][0:R, t * 36:(t + 1) * 36], rbias[0:R, :], ALU.add), s_lg_out, t + 1)

            residual(0)
            dve.wait_ge(st_hs, 64)
            step(dve.memset(L, 0.0))
            step(dve.memset(Lg, -3.0e38))
            dve.wait_ge(ld_rt, 64)
            norm_u(0)
            residual(1)
            norm_u(1)
            for t in range(NT):
                take_u(t)
                if t + 2 < NT:
                    residual(t + 2)
                    norm_u(t + 2)
                take_logits(t)
            iota = const[:, C_IOTA:C_IOTA + NE]
            step(dve.tensor_copy(Lg[:, :, 0:4], L[:, :, 0:4]))
            for t in range(NT):
                ins = dve.max(gmax[:, t, :], Lg[:, t, :])
            step(ins)
            for t in range(NT):
                ins = dve.max_index(gidx[:, t, :], gmax[:, t, :], Lg[:, t, :])
            step(ins)
            step(dve.tensor_copy(gf, gidx[:, :, 0]))
            tt(ex4, L[:, :, 0:4], gmax[:, :, 0:1].to_broadcast((P, NT, 4)), ALU.subtract)
            step(tt(m4, iota[:, 0:4].unsqueeze(1).to_broadcast((P, NT, 4)), gf.unsqueeze(2).to_broadcast((P, NT, 4)), ALU.is_equal))
            t48 = tmp[:, :, 0:NE].rearrange("p t (g e) -> p t g e", g=4)
            for t in range(NT):
                ins = tt(t48[:, t], L[:, t, 4:36].rearrange("p (g e) -> p g e", g=4),
                         m4[:, t, :].unsqueeze(2).to_broadcast((P, 4, 8)), ALU.mult)
            step(ins)
            step(dve.tensor_reduce(es, t48.rearrange("p t g e -> p t e g"), AX.X, ALU.add))
            for t in range(NT):
                ins = dve.max(ev[:, t, :], es[:, t, :])
            step(ins)
            for t in range(NT):
                ins = dve.max_index(eidx[:, t, :], ev[:, t, :], es[:, t, :])
            step(ins)
            tt(e21, ev[:, :, 1], ev[:, :, 0], ALU.subtract).then_inc(s_rt_a, 1)
            step(dve.tensor_copy(eid, eidx[:, :, 0:2]))
            step(stt(eid, gf.unsqueeze(2).to_broadcast((P, NT, 2)), 8.0, eid, ALU.mult, ALU.add))
            step(tt(eid, eid, const[:, C_BAD:C_BAD + NT].unsqueeze(2).to_broadcast((P, NT, 2)), ALU.add))
            oh4 = oh.rearrange("p t (k e) -> p (t k) e", e=NE)
            tm4 = tmp.rearrange("p t (k e) -> p (t k) e", e=NE)
            eidf = eid.rearrange("p t k -> p (t k)")
            step(tt(oh4, iota.unsqueeze(1).to_broadcast((P, 2 * NT, NE)), eidf.unsqueeze(2).to_broadcast((P, 2 * NT, NE)), ALU.is_equal))
            dve.tensor_copy(bef, const[:, C_BEFORE:C_BEFORE + P])
            dve.tensor_copy(oneb, ones)
            tt(ohs.rearrange("p (t e) -> p t e", e=NE), oh[:, :, 0:NE], oh[:, :, NE:2 * NE], ALU.add).then_inc(s_oh_ready, 1)
            dve.wait_ge(s_rt_b, 1)
            step(dve.tensor_reduce(gw, ex4, AX.X, ALU.add))
            step(stt(gw, e21, 1.0, gw, ALU.add, ALU.mult))
            step(dve.reciprocal(wgt[:, :, 0], gw))
            step(tt(wgt[:, :, 1], wgt[:, :, 0], e21, ALU.mult))
            dve.wait_ge(s_cnt_done, 1)
            dve.wait_ge(st_slots, 16)
            for t in range(NT):
                tt(tmp[:, t, :].rearrange("p (k e) -> p k e", e=NE), oh[:, t, :].rearrange("p (k e) -> p k e", e=NE),
                   PS[7][:, t * NE:(t + 1) * NE].unsqueeze(1).to_broadcast((P, 2, NE)), ALU.mult)
            last(ts(ovn, PS[7][:, NT * NE:(NT + 1) * NE], float(S - 1), None, ALU.add), s_cnt_taken, 1)
            rkf = rk.rearrange("p t k -> p (t k)")
            step(dve.tensor_reduce(rkf, tm4, AX.X, ALU.add))
            step(dve.tensor_copy(int_w[:, :], ovn))
            step(ts(int_w[:, :], int_w[:, :], 6, None, ALU.arith_shift_right))
            step(dve.tensor_copy(ovn, int_w[:, :]))
            step(ts(ovn, ovn, -1.0, 0.0, ALU.add, ALU.max))
            step(dve.tensor_tensor_scan(ove, ones[:, 0:NE], ovn, 0.0, ALU.mult, ALU.add))
            step(tt(ovb, ove, ovn, ALU.subtract))
            step(tt(tm4, oh4, ovb.unsqueeze(1).to_broadcast((P, 2 * NT, NE)), ALU.mult))
            step(dve.tensor_reduce(ovt.rearrange("p t k -> p (t k)"), tm4, AX.X, ALU.add))
            step(dve.tensor_copy(slot_i[:, :, :], rk))
            si = slot_i[:, :, :]
            step(ts(si, si, 6, None, ALU.arith_shift_right))
            step(dve.tensor_copy(rq, si))
            step(stt(rr, rq, -float(S), rk, ALU.mult, ALU.add))
            step(ts(cmp0, rq, 0.5, None, ALU.is_gt))
            step(tt(ovt, ovt, rq, ALU.add))
            step(stt(ovt, ovt, float(NE - 1), eid, ALU.add, ALU.subtract))
            step(tt(ovt, ovt, cmp0, ALU.mult))
            step(tt(ovt, ovt, eid, ALU.add))
            step(stt(rr, ovt, float(S), rr, ALU.mult, ALU.add))
            step(dve.tensor_copy(si, rr))
            step(dve.tensor_copy(tok_i[:, :], const[:, C_TOKID:C_TOKID + NT]))
            t16 = tmp[0:1, :, :].rearrange("p t e -> p (t e)")
            for j in range(0, EXTRA, 8):
                tj = t16[:, 0:8 * NE].rearrange("p (j e) -> p j e", e=NE)
                step(tt(tj, ove[0:1, :].unsqueeze(1).to_broadcast((1, 8, NE)),
                        iota[0:1, j:j + 8].unsqueeze(2).to_broadcast((1, 8, NE)), ALU.is_le))
                step(dve.tensor_reduce(rk.rearrange("p t k -> p (t k)")[0:1, 0:8], tj, AX.X, ALU.add))
                step(ts(btab[:, NE + j:NE + j + 8], rk.rearrange("p t k -> p (t k)")[0:1, 0:8], float(NE - 1), None, ALU.min))
            step(dve.tensor_copy(btab[:, 0:NE], iota[0:1, :]))
            step(ts(rk[0:1, 0, :], ove[0:1, NE - 1:NE].to_broadcast((1, 2)), float(NE + U - 1), None, ALU.add))
            step(dve.tensor_copy(nloop[:, :], rk[0:1, 0, :]))
            step(ts(nloop[:, :], nloop[:, :], 2, None, ALU.arith_shift_right))
            ts(nloop[:, 1:2], nloop[:, 1:2], -1, None, ALU.add).then_inc(s_rt_ready, 1)
            dve.memset(G, 0.0).then_inc(s_g_init, 1)
            dve.memset(idle[:, 4:5], 0.0).then_inc(s_ysb_free, 1)

            def take_block(b2):
                tt(uT[:, b2, :].rearrange("p (k c) -> p k c", c=S), PS[6 + b2][:, :].rearrange("p (k c) -> p k c", c=S),
                   gains(V_FFN, 0, KT, S), ALU.mult).then_inc(s_uT_ready, 1)

            n = dve.value_load(nloop[0:1, 0:1], min_val=NE // U, max_val=NB // U)
            dve.wait_ge(s_T_done, 1)
            take_block(0)
            with dve.Fori(0, n) as i:
                for s in range(U):
                    dve.wait_ge(s_sg_ready, i * U + (s + 1))
                    dve.wait_ge(s_up_done, i * U + (s + 1))
                    tt(actT[:, s % 2, :], PS[1][:, 0:2 * S], sg[:, s % 2, :], ALU.mult).then_inc(s_act_ready, 1)
                    dve.wait_ge(s_T_done, i * U + (s + 2))
                    take_block((s + 1) % 2)

            def combine(t):
                R = ROWS[t]
                dve.wait_ge(yg_full[t], 32)
                step(stt(h1[0:R, t, :], Yg[0:R, 2 * t, :], wgt[0:R, t, 0:1], h1[0:R, t, :], ALU.mult, ALU.add))
                stt(h1[0:R, t, :], Yg[0:R, 2 * t + 1, :], wgt[0:R, t, 1:2], h1[0:R, t, :], ALU.mult, ALU.add).then_inc(s_f_h2, 1)
                dve.wait_ge(s_f_rstd, t + 1)
                if t >= 2:
                    dve.wait_ge(s_f_T, 2 * (t - 1))
                ts(row[0:R, t % 2, :], h1[0:R, t, :], rstd[0:R, 10 + t:11 + t], None, ALU.mult).then_inc(s_f_v, 1)

            def take_v(t):
                if t >= 2:
                    dve.wait_ge(s_f_g, 2 * (t - 1))
                for half in range(2):
                    dve.wait_ge(s_f_T, 2 * t + half + 1)
                    take_rows(PS[6 + half], t, half, V_PLE, s_f_vT)

            def finish(t):
                R = ROWS[t]
                gate = Yg[0:R, 2 * t, :]
                for h in range(2):
                    hh = slice(h * 512, (h + 1) * 512)
                    dve.wait_ge(s_f_g, 2 * t + h + 1)
                    tt(gate[:, hh], PS[2 * (t % 2) + h][0:R, :], bple[0:R, hh], ALU.add).then_inc(s_f_gb, 1)
                dve.wait_ge(s_f_sig, t + 1)
                step(tt(gate, gate, pp[0:R, t, :], ALU.mult))
                last(tt(h1[0:R, t, :], h1[0:R, t, :], gate, ALU.add), s_f_h3, t + 1)
                dve.wait_ge(s_f_r2, t + 1)
                stt(yout[0:R, t, :], h1[0:R, t, :], rstd[0:R, 15 + t:16 + t], bfin[0:R, :], ALU.mult, ALU.mult).then_inc(s_f_y, 1)

            dve.wait_ge(ld_bias, 32)
            combine(0)
            take_v(0)
            combine(1)
            take_v(1)
            for t in range(NT):
                if t + 2 < NT:
                    combine(t + 2)
                    take_v(t + 2)
                finish(t)


_INS = ["x_prompt", "x_sample", "p_prompt", "p_sample", "state_pool", "state_conv", "state_ssm", "norm_mix",
        "w_in", "pool_lin_w", "pool_lin_b", "pool_scale", "conv_w", "conv_b", "dt_bias", "a_log", "d_skip",
        "ssd_norm", "w_out", "norm_ffn", "router_grp_w", "router_grp_b", "router_exp_w", "router_exp_b",
        "exp_w_gate", "exp_w_up", "exp_w_down", "norm_ple", "ple_gate_w", "ple_gate_b", "ple_proj_w", "norm_final"]
_OUTS = [("y_p", (1, SEQ, D)), ("y_s", (NS, 1, D)), ("pool_p", (1, 1, BUF, PW)), ("conv_p", (1, 1, TAPS - 1, CONV)),
         ("ssm_p", (1, 1, NH, HD, NST)), ("pool_s", (1, NS, BUF, PW)), ("conv_s", (1, NS, TAPS - 1, CONV)),
         ("ssm_s", (1, NS, NH, HD, NST))]


def kernel(**inputs):
    import numpy as np
    import concourse.bacc as bacc
    from concourse.bass_utils import run_bass_kernel_spmd

    nc = bacc.Bacc("TRN2", target_bir_lowering=False, num_devices=1)
    arrays = {f"in_{name}": np.ascontiguousarray(inputs[name]) for name in _INS}
    for name in ("exp_w_gate", "exp_w_up", "exp_w_down"):
        w = arrays[f"in_{name}"]
        arrays[f"in_{name}"] = w.reshape(NE, w.shape[3], w.shape[4])
    arrays["in_consts"], arrays["in_heads"] = shape_constants(np)
    a = {k[3:]: nc.dram_tensor(k, v.shape, F32, kind="ExternalInput").ap() for k, v in arrays.items()}
    o = {name: nc.dram_tensor(f"out_{name}", shape, F32, kind="ExternalOutput").ap() for name, shape in _OUTS}
    build(nc, a, o)
    r = run_bass_kernel_spmd(nc, [arrays], core_ids=[0])
    return tuple(r.results[0][f"out_{name}"] for name, _ in _OUTS)
```

```python
import concourse.bass as bass
from concourse import mybir
from contextlib import ExitStack

F32 = mybir.dt.float32
BF16 = mybir.dt.bfloat16
I32 = mybir.dt.int32
U32 = mybir.dt.uint32
ALU = mybir.AluOpType
ACT = mybir.ActivationFunctionType
AX = mybir.AxisListType

P = 128
D = 1024
KT = D // P
SEQ, NS = 512, 8
TOK = SEQ + NS
HALF = TOK // 2
NT = 5
ROWS = [128, 128, 128, 128, NS]
PW, NG, WINS, BUF = 512, 4, (2, 4, 8, 16), 15
NH, HD, NST = 8, 64, 64
XT = 6
CONV = XT * P
TAPS = 4
NC_ = SEQ // P
IN_DIM = 1800
NE, FF, PLE = 32, 256, 256
S = 64
EXTRA = 2 * TOK // S
NB = NE + EXTRA
U = 4
NBT = NB + U
NONE = 1 << 20
EPS = 1e-6
GU = KT * 2 * FF
DN = 2 * D

V_MIX, V_PB, V_PS, V_CW, V_CB, V_SN, V_FFN, V_PLE, NV = 0, 8, 12, 16, 40, 46, 50, 58, 66

C_ID, C_CAUSAL, C_BEFORE, C_ONES, C_I2, C_INV, C_POOLSEL, C_IOTA, C_TOKID, C_BAD, C_INVW, C_EPS = (
    0, 128, 256, 384, 512, 576, 640, 672, 704, 709, 714, 718)
NCONST = 719
H_EXP, H_ROW, NHEAD = 0, 512, 1536


def shape_constants(np):
    c = np.zeros((P, NCONST), np.float32)
    i = np.arange(P)
    c[:, C_ID:C_ID + P] = np.eye(P)
    c[:, C_CAUSAL:C_CAUSAL + P] = i[None, :] >= i[:, None]
    c[:, C_BEFORE:C_BEFORE + P] = i[:, None] < i[None, :]
    c[:, C_ONES:C_ONES + P] = 1
    c[:, C_I2:C_I2 + 64] = (i[:, None] % 64) == np.arange(64)[None, :]
    for g, w in enumerate(WINS):
        c[:, C_INV + 16 * g:C_INV + 16 * g + 16] = 1.0 / np.minimum(np.arange(16) + 1, w)
        for b in range(NS):
            for tau in range(BUF):
                c[b * BUF + tau, C_POOLSEL + 8 * g + b] = tau >= BUF + 1 - w
        c[:, C_INVW + g] = 1.0 / w
    c[:, C_IOTA:C_IOTA + 32] = np.arange(32)
    for t in range(NT):
        c[:, C_TOKID + t] = t * P + i
        c[:, C_BAD + t] = 4096.0 * (i >= ROWS[t])
    c[:, C_EPS] = EPS
    h = np.zeros((NH, NHEAD), np.float32)
    for t in range(4):
        for p in range(P):
            h[2 * t + p // 64, H_EXP + t * P + p] = 1
    for k in range(NH):
        h[k, H_ROW + k * P:H_ROW + (k + 1) * P] = 1
    return c, h


def build(nc, a, o):
    ctx = ExitStack()
    with ctx:
        def sem(name):
            return ctx.enter_context(nc.semaphore(name))

        class Steps:

            def __init__(self, eng, own):
                self.eng, self.own, self.n = eng, own, 0

            def __call__(self, ins):
                self.n += 1
                ins.then_inc(self.own, 1)
                self.eng.wait_ge(self.own, self.n)

        top = [0]

        def region(n):
            start = top[0]
            top[0] += (n + 7) // 8 * 8
            return start

        R_const = region(NCONST)
        R_x = region(NT * D)
        R_gu = region(U * GU)
        R_dn = region(2 * DN)
        R_aT = region(KT * TOK)
        R_v = region(NG * (BUF + TOK))
        R_xc = region(XT * TOK)
        R_xbc = region(XT * (SEQ + TAPS - 1))
        R_z = region(4 * TOK)
        R_row = region(2 * D)
        R_tb = region(2 * D)
        R_g = region(2 * D)
        R_act = region(2 * FF)
        R_samp = region(3072)
        R_dt = region(2 * TOK)
        R_small = region(1104)
        mem = ctx.enter_context(nc.sbuf_tensor("mem", [P, top[0]], F32))

        def at(off, *shape, rows=P):
            n = 1
            for s in shape:
                n *= s
            view = mem[0:rows, off:off + n]
            if len(shape) == 2:
                view = view.rearrange("p (a b) -> p a b", b=shape[1])
            if len(shape) == 3:
                view = view.rearrange("p (a b c) -> p a b c", b=shape[1], c=shape[2])
            return view

        const = at(R_const, NCONST)
        ident = const[:, C_ID:C_ID + P]
        ones = const[:, C_ONES:C_ONES + P]
        eps = const[:, C_EPS:C_EPS + 1]
        h1 = at(R_x, NT, D)
        w_in = at(R_gu, KT, IN_DIM)
        gu = [at(R_gu + s * GU, 2 * KT, FF) for s in range(U)]
        dn = [at(R_dn + s * DN, 2, D) for s in range(2)]
        w_out = at(R_gu + 2 * GU, KT, D)
        aT = at(R_aT, KT, TOK)
        mixT = aT
        xbc = at(R_xbc, XT, SEQ + TAPS - 1)
        xdtT = at(R_xbc, 4, TOK)
        zs = at(R_z, 4, TOK)
        v = at(R_v, NG, BUF + TOK)
        xc = at(R_xc, XT, TOK)
        row = at(R_row, 2, D)
        junk = at(R_g, D)
        spool = at(R_act, PW, rows=NS * BUF)
        sconv = at(R_dt, CONV, rows=NS * (TAPS - 1))
        headc = at(R_tb, NHEAD, rows=NH)
        w_lin = at(R_tb + NHEAD, NG, P)
        fin = at(R_dn, 4, NST)
        stage_c = at(R_gu + KT * IN_DIM, CONV, rows=11)
        stage_v = at(R_g + D, PW, rows=23)
        H = at(R_gu, NC_, 512)
        xdtE = at(R_gu + 2048, NC_, 512)
        eE = at(R_gu + 4096, 4, SEQ)
        rsg = at(R_gu + 4096, 2, TOK)
        y = at(R_gu + 6144, 4, SEQ)
        dtw = [at(R_dn + i * TOK, TOK, rows=NH) for i in range(6)]
        M = at(R_dn, NH, SEQ)
        BC = at(R_dn + 2048, 4, 512)
        dt = at(R_dt, TOK, rows=NH)
        acs = at(R_dt + TOK, TOK, rows=NH)
        xtok = at(R_g, NC_, 512)
        Btok = at(R_act, NC_, P)
        seg = at(R_row, 2, SEQ)
        Gm = at(R_row + 1024, 2, SEQ)
        hs = at(R_samp, 4, NS * NST)
        stmp = at(R_samp + 2048, 2, NS * NST)
        win = [at(R_row + i * 528, 528) for i in range(2)]
        pp = at(R_xbc, NT, D)
        w_pp = at(R_g, 2, D)
        pT = at(R_aT + KT * D, 2, TOK)
        prow = at(R_dn + DN, NT, PLE)
        w_ple = at(R_aT, KT, D)
        bfin = at(R_samp + 1024, D)
        bple = at(R_samp + 2048, D)
        uTr = at(R_tb, 2, KT * P)
        uT = at(R_tb, 2, KT * S)
        G = at(R_g, 2, D, rows=S)
        sg = mem[S:2 * S, R_act:R_act + 2 * FF].rearrange("p (a b) -> p a b", b=FF)
        act_tok = mem[S:2 * S, R_g:R_g + 2 * FF].rearrange("p (a b) -> p a b", b=FF)
        actT = at(R_aT + KT * D, 2, 2 * S)
        ysb = at(R_row, 2, D, rows=S)
        Yg = at(R_gu, 2 * NT, D)
        yout = at(R_gu + 2 * NT * D, NT, D)
        sm = [R_small]

        def small(*shape, rows=P):
            r = at(sm[0], *shape, rows=rows)
            n = 1
            for s in shape:
                n *= s
            sm[0] += n
            assert sm[0] <= R_small + 1104
            return r

        vec = small(NV)
        ss = small(24)
        rms_ = small(24)
        rstd = small(24)
        acsT = small(NC_, NH)
        RL = small(NC_, NH)
        te = small(NC_, NH)
        cd = small(NC_, NH)
        xcs = small(XT, NS, TAPS)
        cprod = stmp[:, 0, 0:XT * NS * TAPS].rearrange("p (m b k) -> p m b k", b=NS, k=TAPS)
        vs = v[:, :, BUF + SEQ:BUF + TOK]
        vsum = small(NG, NS)
        cst = small(XT, 11)
        vst = small(NG, 23)
        dx = small(4, NS + 1)
        ys = small(4, NS)
        h9 = small(NS + 1, rows=NH)
        hv = small(4, rows=NH)
        rbias = small(36)
        w_rt = small(KT, 36)
        idle = small(8)
        wgt = small(NT, 2)
        ro = [R_samp]

        def rout(*shape, base=ro):
            r = at(base[0], *shape)
            n = 1
            for s in shape:
                n *= s
            base[0] += n
            return r

        L = rout(NT, 36)
        Lg = rout(NT, 8)
        gmax = rout(NT, 8)
        gidx = rout(NT, 8).bitcast(U32)
        m4 = rout(NT, 4)
        ex4 = rout(NT, 4)
        es = rout(NT, 8)
        ev = rout(NT, 8)
        eidx = rout(NT, 8).bitcast(U32)
        gf = rout(NT)
        gw = rout(NT)
        eid = rout(NT, 2)
        e21 = rout(NT)
        rk = rout(NT, 2)
        rq = rout(NT, 2)
        rr = rout(NT, 2)
        ovt = rout(NT, 2)
        cmp0 = rout(NT, 2)
        ohs = rout(NT * 16).bitcast(BF16)
        bef = rout(P // 2).bitcast(BF16)
        oneb = rout(P // 2).bitcast(BF16)
        ovn = rout(NE)
        ove = rout(NE)
        ovb = rout(NE)
        assert ro[0] <= R_samp + 1024
        ro2 = [R_dt]
        oh = rout(NT, 2 * NE, base=ro2)
        tmp = rout(NT, 2 * NE, base=ro2)
        assert ro2[0] <= R_dt + 2 * TOK
        vecrow = ctx.enter_context(nc.sbuf_tensor("vecrow", [NV, P], F32))
        slot_i = ctx.enter_context(nc.sbuf_tensor("slot_i", [P, NT, 2], I32))
        int_w = ctx.enter_context(nc.sbuf_tensor("int_w", [P, NE], I32))
        tok_i = ctx.enter_context(nc.sbuf_tensor("tok_i", [P, NT, 2], I32))
        out_all = ctx.enter_context(nc.sbuf_tensor("out_all", [S, NBT], I32))
        idx_all = ctx.enter_context(nc.sbuf_tensor("idx_all", [S, NBT], I32))
        out_i = [ctx.enter_context(nc.sbuf_tensor(f"out_i{q}", [S, 1], I32)) for q in range(2)]
        idx_i = [ctx.enter_context(nc.sbuf_tensor(f"idx_i{q}", [S, 1], I32)) for q in range(2)]
        btab = ctx.enter_context(nc.sbuf_tensor("btab", [1, NB + 8], I32))
        nloop = ctx.enter_context(nc.sbuf_tensor("nloop", [1, 2], I32))
        PS = [ctx.enter_context(nc.psum_tensor(f"PS{i}", [P, 512], F32)) for i in range(8)]

        u_dram = nc.dram_tensor("u_rows", (TOK, D), F32).ap()
        slots_dram = nc.dram_tensor("slot_tokens", (NBT * S, 1), I32).ap()
        y_dram = nc.dram_tensor("choice_rows", (2 * TOK, D), F32).ap()

        COLS = [("v", m, m * P, P) for m in range(NG)]
        COLS += [("xbc", m, 2 * PW + m * P, P) for m in range(XT)] + [("dt", 0, IN_DIM - NH, NH)]
        COLS += [("z", m, PW + m * P, P) for m in range(4)]
        J_XBC, J_DT, J_Z = NG, NG + XT, NG + XT + 1

        ld_bias = sem("ld_bias")
        ld_const = sem("ld_const")
        ld_head = sem("ld_head")
        ld_hs = sem("ld_hs")
        ld_hv = sem("ld_hv")
        ld_lin = sem("ld_lin")
        ld_p = sem("ld_p")
        ld_rt = sem("ld_rt")
        ld_state_c = sem("ld_state_c")
        ld_state_p = sem("ld_state_p")
        ld_wout = sem("ld_wout")
        ld_wple = sem("ld_wple")
        own_act = sem("own_act")
        own_dve = sem("own_dve")
        own_pool = sem("own_pool")
        s_M_ready = sem("s_M_ready")
        s_R_done = sem("s_R_done")
        s_R_out = sem("s_R_out")
        s_S_done = sem("s_S_done")
        s_S_out = sem("s_S_out")
        s_T_done = sem("s_T_done")
        s_YO_done = sem("s_YO_done")
        s_Y_done = sem("s_Y_done")
        s_Y_out = sem("s_Y_out")
        s_Y_ready = sem("s_Y_ready")
        s_aT_taken = sem("s_aT_taken")
        s_act_ready = sem("s_act_ready")
        s_actT_done = sem("s_actT_done")
        s_actT_ready = sem("s_actT_ready")
        s_cnt_done = sem("s_cnt_done")
        s_cnt_taken = sem("s_cnt_taken")
        s_conv_out = sem("s_conv_out")
        s_conv_pre = sem("s_conv_pre")
        s_convs_pre = sem("s_convs_pre")
        s_cst_T = sem("s_cst_T")
        s_cst_out = sem("s_cst_out")
        s_cst_ready = sem("s_cst_ready")
        s_diag_ready = sem("s_diag_ready")
        s_dt_exp = sem("s_dt_exp")
        s_dt_ln = sem("s_dt_ln")
        s_dt_neg = sem("s_dt_neg")
        s_dt_ready = sem("s_dt_ready")
        s_dt_u = sem("s_dt_u")
        s_dta_ready = sem("s_dta_ready")
        s_eE_done = sem("s_eE_done")
        s_eE_out = sem("s_eE_out")
        s_exp_a = sem("s_exp_a")
        s_f_T = sem("s_f_T")
        s_f_g = sem("s_f_g")
        s_f_gb = sem("s_f_gb")
        s_f_h2 = sem("s_f_h2")
        s_f_h3 = sem("s_f_h3")
        s_f_r2 = sem("s_f_r2")
        s_f_rstd = sem("s_f_rstd")
        s_f_sig = sem("s_f_sig")
        s_f_v = sem("s_f_v")
        s_f_vT = sem("s_f_vT")
        s_f_y = sem("s_f_y")
        s_fin_T = sem("s_fin_T")
        s_fin_out = sem("s_fin_out")
        s_g_init = sem("s_g_init")
        s_gated = sem("s_gated")
        s_gn_done = sem("s_gn_done")
        s_gn_ln = sem("s_gn_ln")
        s_gn_out = sem("s_gn_out")
        s_h9_ready = sem("s_h9_ready")
        s_idle = sem("s_idle")
        s_idx = sem("s_idx")
        s_inproj_done = sem("s_inproj_done")
        s_inproj_out = sem("s_inproj_out")
        s_lg_done = sem("s_lg_done")
        s_lg_out = sem("s_lg_out")
        s_m_ready = sem("s_m_ready")
        s_mixP_ready = sem("s_mixP_ready")
        s_mix_ready = sem("s_mix_ready")
        s_oh_ready = sem("s_oh_ready")
        s_outp_done = sem("s_outp_done")
        s_outp_out = sem("s_outp_out")
        s_pT_done = sem("s_pT_done")
        s_pT_out = sem("s_pT_out")
        s_pads = sem("s_pads")
        s_pool_done = sem("s_pool_done")
        s_pp_done = sem("s_pp_done")
        s_pp_out = sem("s_pp_out")
        s_r_rstd = sem("s_r_rstd")
        s_rstd_x = sem("s_rstd_x")
        s_rt_a = sem("s_rt_a")
        s_rt_b = sem("s_rt_b")
        s_rt_ready = sem("s_rt_ready")
        s_samp_done = sem("s_samp_done")
        s_scan1_done = sem("s_scan1_done")
        s_scan1_out = sem("s_scan1_out")
        s_seg_exp = sem("s_seg_exp")
        s_sg_ready = sem("s_sg_ready")
        s_sq_out = sem("s_sq_out")
        s_states_T = sem("s_states_T")
        s_states_in = sem("s_states_in")
        s_te_in = sem("s_te_in")
        s_te_ready = sem("s_te_ready")
        s_uT_ready = sem("s_uT_ready")
        s_uTr_done = sem("s_uTr_done")
        s_uTr_out = sem("s_uTr_out")
        s_u_ready = sem("s_u_ready")
        s_up_done = sem("s_up_done")
        s_vec_T = sem("s_vec_T")
        s_vst_ready = sem("s_vst_ready")
        s_xT_done = sem("s_xT_done")
        s_xdtE_ready = sem("s_xdtE_ready")
        s_xn_ready = sem("s_xn_ready")
        s_ysb_free = sem("s_ysb_free")
        slots_filled = sem("slots_filled")
        st_conv = sem("st_conv")
        st_fin = sem("st_fin")
        st_hs = sem("st_hs")
        st_out = sem("st_out")
        st_pool = sem("st_pool")
        st_shift = sem("st_shift")
        st_slots = sem("st_slots")
        ld_vec = [sem(f"ld_vec{i}") for i in range(2)]
        ld_x = [sem(f"ld_x{i}") for i in range(NT)]
        ld_w = [sem(f"ld_w{i}") for i in range(3)]
        w_full = [sem(f"w_full{i}") for i in range(U)]
        d_full = [sem(f"d_full{i}") for i in range(2)]
        idx_full = sem("idx_full")
        g_full = [sem(f"g_full{i}") for i in range(2)]
        y_written = [sem(f"y_written{i}") for i in range(2)]
        u_stored = [sem(f"u_stored{i}") for i in range(2)]
        yg_full = [sem(f"yg_full{i}") for i in range(NT)]
        block = ctx.enter_context(nc.Block())

        def load_vectors(eng, first, end):
            signal = ld_vec[0 if first == 0 else 1]
            for name, lo, hi in [("norm_mix", V_MIX, V_PB), ("conv_w", V_CW, V_CB), ("conv_b", V_CB, V_SN),
                                 ("pool_lin_b", V_PB, V_PS), ("pool_scale", V_PS, V_CW), ("ssd_norm", V_SN, V_FFN),
                                 ("norm_ffn", V_FFN, V_PLE), ("norm_ple", V_PLE, NV)][first:end]:
                src = a[name]
                if name == "conv_w":
                    src = src.rearrange("a k (m p) -> (a k m) p", p=P)
                elif name == "pool_lin_b":
                    src = src.rearrange("a g p -> (a g) p")
                else:
                    src = src.rearrange("a (m p) -> (a m) p", p=P)
                eng.dma_start(vecrow[lo:hi, :], src).then_inc(signal, 16)

        @block.sync
        def _(sp):
            sp.dma_start(const, a["consts"]).then_inc(ld_const, 16)
            for t in range(NT):
                src = a["x_prompt"][0, t * P:(t + 1) * P, :] if t < 4 else a["x_sample"][:, 0, :]
                sp.dma_start(h1[0:ROWS[t], t, :], src).then_inc(ld_x[t], 16)
            w = a["w_in"][0].rearrange("(k p) n -> p k n", p=P)
            for i, (lo, hi) in enumerate([(0, PW), (2 * PW, IN_DIM), (PW, 2 * PW)]):
                sp.dma_start(w_in[:, :, lo:hi], w[:, :, lo:hi]).then_inc(ld_w[i], 16)
            for t in range(4):
                sp.dma_start(hs[:, t].rearrange("p (b n) -> p b n", n=NST),
                             a["state_ssm"][0, :, 2 * t:2 * t + 2].rearrange("b h p n -> (h p) b n")
                             ).then_inc(ld_hs, 16)
            sp.dma_start(o["pool_s"][0, :, 0:BUF - 1, :], a["state_pool"][0, :, 1:BUF, :]).then_inc(st_shift, 16)
            sp.dma_start(o["conv_s"][0, :, 0:2, :], a["state_conv"][0, :, 1:3, :]).then_inc(st_shift, 16)
            sp.wait_ge(s_cst_out, 1)
            sp.dma_start(o["conv_p"][0, 0], stage_c[0:3, :]).then_inc(st_conv, 16)
            sp.dma_start(o["conv_s"][0, :, 2, :], stage_c[3:11, :]).then_inc(st_conv, 16)
            sp.dma_start(o["pool_p"][0, 0], stage_v[0:BUF, :]).then_inc(st_pool, 16)
            sp.dma_start(o["pool_s"][0, :, BUF - 1, :], stage_v[BUF:23, :]).then_inc(st_pool, 16)
            sp.wait_ge(s_inproj_done, len(COLS))
            sp.wait_ge(st_conv, 32)
            sp.dma_start(w_out, a["w_out"][0].rearrange("(k p) n -> p k n", p=P)).then_inc(ld_wout, 16)
            sp.wait_ge(s_samp_done, 1)
            for t in range(4):
                sp.dma_start(o["ssm_s"][0, :, 2 * t:2 * t + 2].rearrange("b h p n -> (h p) b n"),
                             hs[:, t].rearrange("p (b n) -> p b n", n=NST)).then_inc(st_hs, 16)
            sp.wait_ge(s_fin_out, 1)
            sp.dma_start(o["ssm_p"][0, 0].rearrange("(t h) p n -> (h p) t n", h=2), fin).then_inc(st_fin, 16)
            sp.wait_ge(s_Y_done, 4)
            sp.dma_start(w_pp, a["ple_proj_w"][0].rearrange("(k p) n -> p k n", p=P)).then_inc(ld_p, 16)
            sp.dma_start(prow[:, 0:4, :], a["p_prompt"][0, 0].rearrange("(t p) n -> p t n", p=P)).then_inc(ld_p, 16)
            sp.dma_start(prow[0:NS, 4, :], a["p_sample"][0, :, 0, :]).then_inc(ld_p, 16)

            def load_gate_up(slot, src_e):
                sp.dma_start(gu[slot][:, 0:KT, :], a["exp_w_gate"][src_e].rearrange("a (k p) f -> p (a k) f", p=P)
                             ).then_inc(w_full[slot], 16)
                sp.dma_start(gu[slot][:, KT:2 * KT, :], a["exp_w_up"][src_e].rearrange("a (k p) f -> p (a k) f", p=P)
                             ).then_inc(w_full[slot], 16)

            def load_down(slot, src_e):
                sp.dma_start(dn[slot], a["exp_w_down"][src_e].rearrange("a (k p) n -> p (a k) n", p=P)
                             ).then_inc(d_full[slot], 16)

            sp.wait_ge(st_fin, 16)
            sp.wait_ge(s_mix_ready, 4)
            for b in range(2):
                load_gate_up(b, bass.ds(b, 1))
            load_down(0, bass.ds(0, 1))
            for t in range(NT):
                sp.wait_ge(s_u_ready, t + 1)
                rows = ROWS[t]
                sp.dma_start(u_dram[t * P:t * P + rows, :], row[0:rows, t % 2, :]).then_inc(u_stored[t % 2], 16)
            sp.wait_ge(st_hs, 64)
            sp.dma_start(bfin, a["norm_final"].unsqueeze(0).to_broadcast((P, D))).then_inc(ld_bias, 16)
            sp.dma_start(bple, a["ple_gate_b"].to_broadcast((P, D))).then_inc(ld_bias, 16)
            sp.wait_ge(s_outp_done, NT)
            for b in range(2, U):
                load_gate_up(b, bass.ds(b, 1))
            sp.dma_start(w_ple, a["ple_gate_w"][0].rearrange("(k p) n -> p k n", p=P)).then_inc(ld_wple, 16)
            sp.wait_ge(s_pT_done, NT)
            load_down(1, bass.ds(1, 1))
            sp.wait_ge(s_rt_ready, 1)
            m = sp.value_load(nloop[0:1, 1:2], min_val=NE // U - 1, max_val=NB // U - 1)
            with sp.Fori(0, m) as i:
                for s in range(U):
                    e = sp.value_load(btab[0:1, bass.ds(i * U + (U + s), 1)], min_val=0, max_val=NE - 1)
                    sp.wait_ge(s_up_done, i * U + (s + 1))
                    load_gate_up(s, bass.ds(e, 1))
                    e = sp.value_load(btab[0:1, bass.ds(i * U + (s + 2), 1)], min_val=0, max_val=NE - 1)
                    sp.wait_ge(s_Y_ready, i * U + (s + 1))
                    load_down(s % 2, bass.ds(e, 1))
            for s in range(2):
                e = sp.value_load(btab[0:1, bass.ds(m * U + (s + 2), 1)], min_val=0, max_val=NE - 1)
                sp.wait_ge(s_Y_ready, m * U + (s + 1))
                load_down(s % 2, bass.ds(e, 1))
            sp.wait_ge(y_written[0], m * 32 + 48)
            sp.wait_ge(y_written[1], m * 32 + 48)
            for t in range(NT):
                sp.dma_start(Yg[0:ROWS[t], 2 * t:2 * t + 2, :],
                             y_dram[2 * t * P:2 * (t * P + ROWS[t]), :].rearrange("(p k) n -> p k n", k=2)
                             ).then_inc(yg_full[t], 16)
            for t in range(NT):
                rows = ROWS[t]
                sp.wait_ge(s_f_y, t + 1)
                dst = o["y_p"][0, t * P:(t + 1) * P, :] if t < 4 else o["y_s"][:, 0, :]
                sp.dma_start(dst, yout[0:rows, t, :]).then_inc(st_out, 16)
            sp.wait_ge(st_out, 16 * NT)
            sp.wait_ge(st_shift, 32)
            sp.wait_ge(st_pool, 32)
            sp.wait_ge(st_hs, 64)
            sp.wait_ge(st_slots, 16)

        @block.tensor
        def _(pe):
            def transpose(dst, src, n):
                return pe.transpose(dst, src, ident[0:n, 0:n])

            pe.wait_ge(ld_const, 16)
            for half in range(2):
                pe.wait_ge(ld_vec[half], 16 * 4)
            transpose(PS[6][:, 0:NV], vecrow[:, :], NV).then_inc(s_vec_T, 1)
            for j in range(2 * NT):
                t, half = j // 2, j % 2
                R = ROWS[t]
                pe.wait_ge(s_xn_ready, t + 1)
                if j >= 2:
                    pe.wait_ge(s_aT_taken, j - 1)
                for q in range(4):
                    k = 4 * half + q
                    ins = transpose(PS[4 + j % 2][:, q * P:q * P + R], row[0:R, t % 2, k * P:(k + 1) * P], R)
                ins.then_inc(s_xT_done, 1)

            pe.wait_ge(ld_state_c, 16)
            pe.wait_ge(ld_state_p, 16)
            for m in range(XT):
                transpose(PS[7][:, m * 24:(m + 1) * 24], sconv[:, m * P:(m + 1) * P], 24)
            for g in range(NG):
                ins = pe.matmul(PS[7][:, 256 + g * NS:256 + (g + 1) * NS], spool[:, g * P:(g + 1) * P],
                                const[0:NS * BUF, C_POOLSEL + 8 * g:C_POOLSEL + 8 * g + 8], start=True, stop=True)
            ins.then_inc(s_states_T, 1)
            def inproj(j):
                kind, m, col, n = COLS[j]
                pe.wait_ge(ld_w[0 if j < J_XBC else 1 if j < J_Z else 2], 16)
                if j >= 2:
                    pe.wait_ge(s_inproj_out, j - 1)
                for k in range(KT):
                    for h in range(2):
                        ins = pe.matmul(PS[2 * (j % 2) + h][0:n, 0:HALF], w_in[:, k, col:col + n],
                                        aT[:, k, h * HALF:(h + 1) * HALF], start=(k == 0), stop=(k == KT - 1))
                ins.then_inc(s_inproj_done, 1)

            pe.wait_ge(s_aT_taken, 2 * NT)
            for j in range(J_Z + 1):
                inproj(j)
            pe.wait_ge(s_cst_ready, 1)
            for m in range(XT):
                transpose(PS[4 + m // 4][0:11, (m % 4) * P:(m % 4 + 1) * P], cst[:, m, :], P)
            pe.wait_ge(s_vst_ready, 1)
            for g in range(NG):
                ins = transpose(PS[6][0:23, g * P:(g + 1) * P], vst[:, g, :], P)
            ins.then_inc(s_cst_T, 1)
            inproj(J_Z + 1)
            pe.wait_ge(ld_lin, 16)
            pe.wait_ge(s_cst_out, 1)
            for g in range(NG):
                pe.wait_ge(s_m_ready, g + 1)
                if g >= 2:
                    pe.wait_ge(s_mixP_ready, g - 1)
                for h in range(2):
                    ins = pe.matmul(PS[4 + 2 * (g % 2) + h][:, 0:HALF], w_lin[:, g, :],
                                    v[:, g, BUF + h * HALF:BUF + (h + 1) * HALF], start=True, stop=True)
                ins.then_inc(s_pool_done, 1)
            pe.wait_ge(s_dt_ready, 1)
            pe.wait_ge(ld_head, 16)
            for t in range(4):
                if t < 2:
                    pe.wait_ge(s_mixP_ready, t + 3)
                if t >= 2:
                    pe.wait_ge(s_scan1_out, t - 1)
                for h in range(2):
                    ins = pe.matmul(PS[4 + 2 * (t % 2) + h][:, 0:HALF], headc[:, H_EXP + t * P:H_EXP + (t + 1) * P],
                                    dt[:, h * HALF:(h + 1) * HALF], start=True, stop=True)
                ins.then_inc(s_scan1_done, 1)
            pe.wait_ge(s_scan1_out, 3)
            for c in range(NC_):
                ins = transpose(PS[4][:, c * NH:(c + 1) * NH], acs[:, c * P:(c + 1) * P], NH)
            ins.then_inc(s_scan1_done, 1)
            for c in range(NC_):
                ins = transpose(PS[5][:, c * P:(c + 1) * P], xc[:, 4, c * P:(c + 1) * P], P)
            ins.then_inc(s_scan1_done, 1)
            pe.wait_ge(s_scan1_out, 4)
            for g in range(2):
                rows = slice(64 * g, 64 * g + 64)
                for c in range(NC_):
                    cc = slice(c * P, (c + 1) * P)
                    ins = pe.matmul(PS[6 + g][:, cc], xc[rows, 4, cc], xc[rows, 5, cc], start=True, stop=True)
                ins.then_inc(s_scan1_done, 1)
            for c in range(NC_):
                pe.wait_ge(s_scan1_out, 5 + c)
                for t in range(4):
                    ins = transpose(PS[4 + c][:, t * P:(t + 1) * P], xdtT[:, t, c * P:(c + 1) * P], P)
                ins.then_inc(s_scan1_done, 1)
            pe.wait_ge(s_h9_ready, 1)
            pe.wait_ge(s_scan1_out, 9)
            for t in range(4):
                ins = pe.matmul(PS[4][:, t * (NS + 1):(t + 1) * (NS + 1)], headc[:, H_EXP + t * P:H_EXP + (t + 1) * P],
                                h9[:, :], start=True, stop=True)
            ins.then_inc(s_scan1_done, 1)
            for q in range(4):
                kind, g = q // 2, q % 2
                rows = slice(64 * g, 64 * g + 64)
                pe.wait_ge(s_diag_ready, kind + 1)
                pe.wait_ge(s_scan1_out, 14 if q == 3 else 10 + q)
                ins = pe.matmul(PS[5 + q % 3][:, :], ones[rows, :], stmp[rows, kind, :], start=True, stop=True)
                ins.then_inc(s_scan1_done, 1)

            def head_row(h):
                pe.wait_ge(s_scan1_out, 17)
                if h >= 4:
                    pe.wait_ge(s_R_out, h - 3)
                pe.matmul(PS[4 + h % 4][:, :], headc[:, H_ROW + h * P:H_ROW + (h + 1) * P], acs[:, 0:SEQ],
                          start=True, stop=True).then_inc(s_R_done, 1)

            for q in range(2):
                inproj(J_Z + 2 + q)
                for h in range(4):
                    head_row(4 * q + h)
            for t in range(4):
                pe.wait_ge(s_R_out, 5 + t)
                pe.matmul(PS[4 + t][:, :], headc[:, H_EXP + t * P:H_EXP + (t + 1) * P], acs[:, 0:SEQ],
                          start=True, stop=True).then_inc(s_eE_done, 1)
            def mix_col(k, t):
                R = ROWS[t]
                return v[:, k, BUF + t * P:BUF + t * P + R] if k < NG else mixT[:, k, t * P:t * P + R]

            def outproj_part(t, k0, k1):
                for h in range(2):
                    for k in range(k0, k1):
                        ins = pe.matmul(PS[(4 + 2 * t) % 8 + h][:, :], mix_col(k, t), w_out[:, k, h * 512:(h + 1) * 512],
                                        start=(k == 0), stop=(k == KT - 1))
                return ins

            def sample_product(bank, col, w):
                for k in range(KT):
                    for q in range(4):
                        ins = pe.matmul(bank[32 * q:32 * q + NS, 0:D // 4], col(k, 4), w[:, k, q * (D // 4):(q + 1) * (D // 4)],
                                        start=(k == 0), stop=(k == KT - 1))
                return ins

            for c in range(NC_):
                pe.wait_ge(s_xdtE_ready, c + 1)
                pe.wait_ge(s_eE_out, c + 1)
                pe.matmul(PS[4 + c][:, :], Btok[:, c, :], xdtE[:, c, :], start=True, stop=True).then_inc(s_S_done, 1)
            pe.wait_ge(s_inproj_out, len(COLS))
            for h in range(NH):
                pe.wait_ge(s_M_ready, h + 1)
                for c in range(NC_):
                    ins = pe.matmul(PS[h // 2][64 * (h % 2):64 * (h % 2) + 64, c * P:(c + 1) * P],
                                    xtok[:, c, h * HD:(h + 1) * HD], M[:, h, c * P:(c + 1) * P],
                                    start=True, stop=True)
                if h % 2:
                    ins.then_inc(s_Y_done, 1)
            for t in range(4):
                rows = slice(64 * (t // 2), 64 * (t // 2) + 64)
                pe.wait_ge(s_S_out, 4)
                for c in range(1, NC_):
                    ins = pe.matmul(PS[4 + t][:, c * P:(c + 1) * P], H[rows, c - 1, t * P:(t + 1) * P],
                                    xc[rows, 5, c * P:(c + 1) * P], start=True, stop=True)
                ins.then_inc(s_YO_done, 1)
            for t in range(4):
                g = t // 2
                rows = slice(64 * g, 64 * g + 64)
                if t == 0 or t == 2:
                    pe.wait_ge(s_Y_out, t + 1)
                ins = pe.transpose(PS[4 + 2 * g][:, (t % 2) * NST:(t % 2 + 1) * NST], H[rows, NC_ - 1, t * P:(t + 1) * P],
                                   ident[rows, 64 * g:64 * g + 64])
            ins.then_inc(s_fin_T, 1)
            pe.wait_ge(ld_wout, 16)
            pe.wait_ge(s_fin_out, 1)
            for t in range(2):
                pe.wait_ge(s_Y_out, 2 * t + 2)
                outproj_part(t, 0, 4)
            for g in range(2):
                pe.wait_ge(s_sq_out, 2 * g + 2)
                for h in range(2):
                    for q in range(2):
                        ins = pe.matmul(PS[2 * g + h][:, 0:HALF], ones, zs[:, 2 * g + q, h * HALF:(h + 1) * HALF],
                                        start=(q == 0), stop=(q == 1))
                ins.then_inc(s_gn_done, 1)

            def outproj(t):
                if t == 0:
                    pe.wait_ge(s_mix_ready, 4)
                if t == 4:
                    pe.wait_ge(s_outp_out, 3)
                if t < 4:
                    ins = outproj_part(t, 4 if t < 2 else 0, KT)
                else:
                    ins = sample_product(PS[0], mix_col, w_out)
                ins.then_inc(s_outp_done, 1)

            def u_rows(t):
                R = ROWS[t]
                pe.wait_ge(s_u_ready, t + 1)
                for half in range(2):
                    j = 2 * t + half
                    if t >= 1:
                        pe.wait_ge(s_uTr_out, j - 1)
                    for q in range(4):
                        k = 4 * half + q
                        ins = transpose(PS[4 + half][:, q * P:q * P + R], row[0:R, t % 2, k * P:(k + 1) * P], R)
                    ins.then_inc(s_uTr_done, 1)

            def route(t):
                R = ROWS[t]
                if t == 0:
                    pe.wait_ge(s_outp_out, 2)
                pe.wait_ge(s_uTr_out, 2 * t + 2)
                pe.wait_ge(ld_rt, 64)
                for k in range(KT):
                    ins = pe.matmul(PS[6][0:R, t * 36:(t + 1) * 36], uTr[:, t % 2, k * P:k * P + R],
                                    w_rt[:, k, :], start=(k == 0), stop=(k == KT - 1))
                ins.then_inc(s_lg_done, 1)

            outproj(0)
            outproj(1)
            u_rows(0)
            outproj(2)
            route(0)
            u_rows(1)
            outproj(3)
            route(1)
            u_rows(2)
            outproj(4)
            route(2)
            u_rows(3)
            pe.wait_ge(ld_p, 48)
            pe.wait_ge(s_outp_out, 2)
            for t in range(NT):
                R = ROWS[t]
                if t >= 1:
                    pe.wait_ge(s_pT_out, t)
                for q in range(2):
                    ins = transpose(PS[7][:, q * P:q * P + R], prow[0:R, t, q * P:(q + 1) * P], R)
                ins.then_inc(s_pT_done, 1)
                if t == 1:
                    route(3)
                    u_rows(4)
            route(4)

            def pleproj(t):
                R = ROWS[t]
                for h in range(2):
                    j = 2 * t + h
                    if j == 0:
                        pe.wait_ge(s_pT_out, NT)
                        pe.wait_ge(s_outp_out, NT)
                    if j >= 4:
                        pe.wait_ge(s_pp_out, j - 3)
                    for q in range(2):
                        ins = pe.matmul(PS[j % 4][0:R, :], pT[:, q, t * P:t * P + R], w_pp[:, q, h * 512:(h + 1) * 512],
                                        start=(q == 0), stop=(q == 1))
                    ins.then_inc(s_pp_done, 1)

            pleproj(0)
            pe.wait_ge(s_oh_ready, 1)
            for t in range(NT + 1):
                for t2 in range(min(t + 1, NT)):
                    last = t2 == min(t, NT - 1)
                    ins = pe.matmul(PS[7][:, t * NE:(t + 1) * NE], bef if t2 == t else oneb, ohs[:, t2 * NE:(t2 + 1) * NE],
                                    start=(t2 == 0), stop=last)
            ins.then_inc(s_cnt_done, 1)
            for t in range(1, NT):
                pleproj(t)

            pe.wait_ge(s_rt_ready, 1)
            n = pe.value_load(nloop[0:1, 0:1], min_val=NE // U, max_val=NB // U)
            pe.wait_ge(s_cnt_taken, 1)
            pe.wait_ge(s_lg_out, NT)
            pe.wait_ge(g_full[0], 16)

            def block_rows(b2):
                for k in range(KT):
                    ins = transpose(PS[6 + b2][:, k * S:(k + 1) * S], G[:, b2, k * P:(k + 1) * P], S)
                ins.then_inc(s_T_done, 1)

            block_rows(0)
            pe.wait_ge(s_pp_out, 2 * NT)
            with pe.Fori(0, n) as i:
                for s in range(U):
                    pe.wait_ge(s_uT_ready, i * U + (s + 1))
                    pe.wait_ge(w_full[s], i * 32 + 32)
                    for k in range(KT):
                        rows_k = uT[:, s % 2, k * S:(k + 1) * S]
                        pe.matmul(PS[0][0:S, 0:FF], rows_k, gu[s][:, k, :], start=(k == 0), stop=(k == KT - 1))
                        if k == 0:
                            pe.wait_ge(g_full[(s + 1) % 2], i * 32 + 16 * ((s + 1) // 2 + 1))
                        ins = pe.matmul(PS[1][S:2 * S, 0:FF], rows_k, gu[s][:, KT + k, :], start=(k == 0), stop=(k == KT - 1))
                    ins.then_inc(s_up_done, 1)
                    block_rows((s + 1) % 2)
                    pe.wait_ge(s_act_ready, i * U + (s + 1))
                    pe.wait_ge(s_ysb_free, i * U + (s + 1))
                    for f in range(2):
                        ins = pe.matmul(PS[2][:, f * S:(f + 1) * S], act_tok[:, s % 2, f * P:(f + 1) * P], ident[S:2 * S, S:2 * S],
                                        start=True, stop=True)
                    ins.then_inc(s_actT_done, 1)
                    pe.wait_ge(s_actT_ready, i * U + (s + 1))
                    pe.wait_ge(d_full[s % 2], i * 32 + 16 * (s // 2 + 1))
                    for f in range(2):
                        for h in range(2):
                            ins = pe.matmul(PS[4 + h][h * S:(h + 1) * S, :], actT[:, s % 2, f * S:(f + 1) * S],
                                            dn[s % 2][:, f, h * 512:(h + 1) * 512], start=(f == 0), stop=(f == 1))
                    ins.then_inc(s_Y_ready, 1)

            def v_rows(t):
                R = ROWS[t]
                pe.wait_ge(s_f_v, t + 1)
                for half in range(2):
                    if t >= 1:
                        pe.wait_ge(s_f_vT, 2 * t - 1 + half)
                    for q in range(4):
                        k = 4 * half + q
                        ins = transpose(PS[6 + half][:, q * P:q * P + R], row[0:R, t % 2, k * P:(k + 1) * P], R)
                    ins.then_inc(s_f_T, 1)

            def gates(t):
                R = ROWS[t]
                pe.wait_ge(s_f_vT, 2 * t + 2)
                if t == 0:
                    pe.wait_ge(ld_wple, 16)
                if t >= 2:
                    pe.wait_ge(s_f_gb, 2 * t - 2)
                if t == 4:
                    sample_product(PS[0], lambda k, t: uTr[:, t % 2, k * P:k * P + NS], w_ple).then_inc(s_f_g, 2)
                    return
                for h in range(2):
                    for k in range(KT):
                        ins = pe.matmul(PS[2 * (t % 2) + h][0:R, :], uTr[:, t % 2, k * P:k * P + R],
                                        w_ple[:, k, h * 512:(h + 1) * 512], start=(k == 0), stop=(k == KT - 1))
                    ins.then_inc(s_f_g, 1)

            v_rows(0)
            for t in range(NT):
                if t + 1 < NT:
                    v_rows(t + 1)
                gates(t)

        @block.scalar
        def _(act):
            step = Steps(act, own_act)
            A = act.activation
            load_vectors(act, 0, 4)
            def rms(t, src, j, squares, ready):
                R = ROWS[t]
                step(A(squares[0:R, :], src, ACT.Square, accum_out=ss[0:R, j:j + 1]))
                A(rms_[0:R, j:j + 1], ss[0:R, j:j + 1], ACT.Sqrt, bias=eps[0:R, :], scale=1.0 / D).then_inc(ready, 1)

            act.wait_ge(ld_const, 16)
            for t in range(NT):
                act.wait_ge(ld_x[t], 16)
                rms(t, h1[0:ROWS[t], t, :], t, junk, s_rstd_x)
            act.dma_start(headc, a["heads"]).then_inc(ld_head, 16)
            act.dma_start(hv[:, 0:1], a["dt_bias"].rearrange("a h -> h a")).then_inc(ld_hv, 16)
            act.dma_start(hv[:, 1:2], a["a_log"].rearrange("a h -> h a")).then_inc(ld_hv, 16)
            act.dma_start(h9[:, NS:NS + 1], a["d_skip"].rearrange("a h -> h a")).then_inc(ld_hv, 16)
            act.dma_start(w_lin, a["pool_lin_w"][0].rearrange("g c d -> c g d")).then_inc(ld_lin, 16)
            act.dma_start(w_rt[:, :, 0:4], a["router_grp_w"][0].rearrange("(k p) n -> p k n", p=P)).then_inc(ld_rt, 16)
            act.dma_start(w_rt[:, :, 4:36], a["router_exp_w"][0].rearrange("(k p) n -> p k n", p=P)).then_inc(ld_rt, 16)
            act.dma_start(rbias[:, 0:4], a["router_grp_b"].to_broadcast((P, 4))).then_inc(ld_rt, 16)
            act.dma_start(rbias[:, 4:36], a["router_exp_b"].to_broadcast((P, NE))).then_inc(ld_rt, 16)
            act.wait_ge(s_states_T, 1)
            A(xcs[:, :, :, 0:3], PS[7][:, 0:144].rearrange("p (m b k) -> p m b k", b=NS, k=3), ACT.Copy)
            A(vsum, PS[7][:, 256:256 + NG * NS].rearrange("p (g b) -> p g b", b=NS), ACT.Copy).then_inc(s_states_in, 1)

            def out(j):
                kind, m, _, n = COLS[j]
                a0, b0 = PS[2 * (j % 2)], PS[2 * (j % 2) + 1]
                cut = SEQ - HALF
                act.wait_ge(s_inproj_done, j + 1)
                if kind == "xbc":
                    A(xbc[:, m, 3:3 + HALF], a0[:, 0:HALF], ACT.Copy)
                    A(xbc[:, m, 3 + HALF:3 + SEQ], b0[:, 0:cut], ACT.Copy)
                    A(xcs[:, m, :, 3], b0[:, cut:HALF], ACT.Copy).then_inc(s_inproj_out, 1)
                elif kind == "dt":
                    A(dtw[0][:, 0:HALF], a0[0:n, 0:HALF], ACT.Identity, bias=hv[:, 0:1])
                    A(dtw[0][:, HALF:TOK], b0[0:n, 0:HALF], ACT.Identity, bias=hv[:, 0:1]).then_inc(s_inproj_out, 1)
                elif kind == "z":
                    A(zs[:, m, 0:HALF], a0[:, 0:HALF], ACT.Silu)
                    A(zs[:, m, HALF:TOK], b0[:, 0:HALF], ACT.Silu).then_inc(s_inproj_out, 1)
                else:
                    A(v[:, m, BUF:BUF + HALF], a0[:, 0:HALF], ACT.Copy)
                    A(v[:, m, BUF + HALF:BUF + TOK], b0[:, 0:HALF], ACT.Copy).then_inc(s_inproj_out, 1)

            def conv_silu(m):
                act.wait_ge(s_conv_pre, m + 1)
                A(xc[:, m, 0:SEQ], xc[:, m, 0:SEQ], ACT.Silu).then_inc(s_conv_out, 1)

            for m in range(NG):
                out(m)
            for m in range(XT):
                out(J_XBC + m)
                if m >= 1:
                    conv_silu(m - 1)
            act.wait_ge(ld_hv, 48)
            out(J_DT)
            conv_silu(5)
            act.wait_ge(s_convs_pre, 1)
            A(xc[:, :, SEQ:TOK], xc[:, :, SEQ:TOK], ACT.Silu).then_inc(s_conv_out, 1)
            A(hv[:, 2:3], hv[:, 1:2], ACT.Exp).then_inc(s_exp_a, 1)
            act.wait_ge(s_dt_neg, 1)
            A(dtw[2], dtw[1], ACT.Exp).then_inc(s_dt_exp, 1)
            act.wait_ge(s_dt_u, 1)
            A(dtw[4], dtw[3], ACT.Ln).then_inc(s_dt_ln, 1)
            act.wait_ge(s_dta_ready, 1)
            A(h9[:, 0:NS], dtw[5][:, SEQ:TOK], ACT.Exp).then_inc(s_h9_ready, 1)
            out(J_Z)
            act.wait_ge(s_cst_T, 1)
            A(stage_c[0:11, 0:512], PS[4][0:11, :], ACT.Copy)
            A(stage_c[0:11, 512:768], PS[5][0:11, 0:256], ACT.Copy)
            A(stage_v[0:23, :], PS[6][0:23, :], ACT.Copy).then_inc(s_cst_out, 1)
            out(J_Z + 1)

            def seg_exp(h):
                act.wait_ge(s_R_out, h + 1)
                A(seg[:, h % 2, :], seg[:, h % 2, :], ACT.Exp).then_inc(s_seg_exp, 1)

            for q in range(2):
                out(J_Z + 2 + q)
                for h in range(4):
                    seg_exp(4 * q + h)
            act.wait_ge(s_te_in, 1)
            A(te, te, ACT.Exp)
            A(cd, RL, ACT.Exp).then_inc(s_te_ready, 1)
            for t in range(4):
                act.wait_ge(s_eE_done, t + 1)
                A(eE[:, t, :], PS[4 + t][:, :], ACT.Exp).then_inc(s_eE_out, 1)
            act.wait_ge(s_fin_T, 1)
            for g in range(2):
                ins = A(fin[:, 2 * g:2 * g + 2, :], PS[4 + 2 * g][:, 0:2 * NST].rearrange("p (t n) -> p t n", n=NST), ACT.Copy)
            ins.then_inc(s_fin_out, 1)
            for t in range(4):
                act.wait_ge(s_gated, t + 1)
                A(zs[:, t, 0:SEQ], y[:, t, :], ACT.Square)
                A(zs[:, t, SEQ:TOK], ys[:, t, :], ACT.Square).then_inc(s_sq_out, 1)
            for g in range(2):
                act.wait_ge(s_gn_done, g + 1)
                for h in range(2):
                    A(rsg[:, g, h * HALF:(h + 1) * HALF], PS[2 * g + h][:, 0:HALF], ACT.Ln,
                      bias=eps, scale=1.0 / (2 * P)).then_inc(s_gn_ln, 1)
            act.wait_ge(s_gn_ln, 4)
            for g in range(2):
                A(rsg[:, g, :], rsg[:, g, :], ACT.Exp, scale=-0.5).then_inc(s_gn_out, 1)
            for t in range(NT):
                act.wait_ge(s_outp_out, t + 1)
                rms(t, h1[0:ROWS[t], t, :], 5 + t, pp[:, NT - 1, :], s_r_rstd)
            for t in range(NT):
                R = ROWS[t]
                act.wait_ge(s_pT_done, t + 1)
                A(pT[:, :, t * P:t * P + R], PS[7][:, 0:2 * P].rearrange("p (q c) -> p q c", c=P)[:, :, 0:R],
                  ACT.Copy).then_inc(s_pT_out, 1)

            def pp_out(j):
                R = ROWS[j // 2]
                act.wait_ge(s_pp_done, j + 1)
                A(pp[0:R, j // 2, (j % 2) * 512:(j % 2 + 1) * 512], PS[j % 4][0:R, :], ACT.Copy).then_inc(s_pp_out, 1)

            pp_out(0)
            pp_out(1)
            act.wait_ge(s_rt_a, 1)
            step(A(ex4, ex4, ACT.Exp))
            A(e21, e21, ACT.Exp).then_inc(s_rt_b, 1)
            for j in range(2, 2 * NT):
                pp_out(j)
            act.wait_ge(s_rt_ready, 1)
            n = act.value_load(nloop[0:1, 0:1], min_val=NE // U, max_val=NB // U)
            with act.Fori(0, n) as i:
                for s in range(U):
                    act.wait_ge(s_up_done, i * U + (s + 1))
                    A(sg[:, s % 2, :], PS[0][0:S, 0:FF], ACT.Silu).then_inc(s_sg_ready, 1)
                    act.wait_ge(s_Y_ready, i * U + (s + 1))
                    act.wait_ge(y_written[s % 2], i * 32 + 16 * (s // 2 + 1))
                    A(ysb[:, s % 2, 0:512], PS[4][0:S, :], ACT.Copy)
                    A(ysb[:, s % 2, 512:1024], PS[5][S:2 * S, :], ACT.Copy).then_inc(s_ysb_free, 1)
            def norm_h2(t):
                act.wait_ge(s_f_h2, t + 1)
                rms(t, h1[0:ROWS[t], t, :], 10 + t, yout[:, t, :], s_f_rstd)

            def final(t):
                R = ROWS[t]
                act.wait_ge(s_f_gb, 2 * t + 2 if t < 4 else 12)
                A(Yg[0:R, 2 * t, :], Yg[0:R, 2 * t, :], ACT.Sigmoid).then_inc(s_f_sig, 1)
                act.wait_ge(s_f_h3, t + 1)
                rms(t, h1[0:R, t, :], 15 + t, yout[:, t, :], s_f_r2)

            norm_h2(0)
            norm_h2(1)
            for t in range(NT):
                if t + 2 < NT:
                    norm_h2(t + 2)
                final(t)

        @block.gpsimd
        def _(pool):
            step = Steps(pool, own_pool)
            load_vectors(pool, 4, 8)
            pool.dma_start(sconv, a["state_conv"][0].rearrange("b r c -> (b r) c")).then_inc(ld_state_c, 16)
            pool.dma_start(spool, a["state_pool"][0].rearrange("b r c -> (b r) c")).then_inc(ld_state_p, 16)
            step(pool.memset(idle[:, :], 0.0))
            pool.memset(xbc[:, :, 0:TAPS - 1], 0.0)
            pool.memset(v[:, :, 0:BUF], 0.0).then_inc(s_pads, 1)
            step(pool.memset(int_w[:, :], NONE))
            pool.dma_start(slots_dram.rearrange("(p s) a -> p (s a)", s=NBT * S // P), int_w[:, 0:NBT * S // P]
                           ).then_inc(st_slots, 16)
            pool.wait_ge(s_inproj_out, NG)
            pool.tensor_copy(vst[:, :, 0:BUF], v[:, :, SEQ:SEQ + BUF])
            step(pool.tensor_copy(vst[:, :, BUF:23], vs))
            pool.wait_ge(s_states_in, 1)
            for g in range(NG):
                src = v[:, g, :]
                for q in range(g + 1):
                    dst = win[q % 2][:, 0:SEQ + BUF]
                    sh = 1 << q
                    lo = 2 * sh - 1
                    step(pool.tensor_tensor(dst[:, lo:], src[:, lo:SEQ + BUF], src[:, lo - sh:SEQ + BUF - sh], ALU.add))
                    src = dst
                first, rest = src[:, BUF:BUF + 16], src[:, BUF + 16:BUF + SEQ]
                pool.tensor_tensor(first, first, const[:, C_INV + 16 * g:C_INV + 16 * g + 16], ALU.mult)
                pool.tensor_scalar(rest, rest, 1.0 / WINS[g], None, ALU.mult)
                step(pool.tensor_tensor(vsum[:, g, :], vsum[:, g, :], vs[:, g, :], ALU.add))
                step(pool.tensor_scalar(vsum[:, g, :], vsum[:, g, :], 1.0 / WINS[g], None, ALU.mult))
                pool.tensor_tensor(vs[:, g, :], vsum[:, g, :], vs[:, g, :], ALU.subtract)
                step(pool.tensor_tensor(v[:, g, BUF:BUF + SEQ], src[:, BUF:BUF + SEQ], v[:, g, BUF:BUF + SEQ], ALU.subtract))
                if g == 0:
                    pool.tensor_copy(idle[:, 4:5], idle[:, 1:2]).then_inc(s_vst_ready, 1)
                pool.tensor_copy(idle[:, 3:4], idle[:, 2:3]).then_inc(s_m_ready, 1)
                pool.wait_ge(s_m_ready, g + 1)
            pool.wait_ge(s_inproj_out, J_XBC + XT)
            pool.tensor_copy(cst[:, :, 0:3], xbc[:, :, SEQ:SEQ + 3])
            pool.tensor_copy(cst[:, :, 3:11], xcs[:, :, :, 3]).then_inc(s_cst_ready, 1)
            pool.wait_ge(s_scan1_out, 17)
            pool.wait_ge(ld_hs, 64)

            def bn(view):
                return view.rearrange("p (b n) -> p b n", n=NST)

            for t in range(4):
                step(pool.tensor_tensor(bn(hs[:, t]), bn(hs[:, t]), dx[:, t, 0:NS].unsqueeze(2).to_broadcast((P, NS, NST)), ALU.mult))
                step(pool.tensor_tensor(bn(stmp[:, 0]), bn(BC[:, t // 2]), xdtT[:, t, SEQ:TOK].unsqueeze(2).to_broadcast((P, NS, NST)), ALU.mult))
                step(pool.tensor_tensor(hs[:, t], hs[:, t], stmp[:, 0], ALU.add))
                step(pool.tensor_tensor(stmp[:, 1], hs[:, t], BC[:, 2 + t // 2], ALU.mult))
                half = NST // 2
                while half > 1:
                    lo = bn(stmp[:, 1])[:, :, 0:half]
                    step(pool.tensor_tensor(lo, lo, bn(stmp[:, 1])[:, :, half:2 * half], ALU.add))
                    half //= 2
                ins = pool.tensor_tensor(ys[:, t, :], bn(stmp[:, 1])[:, :, 0], bn(stmp[:, 1])[:, :, 1], ALU.add)
                if t < 3:
                    step(ins)
            ins.then_inc(s_samp_done, 1)
            pool.wait_ge(s_rt_ready, 1)
            pool.wait_ge(st_slots, 16)
            for t in range(NT):
                R = ROWS[t]
                for k in range(2):
                    pool.indirect_dma_start(slots_dram, bass.IndirectOffsetOnAxis(ap=slot_i[0:R, t, k:k + 1], axis=0),
                                            tok_i[0:R, t, k:k + 1], None).then_inc(slots_filled, 16)
            pool.wait_ge(slots_filled, 16 * 2 * NT)
            pool.dma_start(out_all[:, :], slots_dram.rearrange("(s b) a -> s (b a)", b=NBT)).then_inc(idx_full, 16)
            n = pool.value_load(nloop[0:1, 0:1], min_val=NE // U, max_val=NB // U)
            pool.wait_ge(u_stored[0], 48)
            pool.wait_ge(u_stored[1], 32)
            pool.wait_ge(s_g_init, 2)
            pool.wait_ge(idx_full, 16)
            for q in range(2):
                pool.dma_start(out_i[q][:, :], slots_dram[q * S:(q + 1) * S, :]).then_inc(y_written[q], 16)

            def idle_step(before):
                pool.wait_ge(s_idle, before)
                pool.tensor_tensor(idle[:, 0:1], idle[:, 1:2], idle[:, 2:3], ALU.add).then_inc(s_idle, 1)

            pool.tensor_tensor(idle[:, 0:1], idle[:, 1:2], idle[:, 2:3], ALU.add).then_inc(s_idle, 1)

            def gather(q):
                pool.indirect_dma_start(G[:, q, :], None, u_dram, bass.IndirectOffsetOnAxis(ap=idx_i[q][:, 0:1], axis=0),
                                        bounds_check=TOK - 1, oob_is_err=False).then_inc(g_full[q], 16)

            for q in range(2):
                pool.tensor_copy(idx_i[q][:, :], idx_all[:, q:q + 1]).then_inc(s_idx, 1)
            pool.wait_ge(s_idx, 2)
            for q in range(2):
                gather(q)
            pool.wait_ge(s_T_done, 1)
            pool.wait_ge(g_full[0], 16)
            pool.tensor_copy(idx_i[0][:, :], idx_all[:, 2:3]).then_inc(s_idx, 1)
            pool.wait_ge(s_idx, 3)
            gather(0)
            with pool.Fori(0, n) as i:
                for s in range(U):
                    q = (s + 1) % 2
                    pool.wait_ge(s_T_done, i * U + (s + 2))
                    pool.wait_ge(g_full[q], i * 32 + 16 * ((s + 1) // 2 + 1))
                    idle_step(i * 6 * U + (6 * s + 1))
                    pool.tensor_copy(idx_i[q][:, :], idx_all[:, bass.ds(i * U + (s + 3), 1)]).then_inc(s_idle, 1)
                    idle_step(i * 6 * U + (6 * s + 3))
                    gather(q)
                    pool.wait_ge(y_written[s % 2], i * 32 + 16 * (s // 2 + 1))
                    pool.wait_ge(s_ysb_free, i * U + (s + 2))
                    idle_step(i * 6 * U + (6 * s + 4))
                    pool.tensor_copy(out_i[s % 2][:, :], out_all[:, bass.ds(i * U + s, 1)]).then_inc(s_idle, 1)
                    idle_step(i * 6 * U + (6 * s + 6))
                    pool.indirect_dma_start(y_dram, bass.IndirectOffsetOnAxis(ap=out_i[s % 2][:, 0:1], axis=0),
                                            ysb[:, s % 2, :], None, bounds_check=2 * TOK - 1, oob_is_err=False
                                            ).then_inc(y_written[s % 2], 16)

        @block.vector
        def _(dve):
            step = Steps(dve, own_dve)
            tt, ts, stt = dve.tensor_tensor, dve.tensor_scalar, dve.scalar_tensor_tensor

            def last(ins, signal, count):
                ins.then_inc(signal, 1)
                dve.wait_ge(signal, count)

            def tiles(bank, n=4):
                return bank.rearrange("p (c l) -> p c l", l=bank.shape[1] // n)

            def gains(col, k, n, m):
                return vec[:, col + k:col + k + n].unsqueeze(2).to_broadcast((P, n, m))

            dve.wait_ge(s_vec_T, 1)
            step(dve.tensor_copy(vec, PS[6][:, 0:NV]))

            def norm_x(t):
                R = ROWS[t]
                dve.wait_ge(s_rstd_x, t + 1)
                step(dve.reciprocal(rstd[0:R, t:t + 1], rms_[0:R, t:t + 1]))
                if t >= 2:
                    dve.wait_ge(s_xT_done, 2 * (t - 1))
                ts(row[0:R, t % 2, :], h1[0:R, t, :], rstd[0:R, t:t + 1], None, ALU.mult).then_inc(s_xn_ready, 1)

            def take_x(j):
                t, half = j // 2, j % 2
                R = ROWS[t]
                dve.wait_ge(s_xT_done, j + 1)
                tt(aT[:, 4 * half:4 * half + 4, t * P:t * P + R], tiles(PS[4 + j % 2][:, :])[:, :, 0:R],
                   gains(V_MIX, 4 * half, 4, R), ALU.mult).then_inc(s_aT_taken, 1)

            norm_x(0)
            norm_x(1)
            for t in range(NT):
                take_x(2 * t)
                take_x(2 * t + 1)
                if t + 2 < NT:
                    norm_x(t + 2)
            dve.wait_ge(s_pads, 1)
            for m in range(XT):
                dve.wait_ge(s_inproj_out, J_XBC + m + 1)
                acc = xc[:, m, 0:SEQ]
                step(ts(acc, xbc[:, m, 0:SEQ], vec[:, V_CW + m:V_CW + m + 1], vec[:, V_CB + m:V_CB + m + 1],
                        ALU.mult, ALU.add))
                for k in range(1, TAPS):
                    col = V_CW + k * XT + m
                    ins = stt(acc, xbc[:, m, k:k + SEQ], vec[:, col:col + 1], acc, ALU.mult, ALU.add)
                    if k < TAPS - 1:
                        step(ins)
                ins.then_inc(s_conv_pre, 1)
            dve.wait_ge(s_states_in, 1)
            taps = vec[:, V_CW:V_CW + TAPS * XT].rearrange("p (k m) -> p m k", m=XT)
            step(tt(cprod, xcs, taps.unsqueeze(2).to_broadcast((P, XT, NS, TAPS)), ALU.mult))
            step(dve.tensor_reduce(xc[:, :, SEQ:TOK], cprod, AX.X, ALU.add))
            tt(xc[:, :, SEQ:TOK], xc[:, :, SEQ:TOK], gains(V_CB, 0, XT, NS), ALU.add).then_inc(s_convs_pre, 1)
            raw, neg, e, u, lnu, dta = dtw
            dve.wait_ge(s_inproj_out, J_DT + 1)
            stt(neg, raw, -1.0, raw, ALU.mult, ALU.min).then_inc(s_dt_neg, 1)
            dve.wait_ge(s_dt_exp, 1)
            last(ts(u, e, 1.0, None, ALU.add), s_dt_u, 1)
            step(stt(neg, u, -1.0, e, ALU.add, ALU.subtract))
            step(dve.reciprocal(dt, u))
            step(tt(neg, neg, dt, ALU.mult))
            dve.wait_ge(s_dt_ln, 1)
            step(stt(raw, raw, 0.0, lnu, ALU.max, ALU.add))
            step(tt(dt, raw, neg, ALU.subtract))
            dve.wait_ge(s_exp_a, 1)
            step(ts(hv[:, 3:4], hv[:, 2:3], -1.0, None, ALU.mult))
            last(ts(dta, dt, hv[:, 3:4], None, ALU.mult), s_dta_ready, 1)
            for c in range(NC_):
                cc = slice(c * P, (c + 1) * P)
                ins = dve.tensor_tensor_scan(acs[:, cc], ones[0:NH, :], dta[:, cc], 0.0, ALU.mult, ALU.add)
            last(ins, s_dt_ready, 1)
            dve.wait_ge(s_conv_out, XT + 1)
            i2 = const[:, C_I2:C_I2 + NST].unsqueeze(1).to_broadcast((P, NS, NST))
            for kind in range(2):
                tt(stmp[:, kind, :].rearrange("p (b n) -> p b n", n=NST),
                   xc[:, 4 + kind, SEQ:TOK].unsqueeze(2).to_broadcast((P, NS, NST)), i2, ALU.mult).then_inc(s_diag_ready, 1)
            for g in range(NG):
                dve.wait_ge(s_pool_done, g + 1)
                for h in range(2):
                    ins = ts(v[:, g, BUF + h * HALF:BUF + (h + 1) * HALF], PS[4 + 2 * (g % 2) + h][:, 0:HALF],
                             vec[:, V_PB + g:V_PB + g + 1], vec[:, V_PS + g:V_PS + g + 1], ALU.add, ALU.mult)
                ins.then_inc(s_mixP_ready, 1)
            dve.wait_ge(s_cst_ready, 1)
            for t in range(4):
                dve.wait_ge(s_scan1_done, t + 1)
                for h in range(2):
                    hh = slice(h * HALF, (h + 1) * HALF)
                    ins = tt(xdtT[:, t, hh], PS[4 + 2 * (t % 2) + h][:, 0:HALF], xc[:, t, hh], ALU.mult)
                ins.then_inc(s_scan1_out, 1)
            dve.wait_ge(s_scan1_done, 5)
            dve.tensor_copy(acsT, PS[4][:, 0:NC_ * NH].rearrange("p (c h) -> p c h", h=NH)).then_inc(s_scan1_out, 1)
            dve.wait_ge(s_scan1_done, 6)
            dve.tensor_copy(Btok, tiles(PS[5][:, :])).then_inc(s_scan1_out, 1)
            causal = const[:, C_CAUSAL:C_CAUSAL + P].unsqueeze(1).to_broadcast((P, NC_, P))
            for g in range(2):
                dve.wait_ge(s_scan1_done, 7 + g)
                tt(tiles(Gm[:, g, :]), tiles(PS[6 + g][:, :]), causal, ALU.mult).then_inc(s_scan1_out, 1)
            dve.wait_ge(st_pool, 32)
            for c in range(NC_):
                dve.wait_ge(s_scan1_done, 9 + c)
                dve.tensor_copy(xtok[:, c, :], PS[4 + c][:, :]).then_inc(s_scan1_out, 1)
            dve.wait_ge(s_scan1_done, 13)
            dve.tensor_copy(dx, PS[4][:, 0:4 * (NS + 1)].rearrange("p (t b) -> p t b", b=NS + 1)).then_inc(s_scan1_out, 1)
            for q in range(4):
                dve.wait_ge(s_scan1_done, 14 + q)
                dve.tensor_copy(BC[:, q, :], PS[5 + q % 3][:, :]).then_inc(s_scan1_out, 1)
            dve.wait_ge(s_scan1_out, 17)

            def head_seg(h):
                dve.wait_ge(s_R_done, h + 1)
                bank = PS[4 + h % 4]
                dve.tensor_copy(RL[:, :, h], tiles(bank[:, :])[:, :, P - 1])
                for c in range(NC_):
                    cc = slice(c * P, (c + 1) * P)
                    ins = ts(seg[:, h % 2, cc], bank[:, cc], acsT[:, c, h:h + 1], 0.0, ALU.subtract, ALU.min)
                ins.then_inc(s_R_out, 1)

            def head_scores(h):
                dve.wait_ge(s_seg_exp, h + 1)
                if h == 4:
                    dve.wait_ge(s_samp_done, 1)
                last(tt(M[:, h, :], seg[:, h % 2, :], Gm[:, h // 4, :], ALU.mult), s_M_ready, h + 1)

            head_seg(0)
            for h in range(NH):
                if h + 1 < NH:
                    head_seg(h + 1)
                head_scores(h)
            dve.wait_ge(s_R_out, NH)
            tt(te, RL, acsT, ALU.subtract).then_inc(s_te_in, 1)
            dve.wait_ge(s_te_ready, 1)
            dve.wait_ge(s_inproj_done, len(COLS))
            for c in range(NC_):
                tt(xdtE[:, c, :].rearrange("p (h q) -> p h q", q=HD), xtok[:, c, :].rearrange("p (h q) -> p h q", q=HD),
                   te[:, c, :].unsqueeze(2).to_broadcast((P, NH, HD)), ALU.mult).then_inc(s_xdtE_ready, 1)
            dve.wait_ge(s_S_done, 1)
            last(dve.tensor_copy(H[:, 0, :], PS[4][:, :]), s_S_out, 1)
            for c in range(1, NC_):
                step(tt(H[:, c, :].rearrange("p (h q) -> p h q", q=HD), H[:, c - 1, :].rearrange("p (h q) -> p h q", q=HD),
                        cd[:, c, :].unsqueeze(2).to_broadcast((P, NH, HD)), ALU.mult))
                dve.wait_ge(s_S_done, c + 1)
                last(tt(H[:, c, :], H[:, c, :], PS[4 + c][:, :], ALU.add), s_S_out, c + 1)
            dve.wait_ge(s_eE_out, 4)
            for t in range(4):
                D_col = dx[:, t, NS:NS + 1]
                dve.wait_ge(s_Y_done, t + 1)
                step(stt(y[:, t, :], xc[:, t, 0:SEQ], D_col, PS[t][:, :], ALU.mult, ALU.add))
                dve.wait_ge(s_YO_done, t + 1)
                last(tt(eE[:, t, P:SEQ], PS[4 + t][:, P:SEQ], eE[:, t, P:SEQ], ALU.mult), s_Y_out, t + 1)
                step(tt(y[:, t, P:SEQ], y[:, t, P:SEQ], eE[:, t, P:SEQ], ALU.add))
                dve.wait_ge(s_samp_done, 1)
                step(stt(ys[:, t, :], xc[:, t, SEQ:TOK], D_col, ys[:, t, :], ALU.mult, ALU.add))
                tt(y[:, t, :], y[:, t, :], zs[:, t, 0:SEQ], ALU.mult)
                last(tt(ys[:, t, :], ys[:, t, :], zs[:, t, SEQ:TOK], ALU.mult), s_gated, t + 1)
            for t in range(4):
                dve.wait_ge(s_gn_out, t // 2 + 1)
                wn = vec[:, V_SN + t:V_SN + t + 1]
                stt(mixT[:, 4 + t, 0:SEQ], y[:, t, :], wn, rsg[:, t // 2, 0:SEQ], ALU.mult, ALU.mult)
                stt(mixT[:, 4 + t, SEQ:TOK], ys[:, t, :], wn, rsg[:, t // 2, SEQ:TOK], ALU.mult, ALU.mult).then_inc(s_mix_ready, 1)

            def residual(t):
                R = ROWS[t]
                dve.wait_ge(s_outp_done, t + 1)
                n, w = (2, 512) if t < 4 else (4, D // 4)
                for h in range(n):
                    hh = slice(h * w, (h + 1) * w)
                    src = PS[(4 + 2 * t) % 8 + h][:, :] if t < 4 else PS[0][32 * h:32 * h + NS, 0:w]
                    ins = tt(h1[0:R, t, hh], src, h1[0:R, t, hh], ALU.add)
                ins.then_inc(s_outp_out, 1)

            def norm_u(t):
                R = ROWS[t]
                dve.wait_ge(s_r_rstd, t + 1)
                step(dve.reciprocal(rstd[0:R, 5 + t:6 + t], rms_[0:R, 5 + t:6 + t]))
                if t >= 2:
                    dve.wait_ge(u_stored[t % 2], 16 * (t // 2))
                    dve.wait_ge(s_uTr_done, 2 * (t - 1))
                ts(row[0:R, t % 2, :], h1[0:R, t, :], rstd[0:R, 5 + t:6 + t], None, ALU.mult).then_inc(s_u_ready, 1)

            def take_rows(bank, t, half, gain_col, signal):
                R = ROWS[t]
                tt(uTr[:, t % 2, :].rearrange("p (k c) -> p k c", c=P)[:, 4 * half:4 * half + 4, 0:R],
                   tiles(bank[:, :])[:, :, 0:R], gains(gain_col, 4 * half, 4, R), ALU.mult).then_inc(signal, 1)

            def take_u(t):
                if t >= 2:
                    dve.wait_ge(s_lg_done, t - 1)
                for half in range(2):
                    dve.wait_ge(s_uTr_done, 2 * t + half + 1)
                    take_rows(PS[4 + half], t, half, V_FFN, s_uTr_out)

            def take_logits(t):
                R = ROWS[t]
                dve.wait_ge(s_lg_done, t + 1)
                last(tt(L[0:R, t, :], PS[6][0:R, t * 36:(t + 1) * 36], rbias[0:R, :], ALU.add), s_lg_out, t + 1)

            residual(0)
            dve.wait_ge(st_hs, 64)
            step(dve.memset(L, 0.0))
            step(dve.memset(Lg, -3.0e38))
            dve.wait_ge(ld_rt, 64)
            norm_u(0)
            residual(1)
            norm_u(1)
            for t in range(NT):
                take_u(t)
                if t + 2 < NT:
                    residual(t + 2)
                    norm_u(t + 2)
                take_logits(t)
            iota = const[:, C_IOTA:C_IOTA + NE]
            step(dve.tensor_copy(Lg[:, :, 0:4], L[:, :, 0:4]))
            for t in range(NT):
                ins = dve.max(gmax[:, t, :], Lg[:, t, :])
            step(ins)
            for t in range(NT):
                ins = dve.max_index(gidx[:, t, :], gmax[:, t, :], Lg[:, t, :])
            step(ins)
            step(dve.tensor_copy(gf, gidx[:, :, 0]))
            tt(ex4, L[:, :, 0:4], gmax[:, :, 0:1].to_broadcast((P, NT, 4)), ALU.subtract)
            step(tt(m4, iota[:, 0:4].unsqueeze(1).to_broadcast((P, NT, 4)), gf.unsqueeze(2).to_broadcast((P, NT, 4)), ALU.is_equal))
            t48 = tmp[:, :, 0:NE].rearrange("p t (g e) -> p t g e", g=4)
            for t in range(NT):
                ins = tt(t48[:, t], L[:, t, 4:36].rearrange("p (g e) -> p g e", g=4),
                         m4[:, t, :].unsqueeze(2).to_broadcast((P, 4, 8)), ALU.mult)
            step(ins)
            step(dve.tensor_reduce(es, t48.rearrange("p t g e -> p t e g"), AX.X, ALU.add))
            for t in range(NT):
                ins = dve.max(ev[:, t, :], es[:, t, :])
            step(ins)
            for t in range(NT):
                ins = dve.max_index(eidx[:, t, :], ev[:, t, :], es[:, t, :])
            step(ins)
            tt(e21, ev[:, :, 1], ev[:, :, 0], ALU.subtract).then_inc(s_rt_a, 1)
            step(dve.tensor_copy(eid, eidx[:, :, 0:2]))
            step(stt(eid, gf.unsqueeze(2).to_broadcast((P, NT, 2)), 8.0, eid, ALU.mult, ALU.add))
            step(tt(eid, eid, const[:, C_BAD:C_BAD + NT].unsqueeze(2).to_broadcast((P, NT, 2)), ALU.add))
            oh4 = oh.rearrange("p t (k e) -> p (t k) e", e=NE)
            tm4 = tmp.rearrange("p t (k e) -> p (t k) e", e=NE)
            eidf = eid.rearrange("p t k -> p (t k)")
            step(tt(oh4, iota.unsqueeze(1).to_broadcast((P, 2 * NT, NE)), eidf.unsqueeze(2).to_broadcast((P, 2 * NT, NE)), ALU.is_equal))
            dve.tensor_copy(bef, const[:, C_BEFORE:C_BEFORE + P])
            dve.tensor_copy(oneb, ones)
            tt(ohs.rearrange("p (t e) -> p t e", e=NE), oh[:, :, 0:NE], oh[:, :, NE:2 * NE], ALU.add).then_inc(s_oh_ready, 1)
            dve.wait_ge(s_rt_b, 1)
            step(dve.tensor_reduce(gw, ex4, AX.X, ALU.add))
            step(stt(gw, e21, 1.0, gw, ALU.add, ALU.mult))
            step(dve.reciprocal(wgt[:, :, 0], gw))
            step(tt(wgt[:, :, 1], wgt[:, :, 0], e21, ALU.mult))
            dve.wait_ge(s_cnt_done, 1)
            dve.wait_ge(st_slots, 16)
            for t in range(NT):
                tt(tmp[:, t, :].rearrange("p (k e) -> p k e", e=NE), oh[:, t, :].rearrange("p (k e) -> p k e", e=NE),
                   PS[7][:, t * NE:(t + 1) * NE].unsqueeze(1).to_broadcast((P, 2, NE)), ALU.mult)
            last(ts(ovn, PS[7][:, NT * NE:(NT + 1) * NE], float(S - 1), None, ALU.add), s_cnt_taken, 1)
            rkf = rk.rearrange("p t k -> p (t k)")
            step(dve.tensor_reduce(rkf, tm4, AX.X, ALU.add))
            step(dve.tensor_copy(int_w[:, :], ovn))
            step(ts(int_w[:, :], int_w[:, :], 6, None, ALU.arith_shift_right))
            step(dve.tensor_copy(ovn, int_w[:, :]))
            step(ts(ovn, ovn, -1.0, 0.0, ALU.add, ALU.max))
            step(dve.tensor_tensor_scan(ove, ones[:, 0:NE], ovn, 0.0, ALU.mult, ALU.add))
            step(tt(ovb, ove, ovn, ALU.subtract))
            step(tt(tm4, oh4, ovb.unsqueeze(1).to_broadcast((P, 2 * NT, NE)), ALU.mult))
            step(dve.tensor_reduce(ovt.rearrange("p t k -> p (t k)"), tm4, AX.X, ALU.add))
            step(dve.tensor_copy(slot_i[:, :, :], rk))
            si = slot_i[:, :, :]
            step(ts(si, si, 6, None, ALU.arith_shift_right))
            step(dve.tensor_copy(rq, si))
            step(stt(rr, rq, -float(S), rk, ALU.mult, ALU.add))
            step(ts(cmp0, rq, 0.5, None, ALU.is_gt))
            step(tt(ovt, ovt, rq, ALU.add))
            step(stt(ovt, ovt, float(NE - 1), eid, ALU.add, ALU.subtract))
            step(tt(ovt, ovt, cmp0, ALU.mult))
            step(tt(ovt, ovt, eid, ALU.add))
            step(stt(cmp0, rr, float(NBT), ovt, ALU.mult, ALU.add))
            step(dve.tensor_copy(si, cmp0))
            for k in range(2):
                ins = ts(rr[:, :, k], const[:, C_TOKID:C_TOKID + NT], 2.0, float(k), ALU.mult, ALU.add)
            step(ins)
            step(dve.tensor_copy(tok_i[:, :, :], rr))
            t16 = tmp[0:1, :, :].rearrange("p t e -> p (t e)")
            for j in range(0, EXTRA, 8):
                tj = t16[:, 0:8 * NE].rearrange("p (j e) -> p j e", e=NE)
                step(tt(tj, ove[0:1, :].unsqueeze(1).to_broadcast((1, 8, NE)),
                        iota[0:1, j:j + 8].unsqueeze(2).to_broadcast((1, 8, NE)), ALU.is_le))
                step(dve.tensor_reduce(rk.rearrange("p t k -> p (t k)")[0:1, 0:8], tj, AX.X, ALU.add))
                step(ts(btab[:, NE + j:NE + j + 8], rk.rearrange("p t k -> p (t k)")[0:1, 0:8], float(NE - 1), None, ALU.min))
            step(dve.tensor_copy(btab[:, 0:NE], iota[0:1, :]))
            step(ts(rk[0:1, 0, :], ove[0:1, NE - 1:NE].to_broadcast((1, 2)), float(NE + U - 1), None, ALU.add))
            step(dve.tensor_copy(nloop[:, :], rk[0:1, 0, :]))
            step(ts(nloop[:, :], nloop[:, :], 2, None, ALU.arith_shift_right))
            ts(nloop[:, 1:2], nloop[:, 1:2], -1, None, ALU.add).then_inc(s_rt_ready, 1)
            dve.wait_ge(s_pp_done, 2 * NT)
            dve.memset(G, 0.0).then_inc(s_g_init, 1)
            dve.wait_ge(idx_full, 16)
            ts(idx_all[:, :], out_all[:, :], 1, None, ALU.arith_shift_right).then_inc(s_g_init, 1)
            dve.memset(idle[:, 4:5], 0.0).then_inc(s_ysb_free, 1)

            def take_block(b2):
                tt(uT[:, b2, :].rearrange("p (k c) -> p k c", c=S), PS[6 + b2][:, :].rearrange("p (k c) -> p k c", c=S),
                   gains(V_FFN, 0, KT, S), ALU.mult).then_inc(s_uT_ready, 1)

            n = dve.value_load(nloop[0:1, 0:1], min_val=NE // U, max_val=NB // U)
            dve.wait_ge(s_T_done, 1)
            take_block(0)
            dve.wait_ge(s_pp_out, 2 * NT)
            with dve.Fori(0, n) as i:
                for s in range(U):
                    dve.wait_ge(s_sg_ready, i * U + (s + 1))
                    dve.wait_ge(s_up_done, i * U + (s + 1))
                    tt(act_tok[:, s % 2, :], PS[1][S:2 * S, 0:FF], sg[:, s % 2, :], ALU.mult).then_inc(s_act_ready, 1)
                    dve.wait_ge(s_actT_done, i * U + (s + 1))
                    dve.tensor_copy(actT[:, s % 2, :], PS[2][:, 0:2 * S]).then_inc(s_actT_ready, 1)
                    dve.wait_ge(s_T_done, i * U + (s + 2))
                    take_block((s + 1) % 2)

            def combine(t):
                R = ROWS[t]
                dve.wait_ge(yg_full[t], 16)
                step(stt(h1[0:R, t, :], Yg[0:R, 2 * t, :], wgt[0:R, t, 0:1], h1[0:R, t, :], ALU.mult, ALU.add))
                stt(h1[0:R, t, :], Yg[0:R, 2 * t + 1, :], wgt[0:R, t, 1:2], h1[0:R, t, :], ALU.mult, ALU.add).then_inc(s_f_h2, 1)
                dve.wait_ge(s_f_rstd, t + 1)
                step(dve.reciprocal(rstd[0:R, 10 + t:11 + t], rms_[0:R, 10 + t:11 + t]))
                if t >= 2:
                    dve.wait_ge(s_f_T, 2 * (t - 1))
                ts(row[0:R, t % 2, :], h1[0:R, t, :], rstd[0:R, 10 + t:11 + t], None, ALU.mult).then_inc(s_f_v, 1)

            def take_v(t):
                if t >= 2:
                    dve.wait_ge(s_f_g, 2 * (t - 1))
                for half in range(2):
                    dve.wait_ge(s_f_T, 2 * t + half + 1)
                    take_rows(PS[6 + half], t, half, V_PLE, s_f_vT)

            def finish(t):
                R = ROWS[t]
                gate = Yg[0:R, 2 * t, :]
                n, w = (2, 512) if t < 4 else (4, D // 4)
                for h in range(n):
                    hh = slice(h * w, (h + 1) * w)
                    dve.wait_ge(s_f_g, 2 * t + h + 1 if t < 4 else 10)
                    src = PS[2 * (t % 2) + h][:, :] if t < 4 else PS[0][32 * h:32 * h + NS, 0:w]
                    tt(gate[:, hh], src, bple[0:R, hh], ALU.add).then_inc(s_f_gb, 1)
                dve.wait_ge(s_f_sig, t + 1)
                step(tt(gate, gate, pp[0:R, t, :], ALU.mult))
                last(tt(h1[0:R, t, :], h1[0:R, t, :], gate, ALU.add), s_f_h3, t + 1)
                dve.wait_ge(s_f_r2, t + 1)
                step(dve.reciprocal(rstd[0:R, 15 + t:16 + t], rms_[0:R, 15 + t:16 + t]))
                stt(yout[0:R, t, :], h1[0:R, t, :], rstd[0:R, 15 + t:16 + t], bfin[0:R, :], ALU.mult, ALU.mult).then_inc(s_f_y, 1)

            dve.wait_ge(ld_bias, 32)
            combine(0)
            take_v(0)
            combine(1)
            take_v(1)
            for t in range(NT):
                if t + 2 < NT:
                    combine(t + 2)
                    take_v(t + 2)
                finish(t)


_INS = ["x_prompt", "x_sample", "p_prompt", "p_sample", "state_pool", "state_conv", "state_ssm", "norm_mix",
        "w_in", "pool_lin_w", "pool_lin_b", "pool_scale", "conv_w", "conv_b", "dt_bias", "a_log", "d_skip",
        "ssd_norm", "w_out", "norm_ffn", "router_grp_w", "router_grp_b", "router_exp_w", "router_exp_b",
        "exp_w_gate", "exp_w_up", "exp_w_down", "norm_ple", "ple_gate_w", "ple_gate_b", "ple_proj_w", "norm_final"]
_OUTS = [("y_p", (1, SEQ, D)), ("y_s", (NS, 1, D)), ("pool_p", (1, 1, BUF, PW)), ("conv_p", (1, 1, TAPS - 1, CONV)),
         ("ssm_p", (1, 1, NH, HD, NST)), ("pool_s", (1, NS, BUF, PW)), ("conv_s", (1, NS, TAPS - 1, CONV)),
         ("ssm_s", (1, NS, NH, HD, NST))]


def kernel(**inputs):
    import numpy as np
    import concourse.bacc as bacc
    from concourse.bass_utils import run_bass_kernel_spmd

    nc = bacc.Bacc("TRN2", target_bir_lowering=False, num_devices=1)
    arrays = {f"in_{name}": np.ascontiguousarray(inputs[name]) for name in _INS}
    for name in ("exp_w_gate", "exp_w_up", "exp_w_down"):
        w = arrays[f"in_{name}"]
        arrays[f"in_{name}"] = w.reshape(NE, w.shape[3], w.shape[4])
    arrays["in_consts"], arrays["in_heads"] = shape_constants(np)
    a = {k[3:]: nc.dram_tensor(k, v.shape, F32, kind="ExternalInput").ap() for k, v in arrays.items()}
    o = {name: nc.dram_tensor(f"out_{name}", shape, F32, kind="ExternalOutput").ap() for name, shape in _OUTS}
    build(nc, a, o)
    r = run_bass_kernel_spmd(nc, [arrays], core_ids=[0])
    return tuple(r.results[0][f"out_{name}"] for name, _ in _OUTS)
```

```python
import concourse.bass as bass
from concourse import mybir
from contextlib import ExitStack

F32 = mybir.dt.float32
BF16 = mybir.dt.bfloat16
I32 = mybir.dt.int32
U32 = mybir.dt.uint32
ALU = mybir.AluOpType
ACT = mybir.ActivationFunctionType
AX = mybir.AxisListType

P = 128
D = 1024
KT = D // P
SEQ, NS = 512, 8
TOK = SEQ + NS
HALF = TOK // 2
NT = 5
ROWS = [128, 128, 128, 128, NS]
TAIL = [4, 0, 1, 2, 3]
PW, NG, WINS, BUF = 512, 4, (2, 4, 8, 16), 15
NH, HD, NST = 8, 64, 64
XT = 6
CONV = XT * P
TAPS = 4
NC_ = SEQ // P
IN_DIM = 1800
NE, FF, PLE = 32, 256, 256
S = 64
EXTRA = 2 * TOK // S
NB = NE + EXTRA
U = 4
NBT = NB + U
NONE = 1 << 20
EPS = 1e-6
GU = KT * 2 * FF
DN = 2 * D

V_MIX, V_PB, V_PS, V_CW, V_CB, V_SN, V_FFN, V_PLE, NV = 0, 8, 12, 16, 40, 46, 50, 58, 66

C_ID, C_CAUSAL, C_BEFORE, C_ONES, C_I2, C_INV, C_POOLSEL, C_IOTA, C_TOKID, C_BAD, C_EPS = (
    0, 128, 256, 384, 512, 576, 640, 672, 736, 746, 751)
NCONST = 752
H_EXP, H_ROW, NHEAD = 0, 512, 1536


def shape_constants(np):
    c = np.zeros((P, NCONST), np.float32)
    i = np.arange(P)
    c[:, C_ID:C_ID + P] = np.eye(P)
    c[:, C_CAUSAL:C_CAUSAL + P] = i[None, :] >= i[:, None]
    c[:, C_BEFORE:C_BEFORE + P] = i[:, None] < i[None, :]
    c[:, C_ONES:C_ONES + P] = 1
    c[:, C_I2:C_I2 + 64] = (i[:, None] % 64) == np.arange(64)[None, :]
    for g, w in enumerate(WINS):
        c[:, C_INV + 16 * g:C_INV + 16 * g + 16] = 1.0 / np.minimum(np.arange(16) + 1, w)
        for b in range(NS):
            for tau in range(BUF):
                c[b * BUF + tau, C_POOLSEL + 8 * g + b] = tau >= BUF + 1 - w
    c[:, C_IOTA:C_IOTA + S] = np.arange(S)
    for t in range(NT):
        for k in range(2):
            c[:, C_TOKID + 2 * t + k] = 2 * (t * P + i) + k + 1
        c[:, C_BAD + t] = 4096.0 * (i >= ROWS[t])
    c[:, C_EPS] = EPS
    h = np.zeros((NH, NHEAD), np.float32)
    for t in range(4):
        for p in range(P):
            h[2 * t + p // 64, H_EXP + t * P + p] = 1
    for k in range(NH):
        h[k, H_ROW + k * P:H_ROW + (k + 1) * P] = 1
    return c, h


def build(nc, a, o):
    ctx = ExitStack()
    with ctx:
        def sem(name):
            return ctx.enter_context(nc.semaphore(name))

        class Steps:

            def __init__(self, eng, own):
                self.eng, self.own, self.n = eng, own, 0

            def __call__(self, ins):
                self.n += 1
                ins.then_inc(self.own, 1)
                self.eng.wait_ge(self.own, self.n)

        top = [0]

        def region(n):
            start = top[0]
            top[0] += (n + 7) // 8 * 8
            return start

        R_const = region(NCONST)
        R_x = region(NT * D)
        R_gu = region(U * GU)
        R_dn = region(2 * DN)
        R_aT = region(KT * TOK)
        R_v = region(NG * (BUF + TOK))
        R_xc = region(XT * TOK)
        R_xbc = region(XT * (SEQ + TAPS - 1))
        R_z = region(4 * TOK)
        R_row = region(2 * D)
        R_tb = region(2 * D)
        R_g = region(2 * D)
        R_act = region(2 * FF)
        R_samp = region(3072)
        R_dt = region(2 * TOK)
        R_small = region(1104)
        mem = ctx.enter_context(nc.sbuf_tensor("mem", [P, top[0]], F32))

        def at(off, *shape, rows=P):
            n = 1
            for s in shape:
                n *= s
            view = mem[0:rows, off:off + n]
            if len(shape) == 2:
                view = view.rearrange("p (a b) -> p a b", b=shape[1])
            if len(shape) == 3:
                view = view.rearrange("p (a b c) -> p a b c", b=shape[1], c=shape[2])
            return view

        const = at(R_const, NCONST)
        ident = const[:, C_ID:C_ID + P]
        ones = const[:, C_ONES:C_ONES + P]
        eps = const[:, C_EPS:C_EPS + 1]
        h1 = at(R_x, NT, D)
        w_in = at(R_gu, KT, IN_DIM)
        gu = [at(R_gu + s * GU, 2 * KT, FF) for s in range(U)]
        dn = [at(R_dn + s * DN, 2, D) for s in range(2)]
        w_out = at(R_gu + 2 * GU, KT, D)
        aT = at(R_aT, KT, TOK)
        mixT = aT
        xbc = at(R_xbc, XT, SEQ + TAPS - 1)
        xdtT = at(R_xbc, 4, TOK)
        zs = at(R_z, 4, TOK)
        v = at(R_v, NG, BUF + TOK)
        xc = at(R_xc, XT, TOK)
        row = at(R_row, 2, D)
        junk = at(R_g, D)
        spool = at(R_act, PW, rows=NS * BUF)
        sconv = at(R_dt, CONV, rows=NS * (TAPS - 1))
        headc = at(R_tb, NHEAD, rows=NH)
        w_lin = at(R_tb + NHEAD, NG, P)
        fin = at(R_g, 4, NST)
        stage_c = at(R_gu + KT * IN_DIM, CONV, rows=11)
        stage_v = at(R_g + D, PW, rows=23)
        H = at(R_gu, NC_, 512)
        xdtE = at(R_gu + 2048, NC_, 512)
        eE = at(R_gu + 4096, 4, SEQ)
        rsg = at(R_gu + 4096, 2, TOK)
        y = at(R_gu + 6144, 4, SEQ)
        dtw = [at(R_dn + i * TOK, TOK, rows=NH) for i in range(6)]
        M = at(R_dn, NH, SEQ)
        BC = at(R_dn + 2048, 4, 512)
        dt = at(R_dt, TOK, rows=NH)
        acs = at(R_dt + TOK, TOK, rows=NH)
        xtok = at(R_g, NC_, 512)
        Btok = at(R_act, NC_, P)
        seg = at(R_row, 2, SEQ)
        Gm = at(R_row + 1024, 2, SEQ)
        hs = at(R_samp, 4, NS * NST)
        stmp = at(R_samp + 2048, 2, NS * NST)
        win = [at(R_row + i * 528, 528) for i in range(2)]
        pp = at(R_xbc, NT, D)
        w_pp = at(R_dn, 2, D)
        pT = at(R_aT + KT * D, 2, TOK)
        prow = at(R_dn + DN, NT, PLE)
        w_ple = at(R_aT, KT, D)
        bfin = at(R_samp + 1024, D)
        bple = at(R_samp + 2048, D)
        uTr = at(R_tb, 2, KT * P)
        uT = at(R_tb, 2, KT * S)
        posh = at(R_tb, 2 * NT, S)
        blkh = at(R_tb + 2 * NT * S, 2 * NT, NBT)
        tabe = at(R_tb + 2 * NT * (S + NBT), NBT, rows=S)
        G = at(R_g, 2, D, rows=S)
        sg = mem[S:2 * S, R_act:R_act + 2 * FF].rearrange("p (a b) -> p a b", b=FF)
        act_tok = mem[S:2 * S, R_g:R_g + 2 * FF].rearrange("p (a b) -> p a b", b=FF)
        actT = at(R_aT + KT * D, 2, 2 * S)
        ysb = at(R_row, 2, D, rows=S)
        Yg = at(R_gu, 2 * NT, D)
        yout = at(R_gu + 2 * NT * D, NT, D)
        sm = [R_small]

        def small(*shape, rows=P):
            r = at(sm[0], *shape, rows=rows)
            n = 1
            for s in shape:
                n *= s
            sm[0] += n
            assert sm[0] <= R_small + 1104
            return r

        vec = small(NV)
        ss = small(24)
        rms_ = small(24)
        rstd = small(24)
        acsT = small(NC_, NH)
        RL = small(NC_, NH)
        te = small(NC_, NH)
        cd = small(NC_, NH)
        xcs = small(XT, NS, TAPS)
        cprod = stmp[:, 0, 0:XT * NS * TAPS].rearrange("p (m b k) -> p m b k", b=NS, k=TAPS)
        vs = v[:, :, BUF + SEQ:BUF + TOK]
        vsum = small(NG, NS)
        cst = small(XT, 11)
        vst = small(NG, 23)
        dx = small(4, NS + 1)
        ys = small(4, NS)
        h9 = small(NS + 1, rows=NH)
        hv = small(4, rows=NH)
        rbias = small(36)
        w_rt = small(KT, 36)
        idle = small(8)
        g_ffn = small(KT)
        wgt = small(NT, 2)
        ro = [R_samp]

        def rout(*shape, base=ro):
            r = at(base[0], *shape)
            n = 1
            for s in shape:
                n *= s
            base[0] += n
            return r

        L = rout(NT, 36)
        Lg = rout(NT, 8)
        gmax = rout(NT, 8)
        gidx = rout(NT, 8).bitcast(U32)
        m4 = rout(NT, 4)
        ex4 = rout(NT, 4)
        es = rout(NT, 8)
        ev = rout(NT, 8)
        eidx = rout(NT, 8).bitcast(U32)
        gf = rout(NT)
        gw = rout(NT)
        eid = rout(NT, 2)
        e21 = rout(NT)
        rk = rout(NT, 2)
        rq = rout(NT, 2)
        rr = rout(NT, 2)
        ovt = rout(NT, 2)
        cmp0 = rout(NT, 2)
        ohs = rout(NT * 16).bitcast(BF16)
        bef = rout(P // 2).bitcast(BF16)
        oneb = rout(P // 2).bitcast(BF16)
        ovn = rout(NE)
        ove = rout(NE)
        ovb = rout(NE)
        assert ro[0] <= R_samp + 1024
        ro2 = [R_dt]
        oh = rout(NT, 2 * NE, base=ro2)
        tmp = rout(NT, 2 * NE, base=ro2)
        assert ro2[0] <= R_dt + 2 * TOK
        vecrow = ctx.enter_context(nc.sbuf_tensor("vecrow", [NV, P], F32))
        int_w = ctx.enter_context(nc.sbuf_tensor("int_w", [P, NE], I32))
        rank_i = int_w[:, 0:2 * NT].rearrange("p (t k) -> p t k", k=2)
        out_all = ctx.enter_context(nc.sbuf_tensor("out_all", [S, NBT], I32))
        idx_all = ctx.enter_context(nc.sbuf_tensor("idx_all", [S, NBT], I32))
        prime = ctx.enter_context(nc.sbuf_tensor("prime", [16, 4], I32))
        out_i = [ctx.enter_context(nc.sbuf_tensor(f"out_i{q}", [S, 1], I32)) for q in range(2)]
        idx_i = [ctx.enter_context(nc.sbuf_tensor(f"idx_i{q}", [S, 1], I32)) for q in range(2)]
        btab = ctx.enter_context(nc.sbuf_tensor("btab", [1, NB + 8], I32))
        nloop = ctx.enter_context(nc.sbuf_tensor("nloop", [1, 2], I32))
        PS = [ctx.enter_context(nc.psum_tensor(f"PS{i}", [P, 512], F32)) for i in range(8)]

        u_dram = nc.dram_tensor("u_rows", (TOK, D), F32).ap()
        y_dram = nc.dram_tensor("choice_rows", (2 * TOK, D), F32).ap()

        COLS = [("v", m, m * P, P) for m in range(NG)]
        COLS += [("xbc", m, 2 * PW + m * P, P) for m in range(XT)] + [("dt", 0, IN_DIM - NH, NH)]
        COLS += [("z", m, PW + m * P, P) for m in range(4)]
        J_XBC, J_DT, J_Z = NG, NG + XT, NG + XT + 1

        ld_bias = sem("ld_bias")
        ld_const = sem("ld_const")
        ld_head = sem("ld_head")
        ld_hs = sem("ld_hs")
        ld_hv = sem("ld_hv")
        ld_lin = sem("ld_lin")
        ld_p = sem("ld_p")
        ld_rt = sem("ld_rt")
        ld_state_c = sem("ld_state_c")
        ld_state_p = sem("ld_state_p")
        ld_wout = sem("ld_wout")
        ld_wple = sem("ld_wple")
        own_act = sem("own_act")
        own_dve = sem("own_dve")
        own_pool = sem("own_pool")
        s_M_ready = sem("s_M_ready")
        s_R_done = sem("s_R_done")
        s_R_out = sem("s_R_out")
        s_S_done = sem("s_S_done")
        s_S_out = sem("s_S_out")
        s_T_done = sem("s_T_done")
        s_YO_done = sem("s_YO_done")
        s_Y_done = sem("s_Y_done")
        s_Y_out = sem("s_Y_out")
        s_Y_ready = sem("s_Y_ready")
        s_ys_out = sem("s_ys_out")
        s_slot_ready = sem("s_slot_ready")
        s_tab_done = sem("s_tab_done")
        s_tab_ready = sem("s_tab_ready")
        s_aT_taken = sem("s_aT_taken")
        s_act_ready = sem("s_act_ready")
        s_actT_done = sem("s_actT_done")
        s_actT_ready = sem("s_actT_ready")
        s_cnt_done = sem("s_cnt_done")
        s_cnt_taken = sem("s_cnt_taken")
        s_conv_out = sem("s_conv_out")
        s_conv_pre = sem("s_conv_pre")
        s_convs_pre = sem("s_convs_pre")
        s_cst_T = sem("s_cst_T")
        s_cst_out = sem("s_cst_out")
        s_cst_ready = sem("s_cst_ready")
        s_diag_ready = sem("s_diag_ready")
        s_dt_exp = sem("s_dt_exp")
        s_dt_ln = sem("s_dt_ln")
        s_dt_neg = sem("s_dt_neg")
        s_dt_ready = sem("s_dt_ready")
        s_dt_u = sem("s_dt_u")
        s_dta_ready = sem("s_dta_ready")
        s_eE_done = sem("s_eE_done")
        s_eE_out = sem("s_eE_out")
        s_exp_a = sem("s_exp_a")
        s_f_T = sem("s_f_T")
        s_f_g = sem("s_f_g")
        s_f_gb = sem("s_f_gb")
        s_f_h2 = sem("s_f_h2")
        s_f_h3 = sem("s_f_h3")
        s_f_r2 = sem("s_f_r2")
        s_f_rstd = sem("s_f_rstd")
        s_f_sig = sem("s_f_sig")
        s_f_v = sem("s_f_v")
        s_f_vT = sem("s_f_vT")
        s_f_y = sem("s_f_y")
        s_fin_out = sem("s_fin_out")
        s_gated = sem("s_gated")
        s_gn_done = sem("s_gn_done")
        s_gn_ln = sem("s_gn_ln")
        s_gn_out = sem("s_gn_out")
        s_h9_ready = sem("s_h9_ready")
        s_idle = sem("s_idle")
        s_idx = sem("s_idx")
        s_inproj_done = sem("s_inproj_done")
        s_inproj_out = sem("s_inproj_out")
        s_lg_done = sem("s_lg_done")
        s_lg_out = sem("s_lg_out")
        s_m_ready = sem("s_m_ready")
        s_mixP_ready = sem("s_mixP_ready")
        s_mix_ready = sem("s_mix_ready")
        s_oh_ready = sem("s_oh_ready")
        s_outp_done = sem("s_outp_done")
        s_outp_out = sem("s_outp_out")
        s_pT_done = sem("s_pT_done")
        s_pT_out = sem("s_pT_out")
        s_pads = sem("s_pads")
        s_pool_done = sem("s_pool_done")
        s_pp_done = sem("s_pp_done")
        s_pp_out = sem("s_pp_out")
        s_r_rstd = sem("s_r_rstd")
        s_rstd_x = sem("s_rstd_x")
        s_rt_a = sem("s_rt_a")
        s_rt_b = sem("s_rt_b")
        s_rt_ready = sem("s_rt_ready")
        s_samp_done = sem("s_samp_done")
        s_scan1_done = sem("s_scan1_done")
        s_scan1_out = sem("s_scan1_out")
        s_seg_exp = sem("s_seg_exp")
        s_sg_ready = sem("s_sg_ready")
        s_sq_out = sem("s_sq_out")
        s_states_T = sem("s_states_T")
        s_states_in = sem("s_states_in")
        s_te_in = sem("s_te_in")
        s_te_ready = sem("s_te_ready")
        s_uT_ready = sem("s_uT_ready")
        s_uTr_done = sem("s_uTr_done")
        s_uTr_out = sem("s_uTr_out")
        s_u_ready = sem("s_u_ready")
        s_up_done = sem("s_up_done")
        s_vec_T = sem("s_vec_T")
        s_vst_ready = sem("s_vst_ready")
        s_xT_done = sem("s_xT_done")
        s_xdtE_ready = sem("s_xdtE_ready")
        s_xn_ready = sem("s_xn_ready")
        s_ysb_free = sem("s_ysb_free")
        st_conv = sem("st_conv")
        st_fin = sem("st_fin")
        st_hs = sem("st_hs")
        st_out = sem("st_out")
        st_pool = sem("st_pool")
        st_shift = sem("st_shift")
        ld_vec = [sem(f"ld_vec{i}") for i in range(2)]
        ld_x = [sem(f"ld_x{i}") for i in range(NT)]
        ld_w = [sem(f"ld_w{i}") for i in range(3)]
        w_full = [sem(f"w_full{i}") for i in range(U)]
        d_full = [sem(f"d_full{i}") for i in range(2)]
        g_full = [sem(f"g_full{i}") for i in range(2)]
        y_written = [sem(f"y_written{i}") for i in range(2)]
        u_stored = [sem(f"u_stored{i}") for i in range(2)]
        yg_full = [sem(f"yg_full{i}") for i in range(NT)]
        block = ctx.enter_context(nc.Block())

        def load_vectors(eng, first, end):
            signal = ld_vec[0 if first == 0 else 1]
            for name, lo, hi in [("norm_mix", V_MIX, V_PB), ("conv_w", V_CW, V_CB), ("conv_b", V_CB, V_SN),
                                 ("pool_lin_b", V_PB, V_PS), ("pool_scale", V_PS, V_CW), ("ssd_norm", V_SN, V_FFN),
                                 ("norm_ffn", V_FFN, V_PLE), ("norm_ple", V_PLE, NV)][first:end]:
                src = a[name]
                if name == "conv_w":
                    src = src.rearrange("a k (m p) -> (a k m) p", p=P)
                elif name == "pool_lin_b":
                    src = src.rearrange("a g p -> (a g) p")
                else:
                    src = src.rearrange("a (m p) -> (a m) p", p=P)
                eng.dma_start(vecrow[lo:hi, :], src).then_inc(signal, 16)

        @block.sync
        def _(sp):
            sp.dma_start(const, a["consts"]).then_inc(ld_const, 16)
            for t in range(NT):
                src = a["x_prompt"][0, t * P:(t + 1) * P, :] if t < 4 else a["x_sample"][:, 0, :]
                sp.dma_start(h1[0:ROWS[t], t, :], src).then_inc(ld_x[t], 16)
            w = a["w_in"][0].rearrange("(k p) n -> p k n", p=P)
            for i, (lo, hi) in enumerate([(0, PW), (2 * PW, IN_DIM), (PW, 2 * PW)]):
                sp.dma_start(w_in[:, :, lo:hi], w[:, :, lo:hi]).then_inc(ld_w[i], 16)
            for t in range(4):
                sp.dma_start(hs[:, t].rearrange("p (b n) -> p b n", n=NST),
                             a["state_ssm"][0, :, 2 * t:2 * t + 2].rearrange("b h p n -> (h p) b n")
                             ).then_inc(ld_hs, 16)
            sp.dma_start(o["pool_s"][0, :, 0:BUF - 1, :], a["state_pool"][0, :, 1:BUF, :]).then_inc(st_shift, 16)
            sp.dma_start(o["conv_s"][0, :, 0:2, :], a["state_conv"][0, :, 1:3, :]).then_inc(st_shift, 16)
            sp.wait_ge(s_cst_out, 1)
            sp.dma_start(o["conv_p"][0, 0], stage_c[0:3, :]).then_inc(st_conv, 16)
            sp.dma_start(o["conv_s"][0, :, 2, :], stage_c[3:11, :]).then_inc(st_conv, 16)
            sp.dma_start(o["pool_p"][0, 0], stage_v[0:BUF, :]).then_inc(st_pool, 16)
            sp.dma_start(o["pool_s"][0, :, BUF - 1, :], stage_v[BUF:23, :]).then_inc(st_pool, 16)
            sp.wait_ge(s_inproj_done, len(COLS))
            sp.wait_ge(st_conv, 32)
            sp.dma_start(w_out, a["w_out"][0].rearrange("(k p) n -> p k n", p=P)).then_inc(ld_wout, 16)
            sp.wait_ge(s_samp_done, 4)
            for t in range(4):
                sp.dma_start(o["ssm_s"][0, :, 2 * t:2 * t + 2].rearrange("b h p n -> (h p) b n"),
                             hs[:, t].rearrange("p (b n) -> p b n", n=NST)).then_inc(st_hs, 16)
            sp.wait_ge(s_fin_out, 1)
            sp.dma_start(o["ssm_p"][0, 0].rearrange("(t h) p n -> (h p) t n", h=2), fin).then_inc(st_fin, 16)
            sp.wait_ge(s_Y_done, 4)
            sp.dma_start(w_pp, a["ple_proj_w"][0].rearrange("(k p) n -> p k n", p=P)).then_inc(ld_p, 16)
            sp.dma_start(prow[:, 0:4, :], a["p_prompt"][0, 0].rearrange("(t p) n -> p t n", p=P)).then_inc(ld_p, 16)
            sp.dma_start(prow[0:NS, 4, :], a["p_sample"][0, :, 0, :]).then_inc(ld_p, 16)

            def load_gate_up(slot, src_e):
                sp.dma_start(gu[slot][:, 0:KT, :], a["exp_w_gate"][src_e].rearrange("a (p k) f -> p (a k) f", p=P)
                             ).then_inc(w_full[slot], 16)
                sp.dma_start(gu[slot][:, KT:2 * KT, :], a["exp_w_up"][src_e].rearrange("a (p k) f -> p (a k) f", p=P)
                             ).then_inc(w_full[slot], 16)

            def load_down(slot, src_e):
                sp.dma_start(dn[slot], a["exp_w_down"][src_e].rearrange("a (k p) n -> p (a k) n", p=P)
                             ).then_inc(d_full[slot], 16)

            sp.wait_ge(st_fin, 16)
            sp.wait_ge(s_mix_ready, 4)
            for b in range(2):
                load_gate_up(b, bass.ds(b, 1))
            for t in range(NT):
                sp.wait_ge(s_u_ready, t + 1)
                rows = ROWS[t]
                sp.dma_start(u_dram[t * P:t * P + rows, :], row[0:rows, t % 2, :]).then_inc(u_stored[t % 2], 16)
            sp.wait_ge(st_hs, 64)
            sp.dma_start(bfin, a["norm_final"].unsqueeze(0).to_broadcast((P, D))).then_inc(ld_bias, 16)
            sp.dma_start(bple, a["ple_gate_b"].to_broadcast((P, D))).then_inc(ld_bias, 16)
            sp.wait_ge(s_outp_done, NT)
            for b in range(2, U):
                load_gate_up(b, bass.ds(b, 1))
            sp.dma_start(w_ple, a["ple_gate_w"][0].rearrange("(k p) n -> p k n", p=P)).then_inc(ld_wple, 16)
            sp.wait_ge(s_pT_done, NT)
            load_down(1, bass.ds(1, 1))
            sp.wait_ge(s_pp_done, 2 * NT)
            load_down(0, bass.ds(0, 1))
            sp.wait_ge(s_rt_ready, 1)
            m = sp.value_load(nloop[0:1, 1:2], min_val=NE // U - 1, max_val=NB // U - 1)
            with sp.Fori(0, m) as i:
                for s in range(U):
                    e = sp.value_load(btab[0:1, bass.ds(i * U + (U + s), 1)], min_val=0, max_val=NE - 1)
                    sp.wait_ge(s_up_done, i * U + (s + 1))
                    load_gate_up(s, bass.ds(e, 1))
                    e = sp.value_load(btab[0:1, bass.ds(i * U + (s + 2), 1)], min_val=0, max_val=NE - 1)
                    sp.wait_ge(s_Y_ready, i * U + (s + 1))
                    load_down(s % 2, bass.ds(e, 1))
            for s in range(2):
                e = sp.value_load(btab[0:1, bass.ds(m * U + (s + 2), 1)], min_val=0, max_val=NE - 1)
                sp.wait_ge(s_Y_ready, m * U + (s + 1))
                load_down(s % 2, bass.ds(e, 1))
            sp.wait_ge(y_written[0], m * 32 + 48)
            sp.wait_ge(y_written[1], m * 32 + 48)
            for t in TAIL:
                sp.dma_start(Yg[0:ROWS[t], 2 * t:2 * t + 2, :],
                             y_dram[2 * t * P:2 * (t * P + ROWS[t]), :].rearrange("(p k) n -> p k n", k=2)
                             ).then_inc(yg_full[t], 16)
            for i, t in enumerate(TAIL):
                rows = ROWS[t]
                sp.wait_ge(s_f_y, i + 1)
                dst = o["y_p"][0, t * P:(t + 1) * P, :] if t < 4 else o["y_s"][:, 0, :]
                sp.dma_start(dst, yout[0:rows, t, :]).then_inc(st_out, 16)
            sp.wait_ge(st_out, 16 * NT)
            sp.wait_ge(st_shift, 32)
            sp.wait_ge(st_pool, 32)
            sp.wait_ge(st_hs, 64)

        @block.tensor
        def _(pe):
            def transpose(dst, src, n):
                return pe.transpose(dst, src, ident[0:n, 0:n])

            pe.wait_ge(ld_const, 16)
            for half in range(2):
                pe.wait_ge(ld_vec[half], 16 * 4)
            transpose(PS[6][:, 0:NV], vecrow[:, :], NV).then_inc(s_vec_T, 1)
            for j in range(2 * NT):
                t, half = j // 2, j % 2
                R = ROWS[t]
                pe.wait_ge(s_xn_ready, t + 1)
                if j >= 2:
                    pe.wait_ge(s_aT_taken, j - 1)
                for q in range(4):
                    k = 4 * half + q
                    ins = transpose(PS[4 + j % 2][:, q * P:q * P + R], row[0:R, t % 2, k * P:(k + 1) * P], R)
                ins.then_inc(s_xT_done, 1)

            def inproj(j):
                kind, m, col, n = COLS[j]
                pe.wait_ge(ld_w[0 if j < J_XBC else 1 if j < J_Z else 2], 16)
                if j >= 2:
                    pe.wait_ge(s_inproj_out, j - 1)
                for k in range(KT):
                    if kind == "dt":
                        for q in range(4):
                            ins = pe.matmul(PS[2 * (j % 2)][32 * q:32 * q + n, 0:TOK // 4], w_in[:, k, col:col + n],
                                            aT[:, k, q * (TOK // 4):(q + 1) * (TOK // 4)], start=(k == 0), stop=(k == KT - 1))
                        continue
                    for h in range(2):
                        ins = pe.matmul(PS[2 * (j % 2) + h][0:n, 0:HALF], w_in[:, k, col:col + n],
                                        aT[:, k, h * HALF:(h + 1) * HALF], start=(k == 0), stop=(k == KT - 1))
                ins.then_inc(s_inproj_done, 1)

            pe.wait_ge(s_aT_taken, 2 * NT)
            for j in range(NG):
                inproj(j)
            pe.wait_ge(ld_state_c, 16)
            pe.wait_ge(ld_state_p, 16)
            for m in range(XT):
                transpose(PS[7][:, m * 24:(m + 1) * 24], sconv[:, m * P:(m + 1) * P], 24)
            for g in range(NG):
                ins = pe.matmul(PS[7][:, 256 + g * NS:256 + (g + 1) * NS], spool[:, g * P:(g + 1) * P],
                                const[0:NS * BUF, C_POOLSEL + 8 * g:C_POOLSEL + 8 * g + 8], start=True, stop=True)
            ins.then_inc(s_states_T, 1)
            for j in range(NG, J_Z + 1):
                inproj(j)
            pe.wait_ge(s_cst_ready, 1)
            for m in range(XT):
                transpose(PS[4 + m // 4][0:11, (m % 4) * P:(m % 4 + 1) * P], cst[:, m, :], P)
            pe.wait_ge(s_vst_ready, 1)
            for g in range(NG):
                ins = transpose(PS[6][0:23, g * P:(g + 1) * P], vst[:, g, :], P)
            ins.then_inc(s_cst_T, 1)
            inproj(J_Z + 1)
            pe.wait_ge(ld_lin, 16)
            pe.wait_ge(s_cst_out, 1)
            for g in range(NG):
                pe.wait_ge(s_m_ready, g + 1)
                if g >= 2:
                    pe.wait_ge(s_mixP_ready, g - 1)
                for h in range(2):
                    ins = pe.matmul(PS[4 + 2 * (g % 2) + h][:, 0:HALF], w_lin[:, g, :],
                                    v[:, g, BUF + h * HALF:BUF + (h + 1) * HALF], start=True, stop=True)
                ins.then_inc(s_pool_done, 1)
            pe.wait_ge(s_dt_ready, 1)
            pe.wait_ge(ld_head, 16)
            for t in range(4):
                if t < 2:
                    pe.wait_ge(s_mixP_ready, t + 3)
                if t >= 2:
                    pe.wait_ge(s_scan1_out, t - 1)
                for h in range(2):
                    ins = pe.matmul(PS[4 + 2 * (t % 2) + h][:, 0:HALF], headc[:, H_EXP + t * P:H_EXP + (t + 1) * P],
                                    dt[:, h * HALF:(h + 1) * HALF], start=True, stop=True)
                ins.then_inc(s_scan1_done, 1)
            pe.wait_ge(s_scan1_out, 3)
            for c in range(NC_):
                ins = transpose(PS[4][:, c * NH:(c + 1) * NH], acs[:, c * P:(c + 1) * P], NH)
            ins.then_inc(s_scan1_done, 1)
            for c in range(NC_):
                ins = transpose(PS[5][:, c * P:(c + 1) * P], xc[:, 4, c * P:(c + 1) * P], P)
            ins.then_inc(s_scan1_done, 1)
            pe.wait_ge(s_scan1_out, 4)
            for g in range(2):
                rows = slice(64 * g, 64 * g + 64)
                for c in range(NC_):
                    cc = slice(c * P, (c + 1) * P)
                    ins = pe.matmul(PS[6 + g][:, cc], xc[rows, 4, cc], xc[rows, 5, cc], start=True, stop=True)
                ins.then_inc(s_scan1_done, 1)
            for c in range(NC_):
                pe.wait_ge(s_scan1_out, 5 + c)
                for t in range(4):
                    ins = transpose(PS[4 + c][:, t * P:(t + 1) * P], xdtT[:, t, c * P:(c + 1) * P], P)
                ins.then_inc(s_scan1_done, 1)
            pe.wait_ge(s_h9_ready, 1)
            pe.wait_ge(s_scan1_out, 9)
            for t in range(4):
                ins = pe.matmul(PS[4][:, t * (NS + 1):(t + 1) * (NS + 1)], headc[:, H_EXP + t * P:H_EXP + (t + 1) * P],
                                h9[:, :], start=True, stop=True)
            ins.then_inc(s_scan1_done, 1)
            for q in range(4):
                kind, g = q // 2, q % 2
                rows = slice(64 * g, 64 * g + 64)
                pe.wait_ge(s_diag_ready, kind + 1)
                pe.wait_ge(s_scan1_out, 14 if q == 3 else 10 + q)
                ins = pe.matmul(PS[5 + q % 3][:, :], ones[rows, :], stmp[rows, kind, :], start=True, stop=True)
                ins.then_inc(s_scan1_done, 1)

            def head_row(h):
                pe.wait_ge(s_scan1_out, 17)
                if h >= 4:
                    pe.wait_ge(s_R_out, h - 3)
                pe.matmul(PS[4 + h % 4][:, :], headc[:, H_ROW + h * P:H_ROW + (h + 1) * P], acs[:, 0:SEQ],
                          start=True, stop=True).then_inc(s_R_done, 1)

            for q in range(2):
                for h in range(4):
                    head_row(4 * q + h)
                inproj(J_Z + 2 + q)
            for t in range(4):
                pe.wait_ge(s_R_out, 5 + t)
                pe.matmul(PS[4 + t][:, :], headc[:, H_EXP + t * P:H_EXP + (t + 1) * P], acs[:, 0:SEQ],
                          start=True, stop=True).then_inc(s_eE_done, 1)
            def mix_col(k, t):
                R = ROWS[t]
                return v[:, k, BUF + t * P:BUF + t * P + R] if k < NG else mixT[:, k, t * P:t * P + R]

            def outproj_part(t, k0, k1):
                for h in range(2):
                    for k in range(k0, k1):
                        ins = pe.matmul(PS[(4 + 2 * t) % 8 + h][:, :], mix_col(k, t), w_out[:, k, h * 512:(h + 1) * 512],
                                        start=(k == 0), stop=(k == KT - 1))
                return ins

            def sample_product(bank, col, w, ks=range(KT)):
                for k in ks:
                    for q in range(4):
                        ins = pe.matmul(bank[32 * q:32 * q + NS, 0:D // 4], col(k, 4), w[:, k, q * (D // 4):(q + 1) * (D // 4)],
                                        start=(k == 0), stop=(k == KT - 1))
                return ins

            for c in range(NC_):
                pe.wait_ge(s_xdtE_ready, c + 1)
                pe.wait_ge(s_eE_out, c + 1)
                pe.matmul(PS[4 + c][:, :], Btok[:, c, :], xdtE[:, c, :], start=True, stop=True).then_inc(s_S_done, 1)
            pe.wait_ge(s_inproj_out, len(COLS))
            for h in range(NH):
                pe.wait_ge(s_M_ready, h + 1)
                for c in range(NC_):
                    ins = pe.matmul(PS[h // 2][64 * (h % 2):64 * (h % 2) + 64, c * P:(c + 1) * P],
                                    xtok[:, c, h * HD:(h + 1) * HD], M[:, h, c * P:(c + 1) * P],
                                    start=True, stop=True)
                if h % 2:
                    ins.then_inc(s_Y_done, 1)
            for t in range(4):
                rows = slice(64 * (t // 2), 64 * (t // 2) + 64)
                pe.wait_ge(s_S_out, 4)
                for c in range(1, NC_):
                    ins = pe.matmul(PS[4 + t][:, c * P:(c + 1) * P], H[rows, c - 1, t * P:(t + 1) * P],
                                    xc[rows, 5, c * P:(c + 1) * P], start=True, stop=True)
                ins = pe.transpose(PS[4 + t][:, 0:NST], H[rows, NC_ - 1, t * P:(t + 1) * P], ident[rows, rows])
                ins.then_inc(s_YO_done, 1)
            pe.wait_ge(ld_wout, 16)
            pe.wait_ge(s_Y_out, 2)
            outproj_part(0, 0, 4)
            for g in range(2):
                pe.wait_ge(s_sq_out, 2 * g + 2)
                for h in range(2):
                    for q in range(2):
                        ins = pe.matmul(PS[2 * g + h][:, 0:HALF], ones, zs[:, 2 * g + q, h * HALF:(h + 1) * HALF],
                                        start=(q == 0), stop=(q == 1))
                ins.then_inc(s_gn_done, 1)
            pe.wait_ge(s_Y_out, 4)
            outproj_part(1, 0, 4)

            def outproj(t):
                if t == 0:
                    pe.wait_ge(s_mix_ready, 4)
                if t == 4:
                    pe.wait_ge(s_outp_out, 3)
                if t < 4:
                    ins = outproj_part(t, 4 if t < 2 else 0, KT)
                else:
                    ins = sample_product(PS[0], mix_col, w_out)
                ins.then_inc(s_outp_done, 1)

            def u_rows(t):
                R = ROWS[t]
                pe.wait_ge(s_u_ready, t + 1)
                for half in range(2):
                    j = 2 * t + half
                    if t >= 1:
                        pe.wait_ge(s_uTr_out, j - 1)
                    for q in range(4):
                        k = 4 * half + q
                        ins = transpose(PS[4 + half][:, q * P:q * P + R], row[0:R, t % 2, k * P:(k + 1) * P], R)
                    ins.then_inc(s_uTr_done, 1)

            def route(t):
                R = ROWS[t]
                if t == 0:
                    pe.wait_ge(s_outp_out, 2)
                pe.wait_ge(s_uTr_out, 2 * t + 2)
                pe.wait_ge(ld_rt, 80)
                for k in range(KT):
                    ins = pe.matmul(PS[6][0:R, t * 36:(t + 1) * 36], uTr[:, t % 2, k * P:k * P + R],
                                    w_rt[:, k, :], start=(k == 0), stop=(k == KT - 1))
                ins.then_inc(s_lg_done, 1)

            outproj(0)
            outproj(1)
            u_rows(0)
            outproj(2)
            route(0)
            u_rows(1)
            outproj(3)
            route(1)
            u_rows(2)
            outproj(4)
            route(2)
            u_rows(3)
            pe.wait_ge(ld_p, 48)
            pe.wait_ge(s_outp_out, 2)
            for t in range(NT):
                R = ROWS[t]
                if t >= 1:
                    pe.wait_ge(s_pT_out, t)
                for q in range(2):
                    ins = transpose(PS[7][:, q * P:q * P + R], prow[0:R, t, q * P:(q + 1) * P], R)
                ins.then_inc(s_pT_done, 1)
                if t == 1:
                    route(3)
                    u_rows(4)
            route(4)

            def pleproj(t):
                R = ROWS[t]
                for h in range(2):
                    j = 2 * t + h
                    if j == 0:
                        pe.wait_ge(s_pT_out, NT)
                        pe.wait_ge(s_outp_out, NT)
                    if j >= 4:
                        pe.wait_ge(s_pp_out, j - 3)
                    for q in range(2):
                        ins = pe.matmul(PS[j % 4][0:R, :], pT[:, q, t * P:t * P + R], w_pp[:, q, h * 512:(h + 1) * 512],
                                        start=(q == 0), stop=(q == 1))
                    ins.then_inc(s_pp_done, 1)

            pleproj(0)
            pe.wait_ge(s_oh_ready, 1)
            for t in range(NT + 1):
                for t2 in range(min(t + 1, NT)):
                    last = t2 == min(t, NT - 1)
                    ins = pe.matmul(PS[7][:, t * NE:(t + 1) * NE], bef if t2 == t else oneb, ohs[:, t2 * NE:(t2 + 1) * NE],
                                    start=(t2 == 0), stop=last)
            ins.then_inc(s_cnt_done, 1)
            for t in range(1, NT - 1):
                pleproj(t)
            pe.wait_ge(s_slot_ready, 1)
            pe.wait_ge(s_cnt_taken, 1)
            for j in range(2 * NT):
                ins = pe.matmul(PS[7][0:S, 256:256 + NBT], posh[:, j, :], blkh[:, j, :], start=(j == 0), stop=(j == 2 * NT - 1))
            ins.then_inc(s_tab_done, 1)
            pleproj(NT - 1)

            pe.wait_ge(s_rt_ready, 1)
            n = pe.value_load(nloop[0:1, 0:1], min_val=NE // U, max_val=NB // U)
            pe.wait_ge(s_cnt_taken, 1)
            pe.wait_ge(s_lg_out, NT)
            pe.wait_ge(g_full[0], 16)

            def block_rows(b2):
                for k in range(KT):
                    ins = transpose(PS[6 + b2][:, k * S:(k + 1) * S], G[:, b2, :].rearrange("s (p k) -> s k p", k=KT)[:, k, :], S)
                ins.then_inc(s_T_done, 1)

            block_rows(0)
            pe.wait_ge(s_pp_out, 2 * NT)
            with pe.Fori(0, n) as i:
                for s in range(U):
                    pe.wait_ge(s_uT_ready, i * U + (s + 1))
                    pe.wait_ge(w_full[s], i * 32 + 32)
                    for k in range(KT):
                        rows_k = uT[:, s % 2, k * S:(k + 1) * S]
                        pe.matmul(PS[0][0:S, 0:FF], rows_k, gu[s][:, k, :], start=(k == 0), stop=(k == KT - 1))
                        if k == 0:
                            pe.wait_ge(g_full[(s + 1) % 2], i * 32 + 16 * ((s + 1) // 2 + 1))
                        ins = pe.matmul(PS[1][S:2 * S, 0:FF], rows_k, gu[s][:, KT + k, :], start=(k == 0), stop=(k == KT - 1))
                    ins.then_inc(s_up_done, 1)
                    block_rows((s + 1) % 2)
                    pe.wait_ge(s_act_ready, i * U + (s + 1))
                    pe.wait_ge(s_ysb_free, i * U + (s + 1))
                    for f in range(2):
                        ins = pe.matmul(PS[2][:, f * S:(f + 1) * S], act_tok[:, s % 2, f * P:(f + 1) * P], ident[S:2 * S, S:2 * S],
                                        start=True, stop=True)
                    ins.then_inc(s_actT_done, 1)
                    pe.wait_ge(s_actT_ready, i * U + (s + 1))
                    pe.wait_ge(d_full[s % 2], i * 32 + 16 * (s // 2 + 1))
                    for f in range(2):
                        for h in range(2):
                            ins = pe.matmul(PS[4 + h][h * S:(h + 1) * S, :], actT[:, s % 2, f * S:(f + 1) * S],
                                            dn[s % 2][:, f, h * 512:(h + 1) * 512], start=(f == 0), stop=(f == 1))
                    ins.then_inc(s_Y_ready, 1)

            def v_rows(i):
                R = ROWS[TAIL[i]]
                pe.wait_ge(s_f_v, i + 1)
                for half in range(2):
                    if i >= 1:
                        pe.wait_ge(s_f_vT, 2 * i - 1 + half)
                    for q in range(4):
                        k = 4 * half + q
                        ins = transpose(PS[6 + half][:, q * P:q * P + R], row[0:R, i % 2, k * P:(k + 1) * P], R)
                    ins.then_inc(s_f_T, 1)

            def gates(i):
                pe.wait_ge(s_f_vT, 2 * i + 2)
                if i >= 2:
                    pe.wait_ge(s_f_gb, 2 * i - 2)
                if i == 0:
                    pe.wait_ge(ld_wple, 16)
                    col = lambda k, t: uTr[:, 0, k * P:k * P + NS]
                    sample_product(PS[0], col, w_ple, range(0, 2))
                    v_rows(1)
                    sample_product(PS[0], col, w_ple, range(2, KT)).then_inc(s_f_g, 2)
                    return
                for h in range(2):
                    for k in range(KT):
                        ins = pe.matmul(PS[2 * (i % 2) + h][:, :], uTr[:, i % 2, k * P:(k + 1) * P],
                                        w_ple[:, k, h * 512:(h + 1) * 512], start=(k == 0), stop=(k == KT - 1))
                    ins.then_inc(s_f_g, 1)
                    if h == 0 and i + 1 < NT:
                        v_rows(i + 1)

            v_rows(0)
            for i in range(NT):
                gates(i)

        @block.scalar
        def _(act):
            step = Steps(act, own_act)
            A = act.activation
            load_vectors(act, 0, 4)
            def rms(t, src, j, squares, ready):
                R = ROWS[t]
                step(A(squares[0:R, :], src, ACT.Square, accum_out=ss[0:R, j:j + 1]))
                A(rms_[0:R, j:j + 1], ss[0:R, j:j + 1], ACT.Sqrt, bias=eps[0:R, :], scale=1.0 / D).then_inc(ready, 1)

            act.wait_ge(ld_const, 16)
            for t in range(NT):
                act.wait_ge(ld_x[t], 16)
                rms(t, h1[0:ROWS[t], t, :], t, junk, s_rstd_x)
            act.dma_start(headc, a["heads"]).then_inc(ld_head, 16)
            act.dma_start(hv[:, 0:1], a["dt_bias"].rearrange("a h -> h a")).then_inc(ld_hv, 16)
            act.dma_start(hv[:, 1:2], a["a_log"].rearrange("a h -> h a")).then_inc(ld_hv, 16)
            act.dma_start(h9[:, NS:NS + 1], a["d_skip"].rearrange("a h -> h a")).then_inc(ld_hv, 16)
            act.dma_start(w_lin, a["pool_lin_w"][0].rearrange("g c d -> c g d")).then_inc(ld_lin, 16)
            act.dma_start(g_ffn, a["norm_ffn"].rearrange("a (p k) -> (a p) k", p=P)).then_inc(ld_rt, 16)
            act.dma_start(w_rt[:, :, 0:4], a["router_grp_w"][0].rearrange("(k p) n -> p k n", p=P)).then_inc(ld_rt, 16)
            act.dma_start(w_rt[:, :, 4:36], a["router_exp_w"][0].rearrange("(k p) n -> p k n", p=P)).then_inc(ld_rt, 16)
            act.dma_start(rbias[:, 0:4], a["router_grp_b"].to_broadcast((P, 4))).then_inc(ld_rt, 16)
            act.dma_start(rbias[:, 4:36], a["router_exp_b"].to_broadcast((P, NE))).then_inc(ld_rt, 16)
            def out(j):
                kind, m, _, n = COLS[j]
                a0, b0 = PS[2 * (j % 2)], PS[2 * (j % 2) + 1]
                cut = SEQ - HALF
                act.wait_ge(s_inproj_done, j + 1)
                if kind == "xbc":
                    A(xbc[:, m, 3:3 + HALF], a0[:, 0:HALF], ACT.Copy)
                    A(xbc[:, m, 3 + HALF:3 + SEQ], b0[:, 0:cut], ACT.Copy)
                    A(xcs[:, m, :, 3], b0[:, cut:HALF], ACT.Copy).then_inc(s_inproj_out, 1)
                elif kind == "dt":
                    for q in range(4):
                        ins = A(dtw[0][:, q * (TOK // 4):(q + 1) * (TOK // 4)], a0[32 * q:32 * q + n, 0:TOK // 4],
                                ACT.Identity, bias=hv[:, 0:1])
                    ins.then_inc(s_inproj_out, 1)
                elif kind == "z":
                    A(zs[:, m, 0:HALF], a0[:, 0:HALF], ACT.Silu)
                    A(zs[:, m, HALF:TOK], b0[:, 0:HALF], ACT.Silu).then_inc(s_inproj_out, 1)
                else:
                    A(v[:, m, BUF:BUF + HALF], a0[:, 0:HALF], ACT.Copy)
                    A(v[:, m, BUF + HALF:BUF + TOK], b0[:, 0:HALF], ACT.Copy).then_inc(s_inproj_out, 1)

            def conv_silu(m):
                act.wait_ge(s_conv_pre, m + 1)
                A(xc[:, m, 0:SEQ], xc[:, m, 0:SEQ], ACT.Silu).then_inc(s_conv_out, 1)

            for m in range(NG):
                out(m)
            act.wait_ge(s_states_T, 1)
            A(xcs[:, :, :, 0:3], PS[7][:, 0:144].rearrange("p (m b k) -> p m b k", b=NS, k=3), ACT.Copy)
            A(vsum, PS[7][:, 256:256 + NG * NS].rearrange("p (g b) -> p g b", b=NS), ACT.Copy).then_inc(s_states_in, 1)
            for m in range(XT):
                out(J_XBC + m)
                if m >= 1:
                    conv_silu(m - 1)
            act.wait_ge(ld_hv, 48)
            out(J_DT)
            conv_silu(5)
            act.wait_ge(s_convs_pre, 1)
            A(xc[:, :, SEQ:TOK], xc[:, :, SEQ:TOK], ACT.Silu).then_inc(s_conv_out, 1)
            A(hv[:, 2:3], hv[:, 1:2], ACT.Exp).then_inc(s_exp_a, 1)
            act.wait_ge(s_dt_neg, 1)
            A(dtw[2], dtw[1], ACT.Exp).then_inc(s_dt_exp, 1)
            act.wait_ge(s_dt_u, 1)
            A(dtw[4], dtw[3], ACT.Ln).then_inc(s_dt_ln, 1)
            act.wait_ge(s_dta_ready, 1)
            A(h9[:, 0:NS], dtw[5][:, SEQ:TOK], ACT.Exp).then_inc(s_h9_ready, 1)
            out(J_Z)
            act.wait_ge(s_cst_T, 1)
            A(stage_c[0:11, 0:512], PS[4][0:11, :], ACT.Copy)
            A(stage_c[0:11, 512:768], PS[5][0:11, 0:256], ACT.Copy)
            A(stage_v[0:23, :], PS[6][0:23, :], ACT.Copy).then_inc(s_cst_out, 1)
            out(J_Z + 1)

            def seg_exp(h):
                act.wait_ge(s_R_out, h + 1)
                A(seg[:, h % 2, :], seg[:, h % 2, :], ACT.Exp).then_inc(s_seg_exp, 1)

            for q in range(2):
                for h in range(4):
                    seg_exp(4 * q + h)
                if q == 0:
                    out(J_Z + 2)
            act.wait_ge(s_te_in, 1)
            A(te, te, ACT.Exp)
            A(cd, RL, ACT.Exp).then_inc(s_te_ready, 1)
            for t in range(4):
                act.wait_ge(s_eE_done, t + 1)
                A(eE[:, t, :], PS[4 + t][:, :], ACT.Exp).then_inc(s_eE_out, 1)
            out(J_Z + 3)
            for t in range(4):
                act.wait_ge(s_gated, t + 1)
                A(zs[:, t, 0:SEQ], y[:, t, :], ACT.Square)
                A(zs[:, t, SEQ:TOK], ys[:, t, :], ACT.Square).then_inc(s_sq_out, 1)
            for g in range(2):
                act.wait_ge(s_gn_done, g + 1)
                for h in range(2):
                    A(rsg[:, g, h * HALF:(h + 1) * HALF], PS[2 * g + h][:, 0:HALF], ACT.Ln,
                      bias=eps, scale=1.0 / (2 * P)).then_inc(s_gn_ln, 1)
            act.wait_ge(s_gn_ln, 4)
            for g in range(2):
                A(rsg[:, g, :], rsg[:, g, :], ACT.Exp, scale=-0.5).then_inc(s_gn_out, 1)
            for t in range(NT):
                act.wait_ge(s_outp_out, t + 1)
                rms(t, h1[0:ROWS[t], t, :], 5 + t, pp[:, NT - 1, :], s_r_rstd)
            for t in range(NT):
                R = ROWS[t]
                act.wait_ge(s_pT_done, t + 1)
                A(pT[:, :, t * P:t * P + R], PS[7][:, 0:2 * P].rearrange("p (q c) -> p q c", c=P)[:, :, 0:R],
                  ACT.Copy).then_inc(s_pT_out, 1)

            def pp_out(j):
                R = ROWS[j // 2]
                act.wait_ge(s_pp_done, j + 1)
                A(pp[0:R, j // 2, (j % 2) * 512:(j % 2 + 1) * 512], PS[j % 4][0:R, :], ACT.Copy).then_inc(s_pp_out, 1)

            pp_out(0)
            pp_out(1)
            act.wait_ge(s_rt_a, 1)
            step(A(ex4, ex4, ACT.Exp))
            A(e21, e21, ACT.Exp).then_inc(s_rt_b, 1)
            for j in range(2, 2 * NT):
                pp_out(j)
            act.wait_ge(s_rt_ready, 1)
            n = act.value_load(nloop[0:1, 0:1], min_val=NE // U, max_val=NB // U)
            with act.Fori(0, n) as i:
                for s in range(U):
                    act.wait_ge(s_up_done, i * U + (s + 1))
                    A(sg[:, s % 2, :], PS[0][0:S, 0:FF], ACT.Silu).then_inc(s_sg_ready, 1)
                    act.wait_ge(s_Y_ready, i * U + (s + 1))
                    act.wait_ge(y_written[s % 2], i * 32 + 16 * (s // 2 + 1))
                    A(ysb[:, s % 2, 0:512], PS[4][0:S, :], ACT.Copy)
                    A(ysb[:, s % 2, 512:1024], PS[5][S:2 * S, :], ACT.Copy).then_inc(s_ysb_free, 1)
            A(rms_[:, 20:21], eps, ACT.Sqrt)
            def norm_h2(i):
                t = TAIL[i]
                act.wait_ge(s_f_h2, i + 1)
                rms(t, h1[0:ROWS[t], t, :], 10 + t, yout[:, t, :], s_f_rstd)

            def sigmoid(i):
                t = TAIL[i]
                for h in range(2):
                    gate = Yg[0:ROWS[t], 2 * t, h * 512:(h + 1) * 512]
                    act.wait_ge(s_f_gb, 2 * i + h + 1)
                    A(gate, gate, ACT.Sigmoid).then_inc(s_f_sig, 1)

            def norm_h3(i):
                t = TAIL[i]
                act.wait_ge(s_f_h3, i + 1)
                rms(t, h1[0:ROWS[t], t, :], 15 + t, yout[:, t, :], s_f_r2)

            norm_h2(0)
            norm_h2(1)
            norm_h2(2)
            for i in range(NT):
                sigmoid(i)
                if i + 3 < NT:
                    norm_h2(i + 3)
                norm_h3(i)

        @block.gpsimd
        def _(pool):
            step = Steps(pool, own_pool)
            load_vectors(pool, 4, 8)
            pool.dma_start(sconv, a["state_conv"][0].rearrange("b r c -> (b r) c")).then_inc(ld_state_c, 16)
            pool.dma_start(spool, a["state_pool"][0].rearrange("b r c -> (b r) c")).then_inc(ld_state_p, 16)
            step(pool.memset(idle[:, :], 0.0))
            pool.memset(xbc[:, :, 0:TAPS - 1], 0.0)
            pool.memset(v[:, :, 0:BUF], 0.0).then_inc(s_pads, 1)
            pool.wait_ge(s_inproj_out, NG)
            pool.tensor_copy(vst[:, :, 0:BUF], v[:, :, SEQ:SEQ + BUF])
            step(pool.tensor_copy(vst[:, :, BUF:23], vs))
            pool.wait_ge(s_states_in, 1)
            for g in range(NG):
                src = v[:, g, :]
                for q in range(g + 1):
                    dst = win[q % 2][:, 0:SEQ + BUF]
                    sh = 1 << q
                    lo = 2 * sh - 1
                    step(pool.tensor_tensor(dst[:, lo:], src[:, lo:SEQ + BUF], src[:, lo - sh:SEQ + BUF - sh], ALU.add))
                    src = dst
                first, rest = src[:, BUF:BUF + 16], src[:, BUF + 16:BUF + SEQ]
                pool.tensor_tensor(first, first, const[:, C_INV + 16 * g:C_INV + 16 * g + 16], ALU.mult)
                pool.tensor_scalar(rest, rest, 1.0 / WINS[g], None, ALU.mult)
                step(pool.tensor_tensor(vsum[:, g, :], vsum[:, g, :], vs[:, g, :], ALU.add))
                step(pool.tensor_scalar(vsum[:, g, :], vsum[:, g, :], 1.0 / WINS[g], None, ALU.mult))
                pool.tensor_tensor(vs[:, g, :], vsum[:, g, :], vs[:, g, :], ALU.subtract)
                step(pool.tensor_tensor(v[:, g, BUF:BUF + SEQ], src[:, BUF:BUF + SEQ], v[:, g, BUF:BUF + SEQ], ALU.subtract))
                if g == 0:
                    pool.tensor_copy(idle[:, 4:5], idle[:, 1:2]).then_inc(s_vst_ready, 1)
                pool.tensor_copy(idle[:, 3:4], idle[:, 2:3]).then_inc(s_m_ready, 1)
                pool.wait_ge(s_m_ready, g + 1)
            pool.wait_ge(s_inproj_out, J_XBC + XT)
            pool.tensor_copy(cst[:, :, 0:3], xbc[:, :, SEQ:SEQ + 3])
            pool.tensor_copy(cst[:, :, 3:11], xcs[:, :, :, 3]).then_inc(s_cst_ready, 1)
            pool.wait_ge(s_scan1_out, 17)
            pool.wait_ge(ld_hs, 64)

            def bn(view):
                return view.rearrange("p (b n) -> p b n", n=NST)

            for t in range(4):
                step(pool.tensor_tensor(bn(hs[:, t]), bn(hs[:, t]), dx[:, t, 0:NS].unsqueeze(2).to_broadcast((P, NS, NST)), ALU.mult))
                step(pool.tensor_tensor(bn(stmp[:, 0]), bn(BC[:, t // 2]), xdtT[:, t, SEQ:TOK].unsqueeze(2).to_broadcast((P, NS, NST)), ALU.mult))
                step(pool.tensor_tensor(hs[:, t], hs[:, t], stmp[:, 0], ALU.add))
                if t >= 1:
                    pool.wait_ge(s_ys_out, t)
                pool.tensor_tensor(stmp[:, 1], hs[:, t], BC[:, 2 + t // 2], ALU.mult).then_inc(s_samp_done, 1)
            pool.wait_ge(st_fin, 16)
            step(pool.memset(G, 0.0))
            step(pool.memset(prime[:, :], 0))
            for q in range(2):
                pool.dma_start(prime[:, 2 + q:3 + q], prime[:, q:q + 1], allow_slow_non_contiguous=True
                               ).then_inc(y_written[q], 16)
            pool.wait_ge(s_tab_ready, 1)
            pool.wait_ge(u_stored[0], 48)
            pool.wait_ge(u_stored[1], 32)
            def idle_step(before):
                pool.wait_ge(s_idle, before)
                pool.tensor_tensor(idle[:, 0:1], idle[:, 1:2], idle[:, 2:3], ALU.add).then_inc(s_idle, 1)

            pool.tensor_tensor(idle[:, 0:1], idle[:, 1:2], idle[:, 2:3], ALU.add).then_inc(s_idle, 1)

            def gather(q):
                pool.indirect_dma_start(G[:, q, :], None, u_dram, bass.IndirectOffsetOnAxis(ap=idx_i[q][:, 0:1], axis=0),
                                        bounds_check=TOK - 1, oob_is_err=False).then_inc(g_full[q], 16)

            for q in range(2):
                pool.tensor_copy(idx_i[q][:, :], idx_all[:, q:q + 1]).then_inc(s_idx, 1)
            pool.wait_ge(s_idx, 2)
            for q in range(2):
                gather(q)
            pool.wait_ge(s_rt_ready, 1)
            n = pool.value_load(nloop[0:1, 0:1], min_val=NE // U, max_val=NB // U)
            pool.wait_ge(s_T_done, 1)
            pool.wait_ge(g_full[0], 16)
            pool.tensor_copy(idx_i[0][:, :], idx_all[:, 2:3]).then_inc(s_idx, 1)
            pool.wait_ge(s_idx, 3)
            gather(0)
            with pool.Fori(0, n) as i:
                for s in range(U):
                    q = (s + 1) % 2
                    pool.wait_ge(s_T_done, i * U + (s + 2))
                    pool.wait_ge(g_full[q], i * 32 + 16 * ((s + 1) // 2 + 1))
                    idle_step(i * 6 * U + (6 * s + 1))
                    pool.tensor_copy(idx_i[q][:, :], idx_all[:, bass.ds(i * U + (s + 3), 1)]).then_inc(s_idle, 1)
                    idle_step(i * 6 * U + (6 * s + 3))
                    gather(q)
                    pool.wait_ge(y_written[s % 2], i * 32 + 16 * (s // 2 + 1))
                    pool.wait_ge(s_ysb_free, i * U + (s + 2))
                    idle_step(i * 6 * U + (6 * s + 4))
                    pool.tensor_copy(out_i[s % 2][:, :], out_all[:, bass.ds(i * U + s, 1)]).then_inc(s_idle, 1)
                    idle_step(i * 6 * U + (6 * s + 6))
                    pool.indirect_dma_start(y_dram, bass.IndirectOffsetOnAxis(ap=out_i[s % 2][:, 0:1], axis=0),
                                            ysb[:, s % 2, :], None, bounds_check=2 * TOK - 1, oob_is_err=False
                                            ).then_inc(y_written[s % 2], 16)

        @block.vector
        def _(dve):
            step = Steps(dve, own_dve)
            tt, ts, stt = dve.tensor_tensor, dve.tensor_scalar, dve.scalar_tensor_tensor

            def last(ins, signal, count):
                ins.then_inc(signal, 1)
                dve.wait_ge(signal, count)

            def tiles(bank, n=4):
                return bank.rearrange("p (c l) -> p c l", l=bank.shape[1] // n)

            def gains(col, k, n, m):
                return vec[:, col + k:col + k + n].unsqueeze(2).to_broadcast((P, n, m))

            dve.wait_ge(s_vec_T, 1)
            step(dve.tensor_copy(vec, PS[6][:, 0:NV]))

            def norm_x(t):
                R = ROWS[t]
                dve.wait_ge(s_rstd_x, t + 1)
                step(dve.reciprocal(rstd[0:R, t:t + 1], rms_[0:R, t:t + 1]))
                if t >= 2:
                    dve.wait_ge(s_xT_done, 2 * (t - 1))
                ts(row[0:R, t % 2, :], h1[0:R, t, :], rstd[0:R, t:t + 1], None, ALU.mult).then_inc(s_xn_ready, 1)

            def take_x(j):
                t, half = j // 2, j % 2
                R = ROWS[t]
                dve.wait_ge(s_xT_done, j + 1)
                tt(aT[:, 4 * half:4 * half + 4, t * P:t * P + R], tiles(PS[4 + j % 2][:, :])[:, :, 0:R],
                   gains(V_MIX, 4 * half, 4, R), ALU.mult).then_inc(s_aT_taken, 1)

            norm_x(0)
            norm_x(1)
            for t in range(NT):
                take_x(2 * t)
                take_x(2 * t + 1)
                if t + 2 < NT:
                    norm_x(t + 2)
            dve.wait_ge(s_pads, 1)
            for m in range(XT):
                dve.wait_ge(s_inproj_out, J_XBC + m + 1)
                acc = xc[:, m, 0:SEQ]
                step(ts(acc, xbc[:, m, 0:SEQ], vec[:, V_CW + m:V_CW + m + 1], vec[:, V_CB + m:V_CB + m + 1],
                        ALU.mult, ALU.add))
                for k in range(1, TAPS):
                    col = V_CW + k * XT + m
                    ins = stt(acc, xbc[:, m, k:k + SEQ], vec[:, col:col + 1], acc, ALU.mult, ALU.add)
                    if k < TAPS - 1:
                        step(ins)
                ins.then_inc(s_conv_pre, 1)
            dve.wait_ge(s_states_in, 1)
            taps = vec[:, V_CW:V_CW + TAPS * XT].rearrange("p (k m) -> p m k", m=XT)
            step(tt(cprod, xcs, taps.unsqueeze(2).to_broadcast((P, XT, NS, TAPS)), ALU.mult))
            step(dve.tensor_reduce(xc[:, :, SEQ:TOK], cprod, AX.X, ALU.add))
            tt(xc[:, :, SEQ:TOK], xc[:, :, SEQ:TOK], gains(V_CB, 0, XT, NS), ALU.add).then_inc(s_convs_pre, 1)
            raw, neg, e, u, lnu, dta = dtw
            dve.wait_ge(s_inproj_out, J_DT + 1)
            stt(neg, raw, -1.0, raw, ALU.mult, ALU.min).then_inc(s_dt_neg, 1)
            dve.wait_ge(s_dt_exp, 1)
            last(ts(u, e, 1.0, None, ALU.add), s_dt_u, 1)
            step(stt(neg, u, -1.0, e, ALU.add, ALU.subtract))
            step(dve.reciprocal(dt, u))
            step(tt(neg, neg, dt, ALU.mult))
            dve.wait_ge(s_dt_ln, 1)
            step(stt(raw, raw, 0.0, lnu, ALU.max, ALU.add))
            step(tt(dt, raw, neg, ALU.subtract))
            dve.wait_ge(s_exp_a, 1)
            step(ts(hv[:, 3:4], hv[:, 2:3], -1.0, None, ALU.mult))
            last(ts(dta, dt, hv[:, 3:4], None, ALU.mult), s_dta_ready, 1)
            for c in range(NC_):
                cc = slice(c * P, (c + 1) * P)
                ins = dve.tensor_tensor_scan(acs[:, cc], ones[0:NH, :], dta[:, cc], 0.0, ALU.mult, ALU.add)
            last(ins, s_dt_ready, 1)
            dve.wait_ge(s_conv_out, XT + 1)
            i2 = const[:, C_I2:C_I2 + NST].unsqueeze(1).to_broadcast((P, NS, NST))
            for kind in range(2):
                tt(stmp[:, kind, :].rearrange("p (b n) -> p b n", n=NST),
                   xc[:, 4 + kind, SEQ:TOK].unsqueeze(2).to_broadcast((P, NS, NST)), i2, ALU.mult).then_inc(s_diag_ready, 1)
            for g in range(NG):
                dve.wait_ge(s_pool_done, g + 1)
                for h in range(2):
                    ins = ts(v[:, g, BUF + h * HALF:BUF + (h + 1) * HALF], PS[4 + 2 * (g % 2) + h][:, 0:HALF],
                             vec[:, V_PB + g:V_PB + g + 1], vec[:, V_PS + g:V_PS + g + 1], ALU.add, ALU.mult)
                ins.then_inc(s_mixP_ready, 1)
            dve.wait_ge(s_cst_ready, 1)
            for t in range(4):
                dve.wait_ge(s_scan1_done, t + 1)
                for h in range(2):
                    hh = slice(h * HALF, (h + 1) * HALF)
                    ins = tt(xdtT[:, t, hh], PS[4 + 2 * (t % 2) + h][:, 0:HALF], xc[:, t, hh], ALU.mult)
                ins.then_inc(s_scan1_out, 1)
            dve.wait_ge(s_scan1_done, 5)
            dve.tensor_copy(acsT, PS[4][:, 0:NC_ * NH].rearrange("p (c h) -> p c h", h=NH)).then_inc(s_scan1_out, 1)
            dve.wait_ge(s_scan1_done, 6)
            dve.tensor_copy(Btok, tiles(PS[5][:, :])).then_inc(s_scan1_out, 1)
            causal = const[:, C_CAUSAL:C_CAUSAL + P].unsqueeze(1).to_broadcast((P, NC_, P))
            for g in range(2):
                dve.wait_ge(s_scan1_done, 7 + g)
                tt(tiles(Gm[:, g, :]), tiles(PS[6 + g][:, :]), causal, ALU.mult).then_inc(s_scan1_out, 1)
            dve.wait_ge(st_pool, 32)
            for c in range(NC_):
                dve.wait_ge(s_scan1_done, 9 + c)
                dve.tensor_copy(xtok[:, c, :], PS[4 + c][:, :]).then_inc(s_scan1_out, 1)
            dve.wait_ge(s_scan1_done, 13)
            dve.tensor_copy(dx, PS[4][:, 0:4 * (NS + 1)].rearrange("p (t b) -> p t b", b=NS + 1)).then_inc(s_scan1_out, 1)
            for q in range(4):
                dve.wait_ge(s_scan1_done, 14 + q)
                dve.tensor_copy(BC[:, q, :], PS[5 + q % 3][:, :]).then_inc(s_scan1_out, 1)
            dve.wait_ge(s_scan1_out, 17)

            def head_seg(h):
                dve.wait_ge(s_R_done, h + 1)
                bank = PS[4 + h % 4]
                dve.tensor_copy(RL[:, :, h], tiles(bank[:, :])[:, :, P - 1])
                for c in range(NC_):
                    cc = slice(c * P, (c + 1) * P)
                    ins = ts(seg[:, h % 2, cc], bank[:, cc], acsT[:, c, h:h + 1], 0.0, ALU.subtract, ALU.min)
                ins.then_inc(s_R_out, 1)

            def sample_sum(t):
                dve.wait_ge(s_samp_done, t + 1)
                dve.tensor_reduce(ys[:, t, :], stmp[:, 1].rearrange("p (b n) -> p b n", n=NST), AX.X, ALU.add
                                  ).then_inc(s_ys_out, 1)

            def head_scores(h):
                dve.wait_ge(s_seg_exp, h + 1)
                last(tt(M[:, h, :], seg[:, h % 2, :], Gm[:, h // 4, :], ALU.mult), s_M_ready, h + 1)

            head_seg(0)
            for h in range(NH):
                if h + 1 < NH:
                    head_seg(h + 1)
                if h in (2, 3):
                    sample_sum(h - 2)
                if h == 4:
                    sample_sum(2)
                    sample_sum(3)
                head_scores(h)
            dve.wait_ge(s_R_out, NH)
            tt(te, RL, acsT, ALU.subtract).then_inc(s_te_in, 1)
            dve.wait_ge(s_te_ready, 1)
            dve.wait_ge(s_inproj_done, len(COLS))
            for c in range(NC_):
                tt(xdtE[:, c, :].rearrange("p (h q) -> p h q", q=HD), xtok[:, c, :].rearrange("p (h q) -> p h q", q=HD),
                   te[:, c, :].unsqueeze(2).to_broadcast((P, NH, HD)), ALU.mult).then_inc(s_xdtE_ready, 1)
            dve.wait_ge(s_S_done, 1)
            last(dve.tensor_copy(H[:, 0, :], PS[4][:, :]), s_S_out, 1)
            for c in range(1, NC_):
                step(tt(H[:, c, :].rearrange("p (h q) -> p h q", q=HD), H[:, c - 1, :].rearrange("p (h q) -> p h q", q=HD),
                        cd[:, c, :].unsqueeze(2).to_broadcast((P, NH, HD)), ALU.mult))
                dve.wait_ge(s_S_done, c + 1)
                last(tt(H[:, c, :], H[:, c, :], PS[4 + c][:, :], ALU.add), s_S_out, c + 1)
            dve.wait_ge(s_eE_out, 4)
            for t in range(4):
                D_col = dx[:, t, NS:NS + 1]
                dve.wait_ge(s_Y_done, t + 1)
                step(stt(y[:, t, :], xc[:, t, 0:SEQ], D_col, PS[t][:, :], ALU.mult, ALU.add))
                dve.wait_ge(s_YO_done, t + 1)
                ins = dve.tensor_copy(fin[:, t, :], PS[4 + t][:, 0:NST])
                if t == 3:
                    ins.then_inc(s_fin_out, 1)
                last(tt(eE[:, t, P:SEQ], PS[4 + t][:, P:SEQ], eE[:, t, P:SEQ], ALU.mult), s_Y_out, t + 1)
                step(tt(y[:, t, P:SEQ], y[:, t, P:SEQ], eE[:, t, P:SEQ], ALU.add))
                if t == 0:
                    dve.wait_ge(s_ys_out, 4)
                step(stt(ys[:, t, :], xc[:, t, SEQ:TOK], D_col, ys[:, t, :], ALU.mult, ALU.add))
                tt(y[:, t, :], y[:, t, :], zs[:, t, 0:SEQ], ALU.mult)
                last(tt(ys[:, t, :], ys[:, t, :], zs[:, t, SEQ:TOK], ALU.mult), s_gated, t + 1)
            for t in range(4):
                dve.wait_ge(s_gn_out, t // 2 + 1)
                wn = vec[:, V_SN + t:V_SN + t + 1]
                stt(mixT[:, 4 + t, 0:SEQ], y[:, t, :], wn, rsg[:, t // 2, 0:SEQ], ALU.mult, ALU.mult)
                stt(mixT[:, 4 + t, SEQ:TOK], ys[:, t, :], wn, rsg[:, t // 2, SEQ:TOK], ALU.mult, ALU.mult).then_inc(s_mix_ready, 1)

            def residual(t):
                R = ROWS[t]
                dve.wait_ge(s_outp_done, t + 1)
                n, w = (2, 512) if t < 4 else (4, D // 4)
                for h in range(n):
                    hh = slice(h * w, (h + 1) * w)
                    src = PS[(4 + 2 * t) % 8 + h][:, :] if t < 4 else PS[0][32 * h:32 * h + NS, 0:w]
                    ins = tt(h1[0:R, t, hh], src, h1[0:R, t, hh], ALU.add)
                ins.then_inc(s_outp_out, 1)

            def norm_u(t):
                R = ROWS[t]
                dve.wait_ge(s_r_rstd, t + 1)
                step(dve.reciprocal(rstd[0:R, 5 + t:6 + t], rms_[0:R, 5 + t:6 + t]))
                if t >= 2:
                    dve.wait_ge(u_stored[t % 2], 16 * (t // 2))
                    dve.wait_ge(s_uTr_done, 2 * (t - 1))
                ts(row[0:R, t % 2, :], h1[0:R, t, :], rstd[0:R, 5 + t:6 + t], None, ALU.mult).then_inc(s_u_ready, 1)

            def take_rows(bank, slot, R, half, gain_col, signal):
                tt(uTr[:, slot, :].rearrange("p (k c) -> p k c", c=P)[:, 4 * half:4 * half + 4, 0:R],
                   tiles(bank[:, :])[:, :, 0:R], gains(gain_col, 4 * half, 4, R), ALU.mult).then_inc(signal, 1)

            def take_u(t):
                if t >= 2:
                    dve.wait_ge(s_lg_done, t - 1)
                for half in range(2):
                    dve.wait_ge(s_uTr_done, 2 * t + half + 1)
                    take_rows(PS[4 + half], t % 2, ROWS[t], half, V_FFN, s_uTr_out)

            def take_logits(t):
                R = ROWS[t]
                dve.wait_ge(s_lg_done, t + 1)
                last(tt(L[0:R, t, :], PS[6][0:R, t * 36:(t + 1) * 36], rbias[0:R, :], ALU.add), s_lg_out, t + 1)

            iota = const[:, C_IOTA:C_IOTA + NE]

            def choose(t):
                step(dve.tensor_copy(Lg[:, t, 0:4], L[:, t, 0:4]))
                step(dve.max(gmax[:, t, :], Lg[:, t, :]))
                step(dve.max_index(gidx[:, t, :], gmax[:, t, :], Lg[:, t, :]))
                step(dve.tensor_copy(gf[:, t:t + 1], gidx[:, t, 0:1]))
                step(ts(m4[:, t, :], iota[:, 0:4], gf[:, t:t + 1], None, ALU.is_equal))
                t48 = tmp[:, t, 0:NE].rearrange("p (g e) -> p g e", g=4)
                step(tt(t48, L[:, t, 4:36].rearrange("p (g e) -> p g e", g=4),
                        m4[:, t, :].unsqueeze(2).to_broadcast((P, 4, 8)), ALU.mult))
                step(dve.tensor_reduce(es[:, t, :], t48.rearrange("p g e -> p e g"), AX.X, ALU.add))
                step(dve.max(ev[:, t, :], es[:, t, :]))
                step(dve.max_index(eidx[:, t, :], ev[:, t, :], es[:, t, :]))

            residual(0)
            dve.wait_ge(st_hs, 64)
            step(dve.memset(L, 0.0))
            step(dve.memset(Lg, -3.0e38))
            dve.wait_ge(ld_rt, 80)
            norm_u(0)
            residual(1)
            norm_u(1)
            for t in range(NT):
                take_u(t)
                if t >= 1:
                    choose(t - 1)
                if t + 2 < NT:
                    residual(t + 2)
                    norm_u(t + 2)
                take_logits(t)
            choose(NT - 1)
            step(tt(ex4, L[:, :, 0:4], gmax[:, :, 0:1].to_broadcast((P, NT, 4)), ALU.subtract))
            tt(e21, ev[:, :, 1], ev[:, :, 0], ALU.subtract).then_inc(s_rt_a, 1)
            step(dve.tensor_copy(eid, eidx[:, :, 0:2]))
            step(stt(eid, gf.unsqueeze(2).to_broadcast((P, NT, 2)), 8.0, eid, ALU.mult, ALU.add))
            step(tt(eid, eid, const[:, C_BAD:C_BAD + NT].unsqueeze(2).to_broadcast((P, NT, 2)), ALU.add))
            oh4 = oh.rearrange("p t (k e) -> p (t k) e", e=NE)
            tm4 = tmp.rearrange("p t (k e) -> p (t k) e", e=NE)
            eidf = eid.rearrange("p t k -> p (t k)")
            step(tt(oh4, iota.unsqueeze(1).to_broadcast((P, 2 * NT, NE)), eidf.unsqueeze(2).to_broadcast((P, 2 * NT, NE)), ALU.is_equal))
            dve.tensor_copy(bef, const[:, C_BEFORE:C_BEFORE + P])
            dve.tensor_copy(oneb, ones)
            tt(ohs.rearrange("p (t e) -> p t e", e=NE), oh[:, :, 0:NE], oh[:, :, NE:2 * NE], ALU.add).then_inc(s_oh_ready, 1)
            dve.wait_ge(s_rt_b, 1)
            step(dve.tensor_reduce(gw, ex4, AX.X, ALU.add))
            step(stt(gw, e21, 1.0, gw, ALU.add, ALU.mult))
            step(dve.reciprocal(wgt[:, :, 0], gw))
            step(tt(wgt[:, :, 1], wgt[:, :, 0], e21, ALU.mult))
            dve.wait_ge(s_cnt_done, 1)
            for t in range(NT):
                tt(tmp[:, t, :].rearrange("p (k e) -> p k e", e=NE), oh[:, t, :].rearrange("p (k e) -> p k e", e=NE),
                   PS[7][:, t * NE:(t + 1) * NE].unsqueeze(1).to_broadcast((P, 2, NE)), ALU.mult)
            last(ts(ovn, PS[7][:, NT * NE:(NT + 1) * NE], float(S - 1), None, ALU.add), s_cnt_taken, 1)
            rkf = rk.rearrange("p t k -> p (t k)")
            step(dve.tensor_reduce(rkf, tm4, AX.X, ALU.add))
            step(dve.tensor_copy(int_w[:, :], ovn))
            step(ts(int_w[:, :], int_w[:, :], 6, None, ALU.arith_shift_right))
            step(dve.tensor_copy(ovn, int_w[:, :]))
            step(ts(ovn, ovn, -1.0, 0.0, ALU.add, ALU.max))
            step(dve.tensor_tensor_scan(ove, ones[:, 0:NE], ovn, 0.0, ALU.mult, ALU.add))
            step(tt(ovb, ove, ovn, ALU.subtract))
            step(tt(tm4, oh4, ovb.unsqueeze(1).to_broadcast((P, 2 * NT, NE)), ALU.mult))
            step(dve.tensor_reduce(ovt.rearrange("p t k -> p (t k)"), tm4, AX.X, ALU.add))
            step(dve.tensor_copy(rank_i, rk))
            step(ts(rank_i, rank_i, 6, None, ALU.arith_shift_right))
            step(dve.tensor_copy(rq, rank_i))
            step(stt(rr, rq, -float(S), rk, ALU.mult, ALU.add))
            step(ts(cmp0, rq, 0.5, None, ALU.is_gt))
            step(tt(ovt, ovt, rq, ALU.add))
            step(stt(ovt, ovt, float(NE - 1), eid, ALU.add, ALU.subtract))
            step(tt(ovt, ovt, cmp0, ALU.mult))
            step(tt(ovt, ovt, eid, ALU.add))
            dve.wait_ge(s_lg_done, NT)
            iota_s = const[:, C_IOTA:C_IOTA + S]
            tt(posh, iota_s.unsqueeze(1).to_broadcast((P, 2 * NT, S)),
               rr.rearrange("p t k -> p (t k)").unsqueeze(2).to_broadcast((P, 2 * NT, S)), ALU.is_equal)
            step(tt(blkh, iota_s[:, 0:NBT].unsqueeze(1).to_broadcast((P, 2 * NT, NBT)),
                    ovt.rearrange("p t k -> p (t k)").unsqueeze(2).to_broadcast((P, 2 * NT, NBT)), ALU.is_equal))
            tt(blkh, blkh, const[:, C_TOKID:C_TOKID + 2 * NT].unsqueeze(2).to_broadcast((P, 2 * NT, NBT)), ALU.mult
               ).then_inc(s_slot_ready, 1)
            dve.wait_ge(s_tab_done, 1)
            tab, empty = PS[7][0:S, 256:256 + NBT], tabe
            step(ts(empty, tab, 0.5, float(NONE), ALU.is_lt, ALU.mult))
            step(stt(out_all[:, :], tab, -1.0, empty, ALU.add, ALU.add))
            ts(idx_all[:, :], out_all[:, :], 1, None, ALU.arith_shift_right).then_inc(s_tab_ready, 1)
            t16 = tmp[0:1, :, :].rearrange("p t e -> p (t e)")
            for j in range(0, EXTRA, 8):
                tj = t16[:, 0:8 * NE].rearrange("p (j e) -> p j e", e=NE)
                step(tt(tj, ove[0:1, :].unsqueeze(1).to_broadcast((1, 8, NE)),
                        iota[0:1, j:j + 8].unsqueeze(2).to_broadcast((1, 8, NE)), ALU.is_le))
                step(dve.tensor_reduce(rk.rearrange("p t k -> p (t k)")[0:1, 0:8], tj, AX.X, ALU.add))
                step(ts(btab[:, NE + j:NE + j + 8], rk.rearrange("p t k -> p (t k)")[0:1, 0:8], float(NE - 1), None, ALU.min))
            step(dve.tensor_copy(btab[:, 0:NE], iota[0:1, :]))
            step(ts(rk[0:1, 0, :], ove[0:1, NE - 1:NE].to_broadcast((1, 2)), float(NE + U - 1), None, ALU.add))
            step(dve.tensor_copy(nloop[:, :], rk[0:1, 0, :]))
            step(ts(nloop[:, :], nloop[:, :], 2, None, ALU.arith_shift_right))
            ts(nloop[:, 1:2], nloop[:, 1:2], -1, None, ALU.add).then_inc(s_rt_ready, 1)
            dve.memset(idle[:, 4:5], 0.0).then_inc(s_ysb_free, 1)

            def take_block(b2):
                tt(uT[:, b2, :].rearrange("p (k c) -> p k c", c=S), PS[6 + b2][:, :].rearrange("p (k c) -> p k c", c=S),
                   g_ffn.unsqueeze(2).to_broadcast((P, KT, S)), ALU.mult).then_inc(s_uT_ready, 1)

            n = dve.value_load(nloop[0:1, 0:1], min_val=NE // U, max_val=NB // U)
            dve.wait_ge(s_T_done, 1)
            take_block(0)
            dve.wait_ge(s_pp_out, 2 * NT)
            with dve.Fori(0, n) as i:
                for s in range(U):
                    dve.wait_ge(s_sg_ready, i * U + (s + 1))
                    dve.wait_ge(s_up_done, i * U + (s + 1))
                    tt(act_tok[:, s % 2, :], PS[1][S:2 * S, 0:FF], sg[:, s % 2, :], ALU.mult).then_inc(s_act_ready, 1)
                    dve.wait_ge(s_actT_done, i * U + (s + 1))
                    dve.tensor_copy(actT[:, s % 2, :], PS[2][:, 0:2 * S]).then_inc(s_actT_ready, 1)
                    dve.wait_ge(s_T_done, i * U + (s + 2))
                    take_block((s + 1) % 2)

            def combine(i):
                t = TAIL[i]
                h = h1[0:ROWS[t], t, :]
                dve.wait_ge(yg_full[t], 16)
                step(stt(h, Yg[0:ROWS[t], 2 * t, :], wgt[0:ROWS[t], t, 0:1], h, ALU.mult, ALU.add))
                stt(h, Yg[0:ROWS[t], 2 * t + 1, :], wgt[0:ROWS[t], t, 1:2], h, ALU.mult, ALU.add).then_inc(s_f_h2, 1)

            def scale(i):
                t = TAIL[i]
                R = ROWS[t]
                dve.wait_ge(s_f_rstd, i + 1)
                step(dve.reciprocal(rstd[0:R, 10 + t:11 + t], rms_[0:R, 10 + t:11 + t]))
                if i >= 2:
                    dve.wait_ge(s_f_T, 2 * (i - 1))
                ts(row[0:R, i % 2, :], h1[0:R, t, :], rstd[0:R, 10 + t:11 + t], None, ALU.mult).then_inc(s_f_v, 1)

            def take_v(i):
                if i >= 2:
                    dve.wait_ge(s_f_g, 2 * (i - 1))
                for half in range(2):
                    dve.wait_ge(s_f_T, 2 * i + half + 1)
                    take_rows(PS[6 + half], i % 2, ROWS[TAIL[i]], half, V_PLE, s_f_vT)

            def gate_sum(i, h):
                t = TAIL[i]
                dve.wait_ge(s_f_g, 2 * i + h + 1)
                if t < 4:
                    hh = slice(h * 512, (h + 1) * 512)
                    ins = tt(Yg[:, 2 * t, hh], PS[2 * (i % 2) + h][:, :], bple[:, hh], ALU.add)
                else:
                    for q in range(2 * h, 2 * h + 2):
                        qq = slice(q * (D // 4), (q + 1) * (D // 4))
                        ins = tt(Yg[0:NS, 2 * t, qq], PS[0][32 * q:32 * q + NS, 0:D // 4], bple[0:NS, qq], ALU.add)
                ins.then_inc(s_f_gb, 1)

            def apply_gate(i, h):
                t = TAIL[i]
                R, hh = ROWS[t], slice(h * 512, (h + 1) * 512)
                gate = Yg[0:R, 2 * t, hh]
                dve.wait_ge(s_f_sig, 2 * i + h + 1)
                step(tt(gate, gate, pp[0:R, t, hh], ALU.mult))
                ins = tt(h1[0:R, t, hh], h1[0:R, t, hh], gate, ALU.add)
                if h:
                    last(ins, s_f_h3, i + 1)

            def finish(i):
                t = TAIL[i]
                R = ROWS[t]
                dve.wait_ge(s_f_r2, i + 1)
                step(dve.reciprocal(rstd[0:R, 15 + t:16 + t], rms_[0:R, 15 + t:16 + t]))
                stt(yout[0:R, t, :], h1[0:R, t, :], rstd[0:R, 15 + t:16 + t], bfin[0:R, :], ALU.mult, ALU.mult).then_inc(s_f_y, 1)

            dve.wait_ge(ld_bias, 32)
            combine(0)
            scale(0)
            combine(1)
            take_v(0)
            scale(1)
            take_v(1)
            combine(2)
            scale(2)
            for i in range(NT):
                gate_sum(i, 0)
                if i == NT - 1:
                    apply_gate(i, 0)
                gate_sum(i, 1)
                if i + 3 < NT:
                    combine(i + 3)
                if 2 <= i + 2 < NT:
                    take_v(i + 2)
                if i < NT - 1:
                    apply_gate(i, 0)
                apply_gate(i, 1)
                if i + 3 < NT:
                    scale(i + 3)
                finish(i)


_INS = ["x_prompt", "x_sample", "p_prompt", "p_sample", "state_pool", "state_conv", "state_ssm", "norm_mix",
        "w_in", "pool_lin_w", "pool_lin_b", "pool_scale", "conv_w", "conv_b", "dt_bias", "a_log", "d_skip",
        "ssd_norm", "w_out", "norm_ffn", "router_grp_w", "router_grp_b", "router_exp_w", "router_exp_b",
        "exp_w_gate", "exp_w_up", "exp_w_down", "norm_ple", "ple_gate_w", "ple_gate_b", "ple_proj_w", "norm_final"]
_OUTS = [("y_p", (1, SEQ, D)), ("y_s", (NS, 1, D)), ("pool_p", (1, 1, BUF, PW)), ("conv_p", (1, 1, TAPS - 1, CONV)),
         ("ssm_p", (1, 1, NH, HD, NST)), ("pool_s", (1, NS, BUF, PW)), ("conv_s", (1, NS, TAPS - 1, CONV)),
         ("ssm_s", (1, NS, NH, HD, NST))]


def kernel(**inputs):
    import numpy as np
    import concourse.bacc as bacc
    from concourse.bass_utils import run_bass_kernel_spmd

    nc = bacc.Bacc("TRN2", target_bir_lowering=False, num_devices=1)
    arrays = {f"in_{name}": np.ascontiguousarray(inputs[name]) for name in _INS}
    for name in ("exp_w_gate", "exp_w_up", "exp_w_down"):
        w = arrays[f"in_{name}"]
        arrays[f"in_{name}"] = w.reshape(NE, w.shape[3], w.shape[4])
    arrays["in_consts"], arrays["in_heads"] = shape_constants(np)
    a = {k[3:]: nc.dram_tensor(k, v.shape, F32, kind="ExternalInput").ap() for k, v in arrays.items()}
    o = {name: nc.dram_tensor(f"out_{name}", shape, F32, kind="ExternalOutput").ap() for name, shape in _OUTS}
    build(nc, a, o)
    r = run_bass_kernel_spmd(nc, [arrays], core_ids=[0])
    return tuple(r.results[0][f"out_{name}"] for name, _ in _OUTS)
```
